# Optimizing a Trainium2 kernel written in Bass

```python
import math
import jax, jax.numpy as jnp
from jax import lax
import numpy as np

D_MODEL = 2048
BATCH = 1
SEQ = 256
DEPTH = 1
DEC_BATCH = 8
DEC_SEQ = 4
PAST_LEN = 2048
PAGE_SIZE = 128

SSM_D_INNER = 2 * D_MODEL
SSM_HEAD_DIM = 64
SSM_N_HEADS = SSM_D_INNER // SSM_HEAD_DIM
SSM_N_GROUPS = 8
SSM_D_STATE = 128
SSM_CONV_WIDTH = 4
SSM_BC = SSM_N_GROUPS * SSM_D_STATE
SSM_CONV_DIM = SSM_D_INNER + 2 * SSM_BC
SSM_CHUNK = 128
HG_KEY_DIM = 128
HG_N_HEADS = D_MODEL // HG_KEY_DIM
HG_VAL_DIM = D_MODEL // HG_N_HEADS
HG_WIDTH_K = HG_N_HEADS * HG_KEY_DIM
HG_WIDTH_V = HG_N_HEADS * HG_VAL_DIM
HG_CHUNK = 64
FFN_HIDDEN = 4 * D_MODEL
PLE_DIM = 256
NORM_EPS = 1e-6
OFF_Z = 0
OFF_XBC = OFF_Z + SSM_D_INNER
OFF_DT = OFF_XBC + SSM_CONV_DIM
OFF_HQ = OFF_DT + SSM_N_HEADS
OFF_HF = OFF_HQ + HG_WIDTH_K
OFF_HI = OFF_HF + HG_WIDTH_K
OFF_HG = OFF_HI + HG_WIDTH_V
OFF_GATE = OFF_HG + HG_WIDTH_V
IN_DIM = OFF_GATE + 2 * D_MODEL

kernel_name = 'ssd_hgrn2_gated_parallel_decoder_step'

def _rmsnorm(x, w):
    xf = x.astype(jnp.float32)
    xf = xf * lax.rsqrt(jnp.mean(xf * xf, axis=-1, keepdims=True) + NORM_EPS)
    return xf * w.astype(jnp.float32)

def _pad_time(a, lp):
    return jnp.pad(a, [(0, 0), (0, lp - a.shape[1])] + [(0, 0)] * (a.ndim - 2))

def _chunks(a, c):
    b, lp = a.shape[:2]
    return jnp.moveaxis(a.reshape((b, lp // c, c) + a.shape[2:]), 1, 0)

def _ssd_chunked(x, dt, a_neg, b_mat, c_mat, h0):
    bsz, L = x.shape[:2]
    G, J = SSM_N_GROUPS, SSM_N_HEADS // SSM_N_GROUPS
    C = min(SSM_CHUNK, L)
    lp = -(-L // C) * C
    xs = _chunks(_pad_time(x, lp).reshape(bsz, lp, G, J, SSM_HEAD_DIM), C)
    dts = _chunks(_pad_time(dt, lp).reshape(bsz, lp, G, J), C)
    bs = _chunks(_pad_time(b_mat, lp), C)
    cs = _chunks(_pad_time(c_mat, lp), C)
    a_g = a_neg.reshape(G, J)
    mask = jnp.tril(jnp.ones((C, C), dtype=bool))[None, :, :, None, None]

    def step(h, inp):
        xc, dtc, bc, cc = inp
        cum = jnp.cumsum(dtc * a_g, axis=1)
        seg = cum[:, :, None] - cum[:, None]
        decay = jnp.exp(jnp.where(mask, seg, -jnp.inf))
        cb = jnp.einsum('btgn,bsgn->btsg', cc, bc)
        m = cb[..., None] * decay * dtc[:, None]
        y = jnp.einsum('btsgj,bsgjp->btgjp', m, xc)
        y = y + jnp.einsum('btgn,bgjpn->btgjp', cc, h) * jnp.exp(cum)[..., None]
        last = cum[:, -1]
        w = dtc * jnp.exp(last[:, None] - cum)
        h = jnp.exp(last)[..., None, None] * h + jnp.einsum('bsgn,bsgj,bsgjp->bgjpn', bc, w, xc)
        return h, y

    h, ys = lax.scan(step, h0.reshape(bsz, G, J, SSM_HEAD_DIM, SSM_D_STATE), (xs, dts, bs, cs))
    y = jnp.moveaxis(ys, 0, 1).reshape(bsz, lp, SSM_N_HEADS, SSM_HEAD_DIM)[:, :L]
    return y, h.reshape(bsz, SSM_N_HEADS, SSM_HEAD_DIM, SSM_D_STATE)

def _hgrn2_chunked(q, k, log_f, v, s0):
    bsz, L = q.shape[:2]
    C = min(HG_CHUNK, L)
    lp = -(-L // C) * C
    qs = _chunks(_pad_time(q, lp), C)
    kks = _chunks(_pad_time(k, lp), C)
    lfs = _chunks(_pad_time(log_f, lp), C)
    vs = _chunks(_pad_time(v, lp), C)
    mask = jnp.tril(jnp.ones((C, C), dtype=bool))[None, :, :, None, None]

    def step(s, inp):
        qc, kc, lfc, vc = inp
        cum = jnp.cumsum(lfc, axis=1)
        seg = cum[:, :, None] - cum[:, None]
        decay = jnp.exp(jnp.where(mask, seg, -jnp.inf))
        att = jnp.einsum('bthk,btshk,bshk->btsh', qc, decay, kc)
        o = jnp.einsum('btsh,bshv->bthv', att, vc)
        o = o + jnp.einsum('bthk,bhkv->bthv', qc * jnp.exp(cum), s)
        last = cum[:, -1]
        s = jnp.exp(last)[..., None] * s + jnp.einsum('bshk,bshv->bhkv', kc * jnp.exp(last[:, None] - cum), vc)
        return s, o

    s, os_ = lax.scan(step, s0, (qs, kks, lfs, vs))
    o = jnp.moveaxis(os_, 0, 1).reshape(bsz, lp, HG_N_HEADS, HG_VAL_DIM)[:, :L]
    return o, s

def _layer(x, p, ssm0, conv0, hg0, lb, norm_mix_pre, w_in, conv_w, conv_b, dt_bias, a_log, d_skip,
           ssm_norm, w_br_a, hg_norm, w_br_b, w_out, norm_mix_post, norm_ffn_pre, w_up, w_down,
           norm_ffn_post, norm_ple, w_ple_gate, w_ple_proj):
    f32 = jnp.float32
    bsz, L, _ = x.shape
    h = _rmsnorm(x, norm_mix_pre)
    proj = jnp.einsum('bld,de->ble', h, w_in.astype(f32))
    z = proj[..., OFF_Z:OFF_XBC]
    xbc = proj[..., OFF_XBC:OFF_DT]
    dt_raw = proj[..., OFF_DT:OFF_HQ]
    hq = proj[..., OFF_HQ:OFF_HF].reshape(bsz, L, HG_N_HEADS, HG_KEY_DIM)
    hf = proj[..., OFF_HF:OFF_HI].reshape(bsz, L, HG_N_HEADS, HG_KEY_DIM)
    hi = proj[..., OFF_HI:OFF_HG].reshape(bsz, L, HG_N_HEADS, HG_VAL_DIM)
    hg = proj[..., OFF_HG:OFF_GATE]
    gates = jax.nn.sigmoid(proj[..., OFF_GATE:].reshape(bsz, L, 2, D_MODEL))

    xpad = jnp.concatenate([conv0.astype(f32), xbc], axis=1)
    new_conv = xpad[:, -(SSM_CONV_WIDTH - 1):]
    xc = lax.conv_general_dilated(xpad, conv_w.astype(f32)[:, None, :], window_strides=(1,), padding='VALID',
                                  dimension_numbers=('NWC', 'WIO', 'NWC'), feature_group_count=SSM_CONV_DIM)
    xc = jax.nn.silu(xc + conv_b.astype(f32))
    xs = xc[..., :SSM_D_INNER].reshape(bsz, L, SSM_N_HEADS, SSM_HEAD_DIM)
    bm = xc[..., SSM_D_INNER:SSM_D_INNER + SSM_BC].reshape(bsz, L, SSM_N_GROUPS, SSM_D_STATE)
    cm = xc[..., SSM_D_INNER + SSM_BC:].reshape(bsz, L, SSM_N_GROUPS, SSM_D_STATE)
    dt = jax.nn.softplus(dt_raw + dt_bias.astype(f32))
    a_neg = -jnp.exp(a_log.astype(f32))
    y, new_ssm = _ssd_chunked(xs, dt, a_neg, bm, cm, ssm0.astype(f32))
    y = y + d_skip.astype(f32)[:, None] * xs
    y = (y.reshape(bsz, L, SSM_D_INNER) * jax.nn.silu(z)).reshape(bsz, L, SSM_N_GROUPS, SSM_D_INNER // SSM_N_GROUPS)
    y = _rmsnorm(y, ssm_norm.reshape(SSM_N_GROUPS, SSM_D_INNER // SSM_N_GROUPS)).reshape(bsz, L, SSM_D_INNER)
    y_a = jnp.einsum('ble,ed->bld', y, w_br_a.astype(f32))

    lb = lb.astype(f32).reshape(HG_N_HEADS, HG_KEY_DIM)
    log_f = jnp.log(lb + (1.0 - lb) * jax.nn.sigmoid(hf))
    k = (1.0 - lb) * jax.nn.sigmoid(-hf)
    o, new_hg = _hgrn2_chunked(hq, k, log_f, hi, hg0.astype(f32))
    o = _rmsnorm(o, hg_norm).reshape(bsz, L, HG_WIDTH_V) * jax.nn.silu(hg)
    y_b = jnp.einsum('ble,ed->bld', o, w_br_b.astype(f32))

    mixed = gates[:, :, 0] * y_a + gates[:, :, 1] * y_b
    mix_out = jnp.einsum('bld,de->ble', mixed, w_out.astype(f32))
    x = x + _rmsnorm(mix_out, norm_mix_post).astype(x.dtype)

    h2 = _rmsnorm(x, norm_ffn_pre)
    u = jnp.square(jax.nn.relu(jnp.einsum('bld,df->blf', h2, w_up.astype(f32))))
    ffn = jnp.einsum('blf,fd->bld', u, w_down.astype(f32))
    x = x + _rmsnorm(ffn, norm_ffn_post).astype(x.dtype)

    g_ple = jax.nn.sigmoid(jnp.einsum('bld,de->ble', _rmsnorm(x, norm_ple), w_ple_gate.astype(f32)))
    e = jnp.einsum('blp,pd->bld', p.astype(f32), w_ple_proj.astype(f32))
    x = x + (g_ple * e).astype(x.dtype)
    return x, new_ssm.astype(ssm0.dtype), new_conv.astype(conv0.dtype), new_hg.astype(hg0.dtype)

def setup_inputs(seed: int = 0) -> dict:
    key = jax.random.key(seed)
    ks = iter(jax.random.split(key, 40))

    def nrm(shape, scale):
        return scale * jax.random.normal(next(ks), shape, jnp.float32)

    def gain(shape):
        return 1.0 + nrm(shape, 0.05)

    u = jax.random.uniform(next(ks), (DEPTH, SSM_N_HEADS), jnp.float32)
    dt0 = jnp.exp(u * (math.log(0.1) - math.log(0.001)) + math.log(0.001))
    dt_bias = dt0 + jnp.log(-jnp.expm1(-dt0))
    a_log = jnp.log(jax.random.uniform(next(ks), (DEPTH, SSM_N_HEADS), jnp.float32, 1.0, 16.0))
    return {
        'x_prompt': nrm((BATCH, SEQ, D_MODEL), 1.0),
        'x_sample': nrm((DEC_BATCH, DEC_SEQ, D_MODEL), 1.0),
        'p_prompt': nrm((DEPTH, BATCH, SEQ, PLE_DIM), 1.0),
        'p_sample': nrm((DEPTH, DEC_BATCH, DEC_SEQ, PLE_DIM), 1.0),
        'state_ssm': nrm((DEPTH, DEC_BATCH, SSM_N_HEADS, SSM_HEAD_DIM, SSM_D_STATE), 0.3),
        'state_conv': nrm((DEPTH, DEC_BATCH, SSM_CONV_WIDTH - 1, SSM_CONV_DIM), 1.0),
        'state_hgrn': nrm((DEPTH, DEC_BATCH, HG_N_HEADS, HG_KEY_DIM, HG_VAL_DIM), 0.3),
        'norm_mix_pre': gain((DEPTH, D_MODEL)),
        'w_in': nrm((DEPTH, D_MODEL, IN_DIM), D_MODEL ** -0.5),
        'conv_w': nrm((DEPTH, SSM_CONV_WIDTH, SSM_CONV_DIM), SSM_CONV_WIDTH ** -0.5),
        'conv_b': nrm((DEPTH, SSM_CONV_DIM), 0.02),
        'dt_bias': dt_bias,
        'a_log': a_log,
        'd_skip': gain((DEPTH, SSM_N_HEADS)),
        'ssm_norm': gain((DEPTH, SSM_D_INNER)),
        'w_br_a': nrm((DEPTH, SSM_D_INNER, D_MODEL), SSM_D_INNER ** -0.5),
        'hg_lb': nrm((DEPTH + 1, HG_WIDTH_K), 0.1),
        'hg_norm': gain((DEPTH, HG_VAL_DIM)),
        'w_br_b': nrm((DEPTH, HG_WIDTH_V, D_MODEL), HG_WIDTH_V ** -0.5),
        'w_out': nrm((DEPTH, D_MODEL, D_MODEL), D_MODEL ** -0.5),
        'norm_mix_post': gain((DEPTH, D_MODEL)),
        'norm_ffn_pre': gain((DEPTH, D_MODEL)),
        'w_up': nrm((DEPTH, D_MODEL, FFN_HIDDEN), D_MODEL ** -0.5),
        'w_down': nrm((DEPTH, FFN_HIDDEN, D_MODEL), FFN_HIDDEN ** -0.5),
        'norm_ffn_post': gain((DEPTH, D_MODEL)),
        'norm_ple': gain((DEPTH, D_MODEL)),
        'w_ple_gate': nrm((DEPTH, D_MODEL, D_MODEL), D_MODEL ** -0.5),
        'w_ple_proj': nrm((DEPTH, PLE_DIM, D_MODEL), PLE_DIM ** -0.5),
    }

def reference(x_prompt, x_sample, p_prompt, p_sample, state_ssm, state_conv, state_hgrn,
              norm_mix_pre, w_in, conv_w, conv_b, dt_bias, a_log, d_skip, ssm_norm, w_br_a,
              hg_lb, hg_norm, w_br_b, w_out, norm_mix_post, norm_ffn_pre, w_up, w_down,
              norm_ffn_post, norm_ple, w_ple_gate, w_ple_proj):
    lbs = jnp.cumsum(jax.nn.softmax(hg_lb.astype(jnp.float32), axis=0), axis=0)
    bp = x_prompt.shape[0]
    ssm_p0 = jnp.zeros((bp, SSM_N_HEADS, SSM_HEAD_DIM, SSM_D_STATE), x_prompt.dtype)
    conv_p0 = jnp.zeros((bp, SSM_CONV_WIDTH - 1, SSM_CONV_DIM), x_prompt.dtype)
    hg_p0 = jnp.zeros((bp, HG_N_HEADS, HG_KEY_DIM, HG_VAL_DIM), x_prompt.dtype)
    yp, ys = x_prompt, x_sample
    ssm_p, conv_p, hg_p, ssm_s, conv_s, hg_s = [], [], [], [], [], []
    for li in range(DEPTH):
        lw = (norm_mix_pre[li], w_in[li], conv_w[li], conv_b[li], dt_bias[li], a_log[li], d_skip[li],
              ssm_norm[li], w_br_a[li], hg_norm[li], w_br_b[li], w_out[li], norm_mix_post[li],
              norm_ffn_pre[li], w_up[li], w_down[li], norm_ffn_post[li], norm_ple[li],
              w_ple_gate[li], w_ple_proj[li])
        yp, s1, c1, g1 = _layer(yp, p_prompt[li], ssm_p0, conv_p0, hg_p0, lbs[li], *lw)
        ys, s2, c2, g2 = _layer(ys, p_sample[li], state_ssm[li], state_conv[li], state_hgrn[li], lbs[li], *lw)
        ssm_p.append(s1)
        conv_p.append(c1)
        hg_p.append(g1)
        ssm_s.append(s2)
        conv_s.append(c2)
        hg_s.append(g2)
    return (yp, ys, jnp.stack(ssm_p), jnp.stack(conv_p), jnp.stack(hg_p),
            jnp.stack(ssm_s), jnp.stack(conv_s), jnp.stack(hg_s))


_drawn_inputs = setup_inputs


def setup_inputs(seed=0):
    import zlib

    import numpy as np

    out = dict(_drawn_inputs(seed))
    spreads = {}
    factors = {'d_skip': 12.186, 'hg_norm': 3.153, 'norm_ple': 22.482, 'ssm_norm': 3.073}
    for name, (base, spread) in spreads.items():
        noise = np.random.default_rng([zlib.crc32(name.encode()), seed]).standard_normal(out[name].shape)
        drawn = base * np.exp(spread * noise) if base else spread * noise
        out[name] = __import__('jax').numpy.asarray(drawn.astype(out[name].dtype))
    for name, factor in factors.items():
        out[name] = (out[name] * factor).astype(out[name].dtype)
    return out
```

```python
from contextlib import ExitStack

import numpy as np

import concourse.bass as bass
from concourse import mybir

F32 = mybir.dt.float32
F32R = mybir.dt.float32r
ALU = mybir.AluOpType
ACT = mybir.ActivationFunctionType
AX = mybir.AxisListType

P = 128
D = 2048
KT = D // P
TP = 256
NB, SB = 8, 4
TS = NB * SB
T = TP + TS
GROUPS = 8
GH = 8
HD = 64
HEADS = 16
PLE = 256
FFN = 8192
FT = FFN // P // 2
CW = 4
XT = 6
EPS = 1e-6

RING = 4
AHEAD = 3
SK = 8

HG_SLABS, HG_TILES = 8, 4
GB_SLABS = 4
SG_SLABS, SG_TILES = 20, 10
GA_SLABS = 6
U_HG, T_HG = 0, 0
U_GB, T_GB = U_HG + HEADS * HG_SLABS, T_HG + HEADS * HG_TILES
U_SG, T_SG = U_GB + KT * GB_SLABS, T_GB + KT * 2
U_GA, T_GA = U_SG + GROUPS * SG_SLABS, T_SG + GROUPS * SG_TILES
U_OUT, T_OUT = U_GA + KT * GA_SLABS, T_GA + KT * 2
U_FFN, T_FFN = U_OUT + KT * 2, T_OUT + KT
HALF_U, HALF_T = FT * 2 + KT * 4, FT + KT
U_PROJ, T_PROJ = U_FFN + 2 * HALF_U, T_FFN + 2 * HALF_T
U_PLE, T_PLE = U_PROJ + 4, T_PROJ + KT
SLABS = U_PLE + KT * 2

LEVELS = (64, 32, 16, 8, 4, 2, 1)
LOFF = {}
_o = 0
for _h in LEVELS:
    LOFF[_h] = _o
    _o += T if _h <= 2 else TP
LAST_OFF = _o
E_COLS = _o + TS
DIAG = (16, 8, 4, 2, 1, 0)
DIAG_S = (2, 1, 0)

C_MIXPRE, C_MIXPOST, C_FFNPRE, C_FFNPOST, C_PLE = (KT * i for i in range(5))
C_HGN = 5 * KT
C_SSMN = C_HGN + 1
C_DSKIP = C_SSMN + 32
C_LB = C_DSKIP + 32
N_COLS = C_LB + 2 * HEADS
K_IDENT, K_ONES = 0, P
K_RESET = 2 * P
K_DIAG = K_RESET + T
K_DIAGS = K_DIAG + len(DIAG) * 64
K_CB = K_DIAGS + len(DIAG_S) * TS
K_BATCH = K_CB + 416
K_EPS = K_BATCH + NB
N_CONST = K_EPS + 1

PW = CW + 1
RAWC = (CW - 1) + TP + NB * (CW - 1 + SB)
CVC = RAWC - (CW - 1)
SOFF = CW - 1 + TP


def constants():
    c = np.zeros((P, N_CONST), np.float32)
    c[:, K_IDENT:K_IDENT + P] = np.eye(P)
    c[:, K_ONES:K_ONES + P] = 1.0
    c[:, K_RESET:K_RESET + T] = 1.0
    c[:, K_RESET] = 0.0
    c[:, K_RESET + TP:K_RESET + T:SB] = 0.0
    s = np.arange(32)[:, None]
    t = np.arange(32)[None, :]

    def pairs(h):
        if h == 0:
            return s == t
        return (s // (2 * h) == t // (2 * h)) & (s % (2 * h) < h) & (t % (2 * h) >= h)
    for n, h in enumerate(DIAG):
        for q in range(4):
            for b in range(2):
                at = K_DIAG + n * 64 + b * 32
                c[32 * q:32 * q + 32, at:at + 32] = pairs(h)
    for n, h in enumerate(DIAG_S):
        c[0:32, K_DIAGS + n * TS:K_DIAGS + (n + 1) * TS] = pairs(h)
    r = np.arange(P)[:, None]
    c[:, K_CB:K_CB + TP] = r <= np.arange(TP)[None, :]
    c[:, K_CB + TP:K_CB + TP + P] = r <= np.arange(P)[None, :]
    c[0:32, K_CB + 384:K_CB + 416] = (s // SB == t // SB) & (s <= t)
    for q in range(3):
        c[32 * q:32 * q + 32, K_BATCH:K_BATCH + NB] = s // SB == np.arange(NB)[None, :]
    c[:, K_EPS] = EPS
    return c


def layer_program(nc, io):
    stack = ExitStack()

    def sem(name):
        return stack.enter_context(nc.semaphore(name))

    base = (nc.sbuf_base + 31) // 32 * 32
    top = nc.sbuf_usable_end // 32 * 32
    place = [base]

    def sb(name, shape, dt=F32):
        t = nc.alloc_sbuf_tensor_at(name, shape, dt, offset=place[0])
        place[0] += (int(np.prod(shape[1:])) * 4 + 31) // 32 * 32
        assert place[0] <= top, (name, place[0] - top)
        return t

    raw = sb("raw", [P, RING, SK, P])
    w_hi = sb("w_hi", [P, RING, SK, P], F32R)
    w_lo = sb("w_lo", [P, RING, SK, P], F32R)
    h_hi = sb("h_hi", [P, KT, T], F32R)
    h_lo = sb("h_lo", [P, KT, T], F32R)
    consts = sb("consts", [P, N_CONST])
    cols = sb("cols", [P, N_COLS])
    lbc = sb("lbc", [P, HEADS, 3])
    tok = sb("tok", [P, 3, 3, HD])
    ident = consts[:, K_IDENT:K_IDENT + P]
    ones = consts[:, K_ONES:K_ONES + P]
    eps = consts[:, K_EPS:K_EPS + 1]
    one_col = consts[:, K_ONES:K_ONES + 1]
    phase = place[0]

    x_in = sb("x_in", [P, KT, T])
    x_sq = sb("x_sq", [P, KT, T])
    x_rs = sb("x_rs", [P, T])
    wdt = sb("wdt", [P, KT, HD])
    hn32 = sb("hn32", [P, KT, T])
    hv = sb("hv", [HD, 2])
    dtz = sb("dtz", [HD, T])
    dta = sb("dta", [HD, T])
    dte = sb("dte", [HD, T])
    dts = sb("dts", [HD, T])
    cum = sb("cum", [HD, T])
    dtw = sb("dtw", [HD, T])
    ecum = sb("ecum", [HD, TS])
    elast = sb("elast", [HD, NB])
    an = sb("an", [HD, 1])
    lbm = sb("lbm", [P, 4, HEADS])

    place[0] = phase
    o_hi = sb("o_hi", [P, HEADS, T], F32R)
    o_lo = sb("o_lo", [P, HEADS, T], F32R)
    after_o = place[0]
    hth = sb("hth", [P, T])
    hq = sb("hq", [P, T])
    hvv = sb("hvv", [P, T])
    hg = sb("hg", [P, T])
    htg = sb("htg", [P, T])
    hf = sb("hf", [P, T])
    hk = sb("hk", [P, T])
    hlf = sb("hlf", [P, T])
    hcum = sb("hcum", [P, T])
    hcur = sb("hcur", [P, 3])
    hnc = sb("hnc", [P, 1])
    he = sb("he", [P, E_COLS])
    hkw = sb("hkw", [P, TP])
    hkt = sb("hkt", [P, P])
    hqt = sb("hqt", [P, P])
    hec = sb("hec", [P, TS])
    hqs = sb("hqs", [P, TS])
    hks = sb("hks", [P, TS])
    hel = sb("hel", [P, NB])
    hdm = sb("hdm", [P, len(DIAG) * 64])
    hab = sb("hab", [P, 2, 32])
    hatt = sb("hatt", [P, 2, P])
    htop = sb("htop", [P, P])
    hdms = sb("hdms", [32, len(DIAG_S) * TS])
    hats = sb("hats", [32, TS])
    hvt = sb("hvt", [P, 3, P])
    hkwt = sb("hkwt", [P, 3, P])
    hv3 = sb("hv3", [96, P], F32R)
    hk3 = sb("hk3", [96, P], F32R)
    hvbd = sb("hvbd", [96, NB, P], F32R)
    hs0 = sb("hs0", [P, NB, P])
    hsn = sb("hsn", [P, NB, P])
    hsp = sb("hsp", [P, P])
    hsq = sb("hsq", [P, T])
    hrs = sb("hrs", [P, T])
    hsg = sb("hsg", [P, T])
    hon = sb("hon", [P, T])
    hso = sb("hso", [P, T])

    place[0] = after_o
    btg = sb("btg", [P, T])
    byb = sb("byb", [P, T])
    bmb = sb("bmb", [P, T])

    y_bytes = 2 * KT * T * 4
    y_at = top - y_bytes
    y32 = nc.alloc_sbuf_tensor_at("y32", [P, 2 * KT, T], F32, offset=y_at)
    m_hi = nc.alloc_sbuf_tensor_at("m_hi", [P, KT, T], F32R, offset=y_at)
    m_lo = nc.alloc_sbuf_tensor_at("m_lo", [P, KT, T], F32R, offset=y_at + y_bytes // 2)
    x2 = nc.alloc_sbuf_tensor_at("x2", [P, KT, T], F32, offset=y_at)
    ffn = nc.alloc_sbuf_tensor_at("ffn", [P, KT, T], F32, offset=y_at + y_bytes // 2)
    place[0] = phase
    craw = sb("craw", [P, 2, RAWC])
    ccv = sb("ccv", [P, RAWC])
    cth = sb("cth", [P, T])
    xf = sb("xf", [P, 4, T])
    bf = sb("bf", [P, T])
    cf = sb("cf", [P, T])
    cbm = sb("cbm", [P, 416])
    cbc = sb("cbc", [P, GH, T])
    me = sb("me", [P, GH, 416])
    xd = sb("xd", [P, 3, GH * HD])
    xw = sb("xw", [P, 3, GH * HD])
    bt = sb("bt", [P, 3, P])
    bt3 = sb("bt3", [96, P], F32R)
    bbd = sb("bbd", [96, NB, P], F32R)
    xw3 = sb("xw3", [96, GH * HD], F32R)
    sz = sb("sz", [P, 4, T])
    yf = sb("yf", [P, 4, T])
    yrs = sb("yrs", [P, T])
    ecp = sb("ecp", [P, 4, TS])
    el = sb("el", [P, GH, NB])
    ssp = sb("ssp", [P, 4, P])
    ht = sb("ht", [P, 4, GH * HD])
    prm = sb("prm", [P, XT, PW])
    prh = sb("prh", [P, XT, PW])
    cst = sb("cst", [P, XT, NB, CW - 1])
    ncv = sb("ncv", [P, XT, (1 + NB) * (CW - 1)])
    cfs = sb("cfs", [P, TS])
    tcur = sb("tcur", [P, 3, 3, GH])
    ncur = sb("ncur", [P, 4])
    dcur = sb("dcur", [P, 4])
    yti = sb("yti", [P, 4, TS])
    assert place[0] <= y_at, place[0] - y_at
    cv_samples = ccv[:, SOFF:RAWC].rearrange("p (b s) -> p b s", b=NB)[:, :, 0:SB]
    ysq = me[:, 0:3, :].rearrange("p h n -> p (h n)")[:, 0:4 * T].rearrange("p (c n) -> p c n", c=4)

    place[0] = phase
    y_hi = sb("y_hi", [P, 2 * KT, T], F32R)
    y_lo = sb("y_lo", [P, 2 * KT, T], F32R)
    after_y = place[0]
    atg = sb("atg", [P, T])
    aya = sb("aya", [P, T])
    amb = sb("amb", [P, T])
    assert place[0] <= y_at, place[0] - y_at

    place[0] = phase
    x_res = sb("x_res", [P, KT, T])
    mo = sb("mo", [P, KT, T])
    nsq = sb("nsq", [P, KT, T])
    assert place[0] <= after_y
    u_hi = nc.alloc_sbuf_tensor_at("u_hi", [P, FT, T], F32R, offset=phase)
    u_lo = nc.alloc_sbuf_tensor_at("u_lo", [P, FT, T], F32R, offset=phase + y_bytes)
    place[0] = phase
    e_out = sb("e_out", [P, KT, T])
    p_in = sb("p_in", [P, 2, T])
    p_hi = sb("p_hi", [P, 2, T], F32R)
    p_lo = sb("p_lo", [P, 2, T], F32R)
    nsq3 = sb("nsq3", [P, KT, T])
    gtg = sb("gtg", [P, 2, T])
    place[0] = after_y
    acc = sb("acc", [P, T])
    nrs = sb("nrs", [P, T])
    tmp = sb("tmp", [P, T])
    assert place[0] <= y_at, place[0] - y_at
    ru = [acc, nrs]

    ps = [stack.enter_context(nc.psum_tensor(f"acc{i}", [P, 512], F32)) for i in range(2)]
    bank = [stack.enter_context(nc.psum_tensor(f"bank{i}", [P, 512], F32)) for i in range(6)]
    b_tv, b_tk, b_diag, b_att, b_o, b_ms = bank

    mixb = nc.dram_tensor("mixb", (KT, P, T), F32, kind="Internal").ap()
    cum_d = nc.dram_tensor("cum_d", (HD, T), F32, kind="Internal").ap()
    ecum_d = nc.dram_tensor("ecum_d", (HD, TS), F32, kind="Internal").ap()
    elast_d = nc.dram_tensor("elast_d", (HD, NB), F32, kind="Internal").ap()

    raw_in = [sem(f"raw_in{k}") for k in range(RING)]
    hi_done = sem("hi_done")
    lo_done = sem("lo_done")
    slab_used = sem("slab_used")
    evac = sem("evac")
    x_land = [sem(f"x_land{i}") for i in range(4)]
    cst_land = sem("cst_land")
    cols_land = sem("cols_land")
    wdt_land = sem("wdt_land")
    act_pro = sem("act_pro")
    dve_pro = sem("dve_pro")
    pe_pro = sem("pe_pro")
    scr_out = sem("scr_out")
    n_sq, n_ms, n_ln, n_rs, n_xn, n_hi, n_lo = (
        sem(f"norm_{s}") for s in ("sq", "ms", "ln", "rs", "xn", "hi", "lo"))

    hg_fk, hg_lf, hg_cum, hg_arg, hg_exp, hg_w = (
        sem(f"hg_{s}") for s in ("fk", "lf", "cum", "arg", "exp", "w"))
    hg_cur = sem("hg_cur")
    hg_tr, hg_attn, hg_tok, hg_tlo, hg_dm, hg_red, hg_ab, hg_vbd, hg_p2 = (
        sem(f"hg_{s}") for s in ("tr", "attn", "tok", "tlo", "dm", "red", "ab", "vbd", "p2"))
    hg_sq, hg_ms, hg_ln, hg_rs, hg_on, hg_so, hg_ohi, hg_olo, hg_st = (
        sem(f"hg_{s}") for s in ("sq", "ms", "ln", "rs", "on", "so", "ohi", "olo", "st"))
    hg_zero = sem("hg_zero")
    hg_s0 = sem("hg_s0_in")
    hg_out = sem("hg_state_out")

    gb_mb, gb_out = sem("gb_mb"), sem("gb_out")

    sg_raw0, sg_prh, sg_conv, sg_th, sg_silu, sg_nc, sg_cur = (
        sem(f"sg_{s}") for s in ("raw0", "prh", "conv", "th", "silu", "nc", "cur"))
    sg_bc, sg_bt, sg_bbd, sg_cbm, sg_seg, sg_exp, sg_m, sg_cfs = (
        sem(f"sg_{s}") for s in ("bc", "bt", "bbd", "cbm", "seg", "exp", "m", "cfs"))
    sg_xt, sg_xd, sg_y, sg_yf, sg_sp, sg_spe, sg_zt, sg_sz, sg_it, sg_su, sg_upa, sg_up = (
        sem(f"sg_{s}") for s in ("xt", "xd", "y", "yf", "sp", "spe", "zt", "sz", "it", "su", "upa", "up"))
    sg_cv, sg_ncur = sem("sg_cv"), sem("sg_ncur")
    sg_btlo, sg_xwhi, sg_xwlo = sem("sg_btlo"), sem("sg_xwhi"), sem("sg_xwlo")
    sg_yi, sg_g, sg_sq, sg_ms, sg_ln, sg_rs, sg_y32 = (
        sem(f"sg_{s}") for s in ("yi", "g", "sq", "ms", "ln", "rs", "y32"))
    sg_par_in, sg_cbc_in, sg_nc_out, sg_sp_out, sg_ec_in = (
        sem(f"sg_{s}") for s in ("par_in", "cbc_in", "nc_out", "sp_out", "ec_in"))
    sg_ht_in = [sem(f"sg_ht_in{i}") for i in range(4)]
    sg_ht_out = [sem(f"sg_ht_out{i}") for i in range(4)]

    y_his, y_los = sem("y_hi_done"), sem("y_lo_done")
    ga_in, ga_t, ga_m, ga_hi, ga_lo = (sem(f"ga_{s}") for s in ("in", "t", "m", "hi", "lo"))
    o_acc = sem("out_acc")
    xr_in = sem("x_res_in")
    x2_a, x2_b = sem("x2_scaled"), sem("x2_done")
    up_sq, up_hi, up_lo = sem("up_sq"), sem("up_hi"), sem("up_lo")
    dn_add, dn_sq, dn_acc = sem("dn_add"), sem("dn_sq"), sem("dn_acc")
    pj_tile = sem("pj_tile")
    p_land, p_his, p_los = sem("p_land"), sem("p_hi_done"), sem("p_lo_done")
    g_t, g_y, y_out = sem("g_t"), sem("g_y"), sem("y_out")

    def one(ap):
        return ap.rearrange("p (a n) -> p a n", a=1)

    def tile_at(t, i):
        return t[:, i:i + 1] if isinstance(i, int) else t[:, bass.ds(i, 1)]

    def blocks(ap, n):
        return ap.rearrange("p (b n) -> p b n", b=n)

    def slab(first, per, it, s):
        return first // RING + it * (per // RING) + s // RING, s % RING

    block = stack.enter_context(nc.Block())

    @block.sync
    def _(sp):
        def load_slab(m, k):
            src = io["w"][bass.ds(m * RING + k, 1)].rearrange("a p s n -> p (a s) n") \
                if not isinstance(m, int) else io["w"][m * RING + k]
            sp.dma_start(raw[:, k], src).then_inc(raw_in[k], 16)

        for c in range(4):
            sp.dma_start(x_in[:, 4 * c:4 * c + 4], io["x"][:, 4 * c:4 * c + 4]).then_inc(x_land[c], 16)
        sp.dma_start(consts[:, :], io["consts"]).then_inc(cst_land, 16)
        sp.dma_start(cols[:, :], io["cols"]).then_inc(cols_land, 16)
        sp.dma_start(hv[:, :], io["hv"]).then_inc(cols_land, 16)
        sp.dma_start(wdt[:, :, :], io["wdt"]).then_inc(wdt_land, 16)
        for k in range(RING):
            load_slab(0, k)
        with sp.Fori(1, SLABS // RING) as m:
            for k in range(RING):
                sp.wait_ge(lo_done, m * RING + (k + 1 - RING))
                load_slab(m, k)

    @block.scalar
    def _(act):
        def split_hi(m, k):
            act.wait_ge(raw_in[k], (m + 1) * 16)
            if not (isinstance(m, int) and m == 0):
                act.wait_ge(slab_used, m * RING + (k + 1 - RING))
            nc.scalar.activation(w_hi[:, k], raw[:, k], ACT.Copy).then_inc(hi_done, 1)

        def ahead(first, per, it, s):
            split_hi(*slab(first, per, it, s + AHEAD))

        def tile_done(first, per, it, s):
            m, k = slab(first, per, it, s)
            act.wait_ge(slab_used, m * RING + (k + 1))

        def steps(n):
            act.wait_ge(act_pro, n)

        for c in range(4):
            act.wait_ge(x_land[c], 16)
            nc.scalar.activation(x_sq[:, 4 * c:4 * c + 4], x_in[:, 4 * c:4 * c + 4],
                                 ACT.Square).then_inc(n_sq, 1)
        act.wait_ge(cst_land, 16)
        act.wait_ge(n_ms, 1)
        nc.scalar.activation(x_rs[:, :], b_ms[:, 0:T], ACT.Ln, bias=eps, scale=1.0 / D).then_inc(n_ln, 1)
        act.wait_ge(n_ln, 1)
        nc.scalar.activation(x_rs[:, :], x_rs[:, :], ACT.Exp, scale=-0.5).then_inc(n_rs, 1)
        for c in range(4):
            act.wait_ge(n_xn, 4 * c + 4)
            nc.scalar.activation(h_hi[:, 4 * c:4 * c + 4], hn32[:, 4 * c:4 * c + 4],
                                 ACT.Copy).then_inc(n_hi, 1)
        for k in range(AHEAD):
            split_hi(0, k)
        act.wait_ge(cols_land, 32)
        nc.scalar.activation(an[:, :], hv[:, 1:2], ACT.Exp).then_inc(act_pro, 1)
        act.wait_ge(dve_pro, 2)
        nc.scalar.activation(lbm[:, 1:3], lbm[:, 1:3], ACT.Exp).then_inc(act_pro, 1)
        act.wait_ge(pe_pro, 1)
        nc.scalar.activation(dtz[:, :], b_tv[0:HD, 0:T], ACT.Identity,
                             bias=hv[:, 0:1]).then_inc(act_pro, 1)
        act.wait_ge(dve_pro, 9)
        nc.scalar.activation(dte[:, :], dta[:, :], ACT.Exp, scale=-1.0).then_inc(act_pro, 1)
        steps(4)
        nc.scalar.activation(dte[:, :], dte[:, :], ACT.Ln, bias=one_col[0:HD]).then_inc(act_pro, 1)
        act.wait_ge(dve_pro, 15)
        nc.scalar.activation(ecum[:, :], cum[:, TP:T], ACT.Exp).then_inc(act_pro, 1)
        nc.scalar.activation(dtw[:, :], dtw[:, :], ACT.Exp).then_inc(act_pro, 1)
        act.wait_ge(pe_pro, 2)
        src = b_tk[:, 0:384].rearrange("p (q b h) -> p q b h", q=3, b=2)
        nc.scalar.activation(tok[:, :, 0:2, :], src, ACT.Copy).then_inc(act_pro, 1)
        src = b_diag[0:32, 0:192].rearrange("p (q h) -> p q h", q=3)
        nc.scalar.activation(tok[0:32, :, 2, :], src, ACT.Copy).then_inc(act_pro, 1)
        steps(9)

        def hgrn(it, first, gemm):
            r = it - 1

            def nxt(s):
                if gemm:
                    ahead(U_HG, HG_SLABS, it, s)

            if first:
                act.wait_ge(scr_out, 48)
            nxt(0)
            nxt(1)
            if not first:
                act.wait_ge(hg_tr, it)
                nc.scalar.activation(hvt[:, 0:2], b_tv[:, 0:256].rearrange("p (b n) -> p b n", b=2), ACT.Copy)
                nc.scalar.activation(hvt[0:32, 2], b_tv[0:32, 256:384], ACT.Copy)
                nc.scalar.activation(hkwt[:, 0:2], b_tk[:, 0:256].rearrange("p (b n) -> p b n", b=2), ACT.Copy)
                nc.scalar.activation(hkwt[0:32, 2], b_tk[0:32, 256:384], ACT.Copy)
                for dst, src in ((hv3[0:32], b_tv), (hv3[64:96], b_tv), (hk3[0:32], b_tk), (hk3[32:64], b_tk)):
                    op = nc.scalar.activation(dst, src[0:32, 256:384], ACT.Copy)
                op.then_inc(hg_tok, 1)
            if gemm:
                tile_done(U_HG, HG_SLABS, it, 1)
                nc.scalar.activation(hth[:, :], ps[0][:, 0:T], ACT.Tanh, scale=0.5).then_inc(evac, 1)
                nxt(2)
                act.wait_ge(hg_fk, it + 1)
                nc.scalar.activation(hlf[:, :], hf[:, :], ACT.Ln).then_inc(hg_lf, 1)
            nxt(3)
            if not first:
                act.wait_ge(hg_p2, it)
                nc.scalar.activation(hsq[:, :], b_o[:, 0:T], ACT.Square).then_inc(hg_sq, 1)
            if gemm:
                tile_done(U_HG, HG_SLABS, it, 3)
                nc.scalar.activation(hq[:, :], ps[1][:, 0:T], ACT.Copy).then_inc(evac, 1)
                nxt(4)
                act.wait_ge(hg_arg, it + 1)
                nc.scalar.activation(he[:, :], he[:, :], ACT.Exp)
                nc.scalar.activation(hkw[:, :], hcum[:, 0:TP], ACT.Exp, bias=hcum[:, TP - 1:TP], scale=-1.0)
                nc.scalar.activation(hkt[:, :], hcum[:, 0:P], ACT.Exp, bias=hcum[:, P - 1:P], scale=-1.0)
                nc.scalar.activation(hqt[:, :], hcum[:, P:TP], ACT.Exp, bias=hnc[:, 0:1])
                nc.scalar.activation(hec[:, :], hcum[:, TP:T], ACT.Exp).then_inc(hg_exp, 1)
            nxt(5)
            if not first:
                act.wait_ge(hg_ms, it)
                nc.scalar.activation(hrs[:, :], b_ms[:, 0:T], ACT.Ln, bias=eps, scale=1.0 / P).then_inc(hg_ln, 1)
                act.wait_ge(hg_ln, it)
                nc.scalar.activation(hrs[:, :], hrs[:, :], ACT.Exp, scale=-0.5).then_inc(hg_rs, 1)
            if gemm:
                tile_done(U_HG, HG_SLABS, it, 5)
                nc.scalar.activation(hvv[:, :], ps[0][:, 0:T], ACT.Copy).then_inc(evac, 1)
            if not first:
                act.wait_ge(hg_so, it)
            nxt(6)
            if not first:
                nc.scalar.activation(tile_at(o_hi, r), one(hso[:, :]), ACT.Copy).then_inc(hg_ohi, 1)
            nxt(7)
            if gemm:
                tile_done(U_HG, HG_SLABS, it, 7)
                nc.scalar.activation(htg[:, :], ps[1][:, 0:T], ACT.Tanh, scale=0.5)
                nc.scalar.activation(hg[:, :], ps[1][:, 0:T], ACT.Copy).then_inc(evac, 1)

        hgrn(0, True, True)
        with act.Fori(1, HEADS) as it:
            hgrn(it, False, True)
        hgrn(HEADS, False, False)

        def branch_b(j, first):
            ahead(U_GB, GB_SLABS, j, 0)
            ahead(U_GB, GB_SLABS, j, 1)
            tile_done(U_GB, GB_SLABS, j, 1)
            if not first:
                act.wait_ge(gb_mb, j)
            nc.scalar.activation(btg[:, :], ps[0][:, 0:T], ACT.Tanh, scale=0.5).then_inc(evac, 1)
            ahead(U_GB, GB_SLABS, j, 2)
            ahead(U_GB, GB_SLABS, j, 3)
            tile_done(U_GB, GB_SLABS, j, 3)
            nc.scalar.activation(byb[:, :], ps[1][:, 0:T], ACT.Copy).then_inc(evac, 1)

        branch_b(0, True)
        with act.Fori(1, KT) as j:
            branch_b(j, False)

        def ssd(g, first, gemm):
            def nxt(s):
                if gemm:
                    ahead(U_SG, SG_SLABS, g, s)

            def conv_in(c):
                tile_done(U_SG, SG_SLABS, g, 2 * c + 1)
                if c >= 2 or not first:
                    act.wait_ge(sg_nc, g * XT + (c - 1))
                dst = craw[:, c % 2]
                nc.scalar.activation(dst[:, CW - 1:SOFF], ps[c % 2][:, 0:TP], ACT.Copy)
                seqs = dst[:, SOFF:RAWC].rearrange("p (b s) -> p b s", b=NB)
                nc.scalar.activation(seqs[:, :, CW - 1:], ps[c % 2][:, TP:T].rearrange("p (b s) -> p b s", b=NB),
                                     ACT.Copy).then_inc(evac, 1)

            def conv_tanh(c):
                act.wait_ge(sg_conv, g * XT + c + 1)
                nc.scalar.activation(cth[:, 0:TP], ccv[:, 0:TP], ACT.Tanh)
                nc.scalar.activation(cth[:, TP:T].rearrange("p (b s) -> p b s", b=NB), cv_samples,
                                     ACT.Tanh).then_inc(sg_th, 1)

            def z_in(c):
                tile_done(U_SG, SG_SLABS, g, 13 + 2 * c)
                act.wait_ge(sg_silu, (g + 1) * XT) if c == 0 else act.wait_ge(sg_sz, g * 4 + c)
                nc.scalar.activation(cth[:, :], ps[c % 2][:, 0:T], ACT.Tanh, scale=0.5)
                nc.scalar.activation(sz[:, c], ps[c % 2][:, 0:T], ACT.Copy, scale=0.5).then_inc(evac, 1)

            for s in range(SG_SLABS):
                if not gemm and s > 10:
                    break
                nxt(s)
                if not first and s == 8:
                    act.wait_ge(sg_g, g)
                    nc.scalar.activation(ysq, yf[:, :, :], ACT.Square).then_inc(sg_sq, 1)
                if not first and s == 10:
                    act.wait_ge(sg_ms, g)
                    nc.scalar.activation(yrs[:, :], b_o[:, 0:T], ACT.Ln, bias=eps, scale=1.0 / 512).then_inc(sg_ln, 1)
                    act.wait_ge(sg_ln, g)
                    nc.scalar.activation(yrs[:, :], yrs[:, :], ACT.Exp, scale=-0.5).then_inc(sg_rs, 1)
                if not gemm:
                    continue
                if s % 2 == 0 and 2 <= s <= 12:
                    conv_tanh(s // 2 - 1)
                if s == 7:
                    act.wait_ge(sg_bc, g + 1)
                    nc.scalar.activation(bt[:, 0:2], bank[0][:, 0:256].rearrange("p (b n) -> p b n", b=2), ACT.Copy)
                    for dst in (bt[0:32, 2], bt3[0:32], bt3[32:64]):
                        op = nc.scalar.activation(dst, bank[0][0:32, 256:384], ACT.Copy)
                    op.then_inc(sg_bt, 1)
                if s in (13, 15):
                    q = (s - 13) // 2
                    act.wait_ge(sg_seg, 2 * g + q + 1)
                    nc.scalar.activation(me[:, 4 * q:4 * q + 4, 0:384], me[:, 4 * q:4 * q + 4, 0:384], ACT.Exp)
                    nc.scalar.activation(me[0:32, 4 * q:4 * q + 4, 384:416], me[0:32, 4 * q:4 * q + 4, 384:416],
                                         ACT.Exp).then_inc(sg_exp, 1)
                if s == 17:
                    act.wait_ge(sg_xd, g + 1)
                    nc.scalar.activation(xw3[0:32], xw[0:32, 2], ACT.Copy)
                    nc.scalar.activation(xw3[64:96], xw[0:32, 2], ACT.Copy).then_inc(sg_xwhi, 1)
                if s == 18:
                    act.wait_ge(sg_sp, g + 1)
                    if not first:
                        act.wait_ge(sg_sp_out, g * 16)
                    nc.scalar.activation(ssp[:, :, :], bank[1][:, :].rearrange("p (b n) -> p b n", b=4),
                                         ACT.Copy).then_inc(sg_spe, 1)
                if s % 2 == 1 and s < 12:
                    conv_in(s // 2)
                if s % 2 == 1 and s > 12:
                    z_in((s - 13) // 2)

        act.wait_ge(sg_raw0, 1)
        ssd(0, True, True)
        with act.Fori(1, GROUPS) as g:
            ssd(g, False, True)
        ssd(GROUPS, False, False)

        for i in range(4):
            act.wait_ge(sg_ht_out[i], 32 * GROUPS)
        act.wait_ge(sg_nc_out, 16 * GROUPS)
        act.wait_ge(sg_sp_out, 16 * GROUPS)
        for c in range(8):
            act.wait_ge(sg_y32, GROUPS)
            nc.scalar.activation(y_hi[:, 4 * c:4 * c + 4], y32[:, 4 * c:4 * c + 4], ACT.Copy).then_inc(y_his, 1)

        def branch_a(i, first):
            for j in range(2):
                t = 2 * i + j
                s0 = GA_SLABS * j
                ahead(U_GA, 2 * GA_SLABS, i, s0)
                ahead(U_GA, 2 * GA_SLABS, i, s0 + 1)
                tile_done(U_GA, 2 * GA_SLABS, i, s0 + 1)
                if not (first and j == 0):
                    act.wait_ge(ga_lo, t)
                nc.scalar.activation(atg[:, :], ps[0][:, 0:T], ACT.Tanh, scale=0.5).then_inc(evac, 1)
                for s in range(2, 6):
                    ahead(U_GA, 2 * GA_SLABS, i, s0 + s)
                tile_done(U_GA, 2 * GA_SLABS, i, s0 + 5)
                nc.scalar.activation(aya[:, :], ps[1][:, 0:T], ACT.Copy).then_inc(evac, 1)
                act.wait_ge(ga_m, t + 1)
                nc.scalar.activation(tile_at(m_hi, t), one(aya[:, :]), ACT.Copy, scale=0.5).then_inc(ga_hi, 1)

        branch_a(0, True)
        with act.Fori(1, KT // 2) as i:
            branch_a(i, False)

        def out_tiles(i, first):
            for j in range(2):
                t = 2 * i + j
                ahead(U_OUT, 4, i, 2 * j)
                ahead(U_OUT, 4, i, 2 * j + 1)
                tile_done(U_OUT, 4, i, 2 * j + 1)
                if not (first and j == 0):
                    act.wait_ge(o_acc, t)
                nc.scalar.activation(tmp[:, :], ps[j][:, 0:T], ACT.Square)
                nc.scalar.activation(tile_at(mo, t), one(ps[j][:, 0:T]), ACT.Copy).then_inc(evac, 1)

        out_tiles(0, True)
        with act.Fori(1, KT // 2) as i:
            out_tiles(i, False)

        def rstd(n, count):
            act.wait_ge(n_ms, n)
            nc.scalar.activation(nrs[:, :], b_ms[:, 0:T], ACT.Ln, bias=eps, scale=1.0 / count).then_inc(n_ln, 1)
            act.wait_ge(n_ln, n)
            nc.scalar.activation(nrs[:, :], nrs[:, :], ACT.Exp, scale=-0.5).then_inc(n_rs, 1)

        def norm_in(n, sq, base_x):
            for c in range(4):
                act.wait_ge(x2_b, base_x + 4 * c + 4)
                nc.scalar.activation(sq[:, 4 * c:4 * c + 4], x2[:, 4 * c:4 * c + 4], ACT.Square).then_inc(n_sq, 1)
            rstd(n, D)
            for c in range(4):
                act.wait_ge(n_xn, KT * (n // 2) + 4 * c + 4)
                nc.scalar.activation(h_hi[:, 4 * c:4 * c + 4], sq[:, 4 * c:4 * c + 4], ACT.Copy).then_inc(n_hi, 1)

        rstd(2, D)
        norm_in(3, nsq, 0)

        def up(i, first, half):
            for j in range(2):
                t = 2 * i + j
                tt = FT * half + t
                fu = U_FFN + HALF_U * half
                ahead(fu, 4, i, 2 * j)
                ahead(fu, 4, i, 2 * j + 1)
                tile_done(fu, 4, i, 2 * j + 1)
                if not (first and half == 0 and j == 0):
                    act.wait_ge(up_lo, tt)
                nc.scalar.activation(ru[j][:, :], ps[j][:, 0:T], ACT.Relu).then_inc(evac, 1)
                act.wait_ge(up_sq, tt + 1)
                nc.scalar.activation(tile_at(u_hi, t), one(tmp[:, :]), ACT.Copy).then_inc(up_hi, 1)

        def down(i, first, half):
            for j in range(2):
                t = 2 * i + j
                fd = U_FFN + HALF_U * half + 2 * FT
                for s in range(4):
                    ahead(fd, 8, i, 4 * j + s)
                tile_done(fd, 8, i, 4 * j + 3)
                if half == 0:
                    nc.scalar.activation(tile_at(ffn, t), one(ps[j][:, 0:T]), ACT.Copy).then_inc(evac, 1)
                else:
                    if not (first and j == 0):
                        act.wait_ge(dn_acc, t)
                    nc.scalar.activation(tmp[:, :], ps[j][:, 0:T], ACT.Copy).then_inc(evac, 1)
                    act.wait_ge(dn_add, t + 1)
                    nc.scalar.activation(one(tmp[:, :]), tile_at(ffn, t), ACT.Square).then_inc(dn_sq, 1)

        for half in range(2):
            up(0, True, half)
            with act.Fori(1, FT // 2) as i:
                up(i, False, half)
            down(0, True, half)
            with act.Fori(1, KT // 2) as i:
                down(i, False, half)

        rstd(4, D)
        act.wait_ge(p_land, 16)
        nc.scalar.activation(p_hi[:, :, :], p_in[:, :, :], ACT.Copy).then_inc(p_his, 1)
        for s in range(4):
            ahead(U_PROJ, 4, 0, s)
            for j in range(4):
                if j < 3:
                    act.wait_ge(pj_tile, 3 * s + j + 1)
                else:
                    act.wait_ge(slab_used, U_PROJ + s + 1)
                nc.scalar.activation(e_out[:, 4 * s + j], ps[j % 2][:, 0:T], ACT.Copy).then_inc(evac, 1)
        norm_in(5, nsq3, KT)

        def ple(i, first, last):
            for j in range(2):
                t = 2 * i + j
                for s in (2 * j, 2 * j + 1):
                    if not (last and s + AHEAD >= 4):
                        ahead(U_PLE, 4, i, s)
                tile_done(U_PLE, 4, i, 2 * j + 1)
                if not first:
                    act.wait_ge(g_y, t - 1)
                nc.scalar.activation(gtg[:, j], ps[j][:, 0:T], ACT.Tanh, scale=0.5).then_inc(evac, 1)

        ple(0, True, False)
        with act.Fori(1, KT // 2 - 1) as i:
            ple(i, False, False)
        ple(KT // 2 - 1, False, True)

    @block.vector
    def _(dve):
        V = nc.vector

        def split_lo(m, k):
            dve.wait_ge(hi_done, m * RING + (k + 1))
            V.tensor_tensor(w_lo[:, k], raw[:, k], w_hi[:, k].bitcast(F32), ALU.subtract).then_inc(lo_done, 1)

        def ahead(first, per, it, s):
            split_lo(*slab(first, per, it, s + AHEAD))

        def steps(n):
            dve.wait_ge(dve_pro, n)

        dve.wait_ge(cols_land, 32)
        lb2 = cols[:, C_LB:C_LB + 32].rearrange("p (r h) -> p r h", r=2)
        V.tensor_tensor(lbm[:, 0], lb2[:, 0], lb2[:, 1], ALU.max).then_inc(dve_pro, 1)
        steps(1)
        V.tensor_tensor(lbm[:, 1:3], lb2, lbm[:, 0:1].to_broadcast([P, 2, HEADS]),
                        ALU.subtract).then_inc(dve_pro, 1)
        dve.wait_ge(n_rs, 1)
        for t in range(KT):
            V.scalar_tensor_tensor(hn32[:, t], x_in[:, t], cols[:, C_MIXPRE + t:C_MIXPRE + t + 1], x_rs[:, :],
                                   ALU.mult, ALU.mult).then_inc(n_xn, 1)
        for c in range(4):
            dve.wait_ge(n_hi, c + 1)
            V.tensor_tensor(h_lo[:, 4 * c:4 * c + 4], hn32[:, 4 * c:4 * c + 4],
                            h_hi[:, 4 * c:4 * c + 4].bitcast(F32), ALU.subtract).then_inc(n_lo, 1)
        for k in range(AHEAD):
            split_lo(0, k)
        dve.wait_ge(act_pro, 2)
        V.tensor_tensor(lbm[:, 3], lbm[:, 1], lbm[:, 2], ALU.add).then_inc(dve_pro, 1)
        steps(3)
        V.reciprocal(lbm[:, 3], lbm[:, 3]).then_inc(dve_pro, 1)
        steps(4)
        V.tensor_tensor(lbm[:, 0], lbm[:, 1], lbm[:, 3], ALU.mult).then_inc(dve_pro, 1)
        steps(5)
        V.tensor_scalar(lbc[:, :, 0], lbm[:, 0], 0.5, 0.5, ALU.mult, ALU.add).then_inc(dve_pro, 1)
        V.tensor_scalar(lbc[:, :, 1], lbm[:, 0], -0.5, 0.5, ALU.mult, ALU.add).then_inc(dve_pro, 1)
        V.tensor_scalar(lbc[:, :, 2], lbm[:, 0], 0.5, -0.5, ALU.mult, ALU.add).then_inc(dve_pro, 1)
        dve.wait_ge(act_pro, 3)
        V.scalar_tensor_tensor(dta[:, :], dtz[:, :], -1.0, dtz[:, :], ALU.mult, ALU.max).then_inc(dve_pro, 1)
        V.tensor_scalar(an[:, :], an[:, :], -1.0, None, ALU.mult).then_inc(dve_pro, 1)
        dve.wait_ge(act_pro, 5)
        V.scalar_tensor_tensor(dts[:, :], dtz[:, :], 0.0, dte[:, :], ALU.max, ALU.add).then_inc(dve_pro, 1)
        steps(11)
        V.tensor_scalar(dta[:, :], dts[:, :], an[:, 0:1], None, ALU.mult).then_inc(dve_pro, 1)
        steps(12)
        V.tensor_tensor_scan(cum[:, :], consts[0:HD, K_RESET:K_RESET + T], dta[:, :], 0.0,
                             ALU.mult, ALU.add).then_inc(dve_pro, 1)
        steps(13)
        V.tensor_scalar(dtw[:, 0:TP], cum[:, 0:TP], cum[:, TP - 1:TP], -1.0,
                        ALU.subtract, ALU.mult).then_inc(dve_pro, 1)
        cs = blocks(cum[:, TP:T], NB)
        V.tensor_tensor(blocks(dtw[:, TP:T], NB), cs[:, :, SB - 1:SB].to_broadcast([HD, NB, SB]), cs,
                        ALU.subtract).then_inc(dve_pro, 1)
        dve.wait_ge(act_pro, 7)
        V.tensor_tensor(dtw[:, :], dtw[:, :], dts[:, :], ALU.mult).then_inc(dve_pro, 1)
        V.tensor_copy(elast[:, :].rearrange("p (b a) -> p b a", a=1),
                      blocks(ecum[:, :], NB)[:, :, SB - 1:SB]).then_inc(dve_pro, 1)

        def level(buf, off, h):
            width = T if h <= 2 else TP
            return buf[:, off:off + width].rearrange("p (b a j) -> p b a j", a=2, j=h)

        def hgrn(it, first, gemm):
            def nxt(s):
                if gemm:
                    ahead(U_HG, HG_SLABS, it, s)

            nxt(0)
            nxt(1)
            if not first:
                dve.wait_ge(hg_tok, it)
                V.tensor_tensor(hv3[32:64], hvt[0:32, 2], hv3[0:32].bitcast(F32), ALU.subtract)
                V.tensor_tensor(hk3[64:96], hkwt[0:32, 2], hk3[0:32].bitcast(F32),
                                ALU.subtract).then_inc(hg_tlo, 1)
                dve.wait_ge(hg_attn, it)
                V.tensor_tensor(hdm[:, :], b_diag[:, 0:384], consts[:, K_DIAG:K_DIAG + 384], ALU.mult)
                V.tensor_tensor(hdms[:, :], b_diag[0:32, 384:480], consts[0:32, K_DIAGS:K_DIAGS + 96],
                                ALU.mult).then_inc(hg_dm, 1)
                dve.wait_ge(hg_dm, it)
                V.tensor_reduce(hab[:, :, :], hdm[:, :].rearrange("p (l b t) -> p b t l", b=2, t=32),
                                AX.X, ALU.add)
                V.tensor_reduce(hats[:, :], hdms[:, :].rearrange("p (l t) -> p t l", t=32),
                                AX.X, ALU.add).then_inc(hg_red, 1)
                att = b_att[:, 0:256].rearrange("p (b t) -> p b t", b=2)
                V.tensor_copy(hatt[0:64, :, 64:128], att[0:64, :, 64:128])
                V.tensor_copy(hatt[0:32, :, 32:64], att[0:32, :, 32:64])
                V.tensor_copy(hatt[64:96, :, 96:128], att[64:96, :, 96:128])
                V.tensor_copy(htop[:, :], b_att[:, 256:384])
                dve.wait_ge(hg_red, it)
                for q in range(4):
                    op = V.tensor_copy(hatt[32 * q:32 * q + 32, :, 32 * q:32 * q + 32],
                                       hab[32 * q:32 * q + 32, :, :])
                op.then_inc(hg_ab, 1)
            if gemm:
                nxt(2)
                dve.wait_ge(evac, T_HG + it * HG_TILES + 1)
                V.tensor_copy(one(hcur[:, :]), tile_at(lbc, it)).then_inc(hg_cur, 1)
                dve.wait_ge(hg_cur, it + 1)
                V.tensor_scalar(hf[:, :], hth[:, :], hcur[:, 1:2], hcur[:, 0:1], ALU.mult, ALU.add)
                V.tensor_scalar(hk[:, :], hth[:, :], hcur[:, 2:3], hcur[:, 1:2], ALU.mult,
                                ALU.add).then_inc(hg_fk, 1)
                nxt(3)
                dve.wait_ge(hg_lf, it + 1)
                V.tensor_tensor_scan(hcum[:, :], consts[:, K_RESET:K_RESET + T], hlf[:, :], 0.0,
                                     ALU.mult, ALU.add).then_inc(hg_cum, 1)
                dve.wait_ge(hg_cum, it + 1)
                V.tensor_scalar(hnc[:, :], hcum[:, P - 1:P], -1.0, None, ALU.mult)
                for h in LEVELS:
                    c4 = level(hcum, 0, h)
                    e4 = level(he, LOFF[h], h)
                    nb = (T if h <= 2 else TP) // (2 * h)
                    ref = c4[:, :, 0, h - 1:h].to_broadcast([P, nb, h])
                    V.tensor_tensor(e4[:, :, 1, :], c4[:, :, 1, :], ref, ALU.subtract)
                    V.tensor_tensor(e4[:, :, 0, :], ref, c4[:, :, 0, :], ALU.subtract)
                c3 = blocks(hcum[:, TP:T], NB)
                V.tensor_tensor(blocks(he[:, LAST_OFF:LAST_OFF + TS], NB),
                                c3[:, :, SB - 1:SB].to_broadcast([P, NB, SB]), c3,
                                ALU.subtract).then_inc(hg_arg, 1)
            nxt(4)
            if not first:
                dve.wait_ge(hg_p2, it)
                dve.wait_ge(hg_s0, it * 16)
                for b in range(NB):
                    half = (b_tv, b_tk)[b // 4]
                    V.scalar_tensor_tensor(hsn[:, b], hs0[:, b], hel[:, b:b + 1],
                                           half[:, P * (b % 4):P * (b % 4) + P], ALU.mult, ALU.add)
                V.tensor_copy(hsp[:, :], b_att[:, 3 * P:4 * P]).then_inc(hg_st, 1)
            if gemm:
                nxt(5)
                dve.wait_ge(hg_exp, it + 1)
                if not first:
                    dve.wait_ge(hg_st, it)
                for h in LEVELS:
                    e4, k4, q4 = level(he, LOFF[h], h), level(hk, 0, h), level(hq, 0, h)
                    V.tensor_tensor(e4[:, :, 0, :], e4[:, :, 0, :], k4[:, :, 0, :], ALU.mult)
                    V.tensor_tensor(e4[:, :, 1, :], e4[:, :, 1, :], q4[:, :, 1, :], ALU.mult)
                V.tensor_tensor(hkw[:, :], hkw[:, :], hk[:, 0:TP], ALU.mult)
                V.tensor_tensor(hkt[:, :], hkt[:, :], hk[:, 0:P], ALU.mult)
                V.tensor_tensor(hqt[:, :], hqt[:, :], hq[:, P:TP], ALU.mult)
                V.tensor_tensor(hqs[:, :], hec[:, :], hq[:, TP:T], ALU.mult)
                V.tensor_tensor(hks[:, :], he[:, LAST_OFF:LAST_OFF + TS], hk[:, TP:T], ALU.mult)
                V.tensor_copy(hel[:, :].rearrange("p (b a) -> p b a", a=1),
                              blocks(hec[:, :], NB)[:, :, SB - 1:SB]).then_inc(hg_w, 1)
            if not first:
                dve.wait_ge(hg_rs, it)
                V.scalar_tensor_tensor(hsg[:, :], htg[:, :], 1.0, hg[:, :], ALU.add, ALU.mult)
                V.scalar_tensor_tensor(hon[:, :], b_o[:, 0:T], cols[:, C_HGN:C_HGN + 1], hrs[:, :],
                                       ALU.mult, ALU.mult).then_inc(hg_on, 1)
                dve.wait_ge(hg_on, it)
                V.scalar_tensor_tensor(hso[:, :], hon[:, :], 0.5, hsg[:, :], ALU.mult,
                                       ALU.mult).then_inc(hg_so, 1)
            nxt(6)
            if not first:
                dve.wait_ge(hg_ohi, it)
                V.tensor_tensor(tile_at(o_lo, it - 1), one(hso[:, :]), tile_at(o_hi, it - 1).bitcast(F32),
                                ALU.subtract).then_inc(hg_olo, 1)
            nxt(7)

        dve.wait_ge(scr_out, 48)
        dve.wait_ge(act_pro, 9)
        V.memset(hatt[:, :, :], 0.0).then_inc(hg_zero, 1)
        dve.wait_ge(hg_zero, 1)
        hgrn(0, True, True)
        with dve.Fori(1, HEADS) as it:
            hgrn(it, False, True)
        hgrn(HEADS, False, False)

        def branch_b(j, first):
            for s in range(GB_SLABS):
                ahead(U_GB, GB_SLABS, j, s)
            dve.wait_ge(evac, j * 2 + (T_GB + 2))
            if not first:
                dve.wait_ge(gb_out, j * 16)
            V.scalar_tensor_tensor(bmb[:, :], btg[:, :], 1.0, byb[:, :], ALU.add, ALU.mult).then_inc(gb_mb, 1)

        branch_b(0, True)
        with dve.Fori(1, KT) as j:
            branch_b(j, False)

        def cur_cols(first_col, g):
            if isinstance(g, int):
                return cols[:, first_col + 4 * g:first_col + 4 * g + 4]
            return cols[:, bass.ds(g * 4 + first_col, 4)]

        def ssd(g, first, gemm):
            r = g - 1

            def y_pair(gg, p):
                dve.wait_ge(sg_y, gg * 4 + (p + 1))
                V.scalar_tensor_tensor(yf[:, p], xf[:, p], dcur[:, p:p + 1], bank[(5, 0)[p % 2]][:, 0:T],
                                       ALU.mult, ALU.add).then_inc(sg_yf, 1)

            def silu_z(gg, c):
                dve.wait_ge(evac, gg * SG_TILES + (T_SG + 7 + c))
                V.scalar_tensor_tensor(sz[:, c], cth[:, :], 1.0, sz[:, c], ALU.add, ALU.mult).then_inc(sg_sz, 1)

            def update(b):
                for i in (b, b + 1):
                    v = ht[:, i % 4].rearrange("p (h d) -> p h d", h=GH)
                    V.tensor_tensor(v, v, el[:, :, i:i + 1].to_broadcast([P, GH, HD]), ALU.mult).then_inc(sg_upa, 1)
                for i in (b, b + 1):
                    dve.wait_ge(sg_upa, r * NB + (i + 1))
                    dve.wait_ge(sg_su, r * NB + (i + 1))
                    V.tensor_tensor(ht[:, i % 4], ht[:, i % 4], bank[2 + i % 2][:, :], ALU.add).then_inc(sg_up, 1)

            def conv(c):
                n = g * (4 * XT) + 4 * c
                dve.wait_ge(evac, g * SG_TILES + (T_SG + 1 + c))
                src = craw[:, c % 2]
                seqs = blocks(src[:, SOFF:RAWC], NB)
                V.tensor_copy(seqs[:, :, 0:CW - 1], cst[:, c]).then_inc(sg_cv, 1)
                dve.wait_ge(sg_cv, n + 1)
                V.tensor_scalar(ccv[:, 0:CVC], src[:, 0:CVC], prh[:, c, 0:1], prh[:, c, CW:CW + 1],
                                ALU.mult, ALU.add).then_inc(sg_cv, 1)
                for w in range(1, CW):
                    dve.wait_ge(sg_cv, n + (w + 1))
                    op = V.scalar_tensor_tensor(ccv[:, 0:CVC], src[:, w:w + CVC], prh[:, c, w:w + 1],
                                                ccv[:, 0:CVC], ALU.mult, ALU.add)
                    op.then_inc(sg_cv if w < CW - 1 else sg_conv, 1)
                V.tensor_copy(ncv[:, c, 0:CW - 1], src[:, TP:SOFF])
                V.tensor_copy(blocks(ncv[:, c, CW - 1:], NB), seqs[:, :, SB:]).then_inc(sg_nc, 1)

            def silu(c):
                dst = (bf[:, :], cf[:, :])[c] if c < 2 else xf[:, c - 2]
                dve.wait_ge(sg_th, g * XT + (c + 1))
                V.scalar_tensor_tensor(dst[:, 0:TP], cth[:, 0:TP], 1.0, ccv[:, 0:TP], ALU.add, ALU.mult)
                V.scalar_tensor_tensor(blocks(dst[:, TP:T], NB), blocks(cth[:, TP:T], NB), 1.0, cv_samples,
                                       ALU.add, ALU.mult).then_inc(sg_silu, 1)

            for s in range(SG_SLABS):
                if not gemm and s > 11:
                    break
                if not first:
                    if s == 0:
                        y_pair(r, 3)
                        silu_z(r, 3)
                        dve.wait_ge(sg_yf, g * 4)
                        dve.wait_ge(sg_sz, g * 4)
                    if s == 1:
                        dve.wait_ge(sg_ec_in, g * 48)
                        dve.wait_ge(sg_it, r * 2 + 1)
                    if s == 6:
                        dve.wait_ge(sg_it, r * 2 + 2)
                    if s in (1, 2, 6, 7):
                        update({1: 0, 2: 2, 6: 4, 7: 6}[s])
                    if s == 7:
                        V.tensor_tensor(yti[:, :, :], blocks(bank[4][:, T:T + 4 * TS], 4), ecp[:, :, :],
                                        ALU.mult).then_inc(sg_yi, 1)
                        dve.wait_ge(sg_yi, r * 2 + 1)
                        V.tensor_tensor(yf[:, :, TP:T], yf[:, :, TP:T], yti[:, :, :], ALU.add).then_inc(sg_yi, 1)
                        dve.wait_ge(sg_yi, r * 2 + 2)
                        V.tensor_tensor(yf[:, :, :], yf[:, :, :], sz[:, :, :], ALU.mult).then_inc(sg_g, 1)
                    if s == 11:
                        V.tensor_copy(ncur[:, :], cur_cols(C_SSMN, r)).then_inc(sg_ncur, 1)
                        dve.wait_ge(sg_ncur, g)
                        dve.wait_ge(sg_rs, g)
                        for p in range(4):
                            dst = y32[:, 4 * r + p:4 * r + p + 1] if not gemm else y32[:, bass.ds(r * 4 + p, 1)]
                            op = V.scalar_tensor_tensor(dst, yf[:, p:p + 1], ncur[:, p:p + 1], one(yrs[:, :]),
                                                        ALU.mult, ALU.mult)
                        op.then_inc(sg_y32, 1)
                if not gemm:
                    continue
                if s % 2 == 1 and 3 <= s <= 13:
                    silu(s // 2 - 1)
                ahead(U_SG, SG_SLABS, g, s)
                if s == 0:
                    dve.wait_ge(sg_par_in, (g + 1) * 32)
                    V.tensor_scalar(prh[:, :, :], prm[:, :, :], 0.5, None, ALU.mult).then_inc(sg_prh, 1)
                    hs = slice(GH * g, GH * g + GH) if isinstance(g, int) else bass.ds(g * GH, GH)
                    V.tensor_copy(tcur[:, :, 0:2, :], tok[:, :, 0:2, hs])
                    V.tensor_copy(tcur[0:32, :, 2, :], tok[0:32, :, 2, hs])
                    V.tensor_copy(dcur[:, :], cur_cols(C_DSKIP, g)).then_inc(sg_cur, 1)
                    dve.wait_ge(sg_prh, g + 1)
                    dve.wait_ge(sg_cur, g + 1)
                    if not first:
                        dve.wait_ge(sg_nc_out, g * 16)
                if s % 2 == 0 and 2 <= s <= 12:
                    conv(s // 2 - 1)
                if s == 8:
                    if not first:
                        dve.wait_ge(sg_it, g * 2)
                    dve.wait_ge(sg_silu, g * XT + 2)
                    V.tensor_copy(cfs[:, :], cf[:, TP:T]).then_inc(sg_cfs, 1)
                if s == 8:
                    dve.wait_ge(sg_bt, g + 1)
                    V.tensor_tensor(bt3[64:96], bt[0:32, 2], bt3[0:32].bitcast(F32),
                                    ALU.subtract).then_inc(sg_btlo, 1)
                    dve.wait_ge(sg_bc, g + 1)
                    V.tensor_tensor(cbm[:, 0:384], bank[1][:, 0:384], consts[:, K_CB:K_CB + 384], ALU.mult)
                    V.tensor_tensor(cbm[0:32, 384:416], bank[1][0:32, 384:416],
                                    consts[0:32, K_CB + 384:K_CB + 416], ALU.mult).then_inc(sg_cbm, 1)
                if s in (14, 16):
                    q = (s - 14) // 2
                    dve.wait_ge(sg_exp, g * 2 + (q + 1))
                    if q == 0:
                        dve.wait_ge(sg_cbm, g + 1)
                    v = me[:, 4 * q:4 * q + 4, 0:384]
                    V.tensor_tensor(v, v, cbm[:, 0:384].unsqueeze(1).to_broadcast([P, 4, 384]), ALU.mult)
                    v = me[0:32, 4 * q:4 * q + 4, 384:416]
                    V.tensor_tensor(v, v, cbm[0:32, 384:416].unsqueeze(1).to_broadcast([32, 4, 32]),
                                    ALU.mult).then_inc(sg_m, 1)
                if s == 15:
                    dve.wait_ge(sg_xt, g + 1)
                    for b in range(3):
                        n = 32 if b == 2 else P
                        src = bank[2 + b][0:n, :].rearrange("p (h d) -> p h d", h=GH)
                        for dst, q in ((xd, 0), (xw, 2)):
                            op = V.tensor_tensor(dst[0:n, b].rearrange("p (h d) -> p h d", h=GH), src,
                                                 tcur[0:n, q, b, :].unsqueeze(2).to_broadcast([n, GH, HD]), ALU.mult)
                    op.then_inc(sg_xd, 1)
                if s in (14, 16, 18):
                    silu_z(g, (s - 14) // 2)
                if s == 18:
                    dve.wait_ge(sg_xwhi, g + 1)
                    V.tensor_tensor(xw3[32:64], xw[0:32, 2], xw3[0:32].bitcast(F32),
                                    ALU.subtract).then_inc(sg_xwlo, 1)
                if s in (17, 18, 19):
                    y_pair(g, s - 17)

        dve.wait_ge(slab_used, U_SG)
        dve.wait_ge(hg_out, 32 * HEADS)
        dve.wait_ge(gb_out, 16 * KT)
        V.memset(craw[:, :, 0:CW - 1], 0.0).then_inc(sg_raw0, 1)
        dve.wait_ge(sg_raw0, 1)
        ssd(0, True, True)
        with dve.Fori(1, GROUPS) as g:
            ssd(g, False, True)
        ssd(GROUPS, False, False)

        for c in range(8):
            dve.wait_ge(y_his, c + 1)
            V.tensor_tensor(y_lo[:, 4 * c:4 * c + 4], y32[:, 4 * c:4 * c + 4],
                            y_hi[:, 4 * c:4 * c + 4].bitcast(F32), ALU.subtract).then_inc(y_los, 1)

        def branch_a(i, first):
            for j in range(2):
                t = i * 2 + j
                for s in range(GA_SLABS):
                    ahead(U_GA, 2 * GA_SLABS, i, GA_SLABS * j + s)
                dve.wait_ge(evac, t * 2 + (T_GA + 2))
                dve.wait_ge(ga_in, t * 16 + 16)
                V.scalar_tensor_tensor(aya[:, :], atg[:, :], 1.0, aya[:, :], ALU.add, ALU.mult).then_inc(ga_t, 1)
                dve.wait_ge(ga_t, t + 1)
                V.tensor_tensor(aya[:, :], aya[:, :], amb[:, :], ALU.add).then_inc(ga_m, 1)
                dve.wait_ge(ga_hi, t + 1)
                V.scalar_tensor_tensor(tile_at(m_lo, t), one(aya[:, :]), 0.5, tile_at(m_hi, t).bitcast(F32),
                                       ALU.mult, ALU.subtract).then_inc(ga_lo, 1)

        branch_a(0, True)
        with dve.Fori(1, KT // 2) as i:
            branch_a(i, False)

        def out_tiles(i, first):
            for j in range(2):
                t = i * 2 + j
                ahead(U_OUT, 4, i, 2 * j)
                ahead(U_OUT, 4, i, 2 * j + 1)
                dve.wait_ge(evac, t + (T_OUT + 1))
                if first and j == 0:
                    V.tensor_copy(acc[:, :], tmp[:, :]).then_inc(o_acc, 1)
                else:
                    dve.wait_ge(o_acc, t)
                    V.tensor_tensor(acc[:, :], acc[:, :], tmp[:, :], ALU.add).then_inc(o_acc, 1)

        out_tiles(0, True)
        with dve.Fori(1, KT // 2) as i:
            out_tiles(i, False)

        def add_normed(c, src, col, residual, base_x):
            for t in range(4 * c, 4 * c + 4):
                op = V.scalar_tensor_tensor(src[:, t], src[:, t], cols[:, col + t:col + t + 1], nrs[:, :],
                                            ALU.mult, ALU.mult)
            op.then_inc(x2_a, 1)
            dve.wait_ge(x2_a, base_x // 4 + c + 1)
            for t in range(4 * c, 4 * c + 4):
                V.tensor_tensor(x2[:, t], src[:, t], residual[:, t], ALU.add).then_inc(x2_b, 1)

        def norm_out(n, sq, col):
            dve.wait_ge(n_rs, n)
            for t in range(KT):
                V.scalar_tensor_tensor(sq[:, t], x2[:, t], cols[:, col + t:col + t + 1], nrs[:, :],
                                       ALU.mult, ALU.mult).then_inc(n_xn, 1)
            for c in range(4):
                dve.wait_ge(n_hi, 4 * (n // 2) + c + 1)
                V.tensor_tensor(h_lo[:, 4 * c:4 * c + 4], sq[:, 4 * c:4 * c + 4],
                                h_hi[:, 4 * c:4 * c + 4].bitcast(F32), ALU.subtract).then_inc(n_lo, 1)

        dve.wait_ge(n_rs, 2)
        dve.wait_ge(xr_in, 16)
        for c in range(4):
            add_normed(c, mo, C_MIXPOST, x_res, 0)
        norm_out(3, nsq, C_FFNPRE)

        def up(i, first, half):
            for j in range(2):
                t = i * 2 + j
                tt = t + FT * half
                fu = U_FFN + HALF_U * half
                ahead(fu, 4, i, 2 * j)
                ahead(fu, 4, i, 2 * j + 1)
                dve.wait_ge(evac, t + (T_FFN + HALF_T * half + 1))
                V.tensor_tensor(tmp[:, :], ru[j][:, :], ru[j][:, :], ALU.mult).then_inc(up_sq, 1)
                dve.wait_ge(up_hi, tt + 1)
                V.tensor_tensor(tile_at(u_lo, t), one(tmp[:, :]), tile_at(u_hi, t).bitcast(F32),
                                ALU.subtract).then_inc(up_lo, 1)

        def down(i, first, half):
            for j in range(2):
                t = i * 2 + j
                for s in range(4):
                    ahead(U_FFN + HALF_U * half + 2 * FT, 8, i, 4 * j + s)
                if half == 0:
                    continue
                dve.wait_ge(evac, t + (T_FFN + HALF_T + FT + 1))
                V.tensor_tensor(tile_at(ffn, t), tile_at(ffn, t), one(tmp[:, :]), ALU.add).then_inc(dn_add, 1)
                dve.wait_ge(dn_sq, t + 1)
                if first and j == 0:
                    V.tensor_copy(acc[:, :], tmp[:, :]).then_inc(dn_acc, 1)
                else:
                    dve.wait_ge(dn_acc, t)
                    V.tensor_tensor(acc[:, :], acc[:, :], tmp[:, :], ALU.add).then_inc(dn_acc, 1)

        for half in range(2):
            up(0, True, half)
            with dve.Fori(1, FT // 2) as i:
                up(i, False, half)
            down(0, True, half)
            with dve.Fori(1, KT // 2) as i:
                down(i, False, half)

        dve.wait_ge(p_his, 1)
        V.tensor_tensor(p_lo[:, :, :], p_in[:, :, :], p_hi[:, :, :].bitcast(F32), ALU.subtract).then_inc(p_los, 1)
        dve.wait_ge(n_rs, 4)
        for c in range(4):
            ahead(U_PROJ, 4, 0, c)
            add_normed(c, ffn, C_FFNPOST, x2, KT)
        norm_out(5, nsq3, C_PLE)

        def ple(i, last):
            for j in range(2):
                t = i * 2 + j
                for s in (2 * j, 2 * j + 1):
                    if not (last and s + AHEAD >= 4):
                        ahead(U_PLE, 4, i, s)
                dve.wait_ge(evac, t + (T_PLE + 1))
                V.scalar_tensor_tensor(one(gtg[:, j]), one(gtg[:, j]), 1.0, tile_at(e_out, t),
                                       ALU.add, ALU.mult).then_inc(g_t, 1)
                dve.wait_ge(g_t, t + 1)
                V.scalar_tensor_tensor(tile_at(x2, t), one(gtg[:, j]), 0.5, tile_at(x2, t),
                                       ALU.mult, ALU.add).then_inc(g_y, 1)

        ple(0, False)
        with dve.Fori(1, KT // 2 - 1) as i:
            ple(i, False)
        ple(KT // 2 - 1, True)

    @block.tensor
    def _(pe):
        M = nc.tensor

        def multiply(m, k, out, hi, lo, kt0, first, last):
            pe.wait_ge(lo_done, m * RING + (k + 1))
            for i in range(SK):
                M.matmul(out, w_hi[:, k, i], hi[:, kt0 + i], start=first and i == 0, stop=False)
                M.matmul(out, w_hi[:, k, i], lo[:, kt0 + i], start=False, stop=False)
                op = M.matmul(out, w_lo[:, k, i], hi[:, kt0 + i], start=False, stop=last and i == SK - 1)
            op.then_inc(slab_used, 1)

        def free(tile, n):
            pe.wait_ge(evac, n + (tile - 1))

        def sum_squares(sq, n, base_c, group=4):
            for c in range(4):
                pe.wait_ge(n_sq, base_c + c + 1)
                for t in range(4 * c, 4 * c + 4):
                    op = M.matmul(b_ms[:, 0:T], ones, sq[:, t], start=t == 0, stop=t == KT - 1)
            op.then_inc(n_ms, 1)

        pe.wait_ge(cst_land, 16)
        sum_squares(x_sq, 1, 0)
        pe.wait_ge(wdt_land, 16)
        pe.wait_ge(n_xn, KT)
        for t in range(KT):
            op = M.matmul(b_tv[0:HD, 0:T], wdt[:, t], hn32[:, t], start=t == 0, stop=t == KT - 1)
        op.then_inc(pe_pro, 1)
        pe.wait_ge(dve_pro, 16)
        for q, src in enumerate((dts, cum, dtw)):
            for b in range(2):
                M.transpose(b_tk[:, (2 * q + b) * HD:(2 * q + b + 1) * HD], src[:, P * b:P * b + P],
                            ident[0:HD, 0:HD])
            op = M.transpose(b_diag[0:32, q * HD:(q + 1) * HD], src[:, TP:T], ident[0:HD, 0:HD])
        op.then_inc(pe_pro, 1)
        pe.wait_ge(n_lo, 4)

        def hgrn(it, first, gemm):
            def nxt(s):
                if not gemm:
                    return
                if s % 2 == 0 and not (first and s < 4):
                    free(T_HG + s // 2, it * HG_TILES)
                multiply(*slab(U_HG, HG_SLABS, it, s), ps[s // 2 % 2][:, 0:T], h_hi, h_lo, SK * (s % 2),
                         s % 2 == 0, s % 2 == 1)

            nxt(0)
            if not first:
                pe.wait_ge(hg_w, it)
                pe.wait_ge(evac, it * HG_TILES + (T_HG - 1))
                M.transpose(b_tv[:, 0:P], hvv[:, 0:P], ident)
                M.transpose(b_tv[:, P:TP], hvv[:, P:TP], ident)
                M.transpose(b_tv[0:32, TP:TP + P], hvv[:, TP:T], ident)
                M.transpose(b_tk[:, 0:P], hkw[:, 0:P], ident)
                M.transpose(b_tk[:, P:TP], hkw[:, P:TP], ident)
                M.transpose(b_tk[0:32, TP:TP + P], hks[:, :], ident).then_inc(hg_tr, 1)
                for b in range(2):
                    c, o = P * b, LOFF[64]
                    M.matmul(b_att[0:64, c + 64:c + P], he[:, o + c:o + c + 64], he[:, o + c + 64:o + c + P],
                             start=True, stop=True)
                    o = LOFF[32]
                    for q in (0, 64):
                        M.matmul(b_att[q:q + 32, c + q + 32:c + q + 64], he[:, o + c + q:o + c + q + 32],
                                 he[:, o + c + q + 32:o + c + q + 64], start=True, stop=True)
                M.matmul(b_att[:, TP:TP + P], hkt[:, :], hqt[:, :], start=True, stop=True)
                for n, h in enumerate(DIAG):
                    for b in range(2):
                        for q in range(4):
                            c = P * b + 32 * q
                            ks = hk[:, c:c + 32] if h == 0 else he[:, LOFF[h] + c:LOFF[h] + c + 32]
                            qs = hq[:, c:c + 32] if h == 0 else he[:, LOFF[h] + c:LOFF[h] + c + 32]
                            M.matmul(b_diag[32 * q:32 * q + 32, 64 * n + 32 * b:64 * n + 32 * b + 32], ks, qs,
                                     start=True, stop=True)
                for n, h in enumerate(DIAG_S):
                    ks = hk[:, TP:T] if h == 0 else he[:, LOFF[h] + TP:LOFF[h] + T]
                    qs = hq[:, TP:T] if h == 0 else he[:, LOFF[h] + TP:LOFF[h] + T]
                    op = M.matmul(b_diag[0:32, 384 + 32 * n:416 + 32 * n], ks, qs, start=True, stop=True)
                op.then_inc(hg_attn, 1)
            nxt(1)
            nxt(2)
            if not first:
                pe.wait_ge(hg_tok, it)
                pe.wait_ge(hg_ab, it)
                pe.wait_ge(hg_s0, it * 16)
                pe.wait_ge(hg_vbd, it)
                M.matmul(b_o[:, 0:P], hvt[:, 0], hatt[:, 0], start=True, stop=True)
                M.matmul(b_o[:, P:TP], hvt[:, 1], hatt[:, 1], start=True, stop=False)
                M.matmul(b_o[:, P:TP], hvt[:, 0], htop[:, :], start=False, stop=True)
                M.matmul(b_o[:, TP:T], hvt[0:32, 2], hats[:, :], start=True, stop=True)
                for b in range(NB):
                    M.matmul(b_o[:, TP + SB * b:TP + SB * b + SB], hs0[:, b], hqs[:, SB * b:SB * b + SB],
                             start=False, stop=True, skip_group_check=True)
                M.matmul(b_att[:, 3 * P:4 * P], hkwt[:, 0], hvt[:, 0], start=True, stop=False)
                M.matmul(b_att[:, 3 * P:4 * P], hkwt[:, 1], hvt[:, 1], start=False, stop=True)
                M.matmul(b_tv[:, :], hk3[:, :], hvbd[:, 0:4].rearrange("p b n -> p (b n)"), start=True, stop=True)
                M.matmul(b_tk[:, :], hk3[:, :], hvbd[:, 4:8].rearrange("p b n -> p (b n)"), start=True,
                         stop=True).then_inc(hg_p2, 1)
            nxt(3)
            nxt(4)
            if not first:
                pe.wait_ge(hg_sq, it)
                M.matmul(b_ms[:, 0:T], ones, hsq[:, :], start=True, stop=True).then_inc(hg_ms, 1)
            for s in range(5, HG_SLABS):
                nxt(s)

        hgrn(0, True, True)
        with pe.Fori(1, HEADS) as it:
            hgrn(it, False, True)
        hgrn(HEADS, False, False)

        pe.wait_ge(hg_olo, HEADS)

        def branch_b(j):
            for s in range(GB_SLABS):
                if s % 2 == 0:
                    free(T_GB + s // 2, j * 2)
                hi, lo = (h_hi, h_lo) if s < 2 else (o_hi, o_lo)
                multiply(*slab(U_GB, GB_SLABS, j, s), ps[s // 2][:, 0:T], hi, lo, SK * (s % 2), s % 2 == 0, s % 2 == 1)

        with pe.Fori(0, KT) as j:
            branch_b(j)

        def ssd(g, first, gemm):
            r = g - 1

            def old_states(half):
                for b in range(4):
                    pe.wait_ge(sg_ht_in[b], r * 32 + 16 * (half + 1))
                pe.wait_ge(sg_cfs, g)
                for p in range(4):
                    for b in range(4):
                        seq = 4 * half + b
                        o = T + TS * p + SB * seq
                        op = M.matmul(bank[4][:, o:o + SB], ht[:, b, P * p:P * p + P], cfs[:, SB * seq:SB * seq + SB],
                                      start=True, stop=True)
                op.then_inc(sg_it, 1)

            def new_states(b):
                for i in (b, b + 1):
                    if i >= 2:
                        pe.wait_ge(sg_up, r * NB + (i - 1))
                    M.matmul(bank[2 + i % 2][:, :], bbd[:, i], xw3[:, :], start=True, stop=True).then_inc(sg_su, 1)

            for s in range(SG_SLABS):
                if not gemm and s > 9:
                    break
                if gemm:
                    t = s // 2
                    if s % 2 == 0:
                        free(T_SG + t, g * SG_TILES)
                    multiply(*slab(U_SG, SG_SLABS, g, s), ps[t % 2][:, 0:T], h_hi, h_lo, SK * (s % 2),
                             s % 2 == 0, s % 2 == 1)
                if not first:
                    if s == 0:
                        old_states(0)
                        pe.wait_ge(sg_bbd, g)
                        pe.wait_ge(sg_xwlo, g)
                        new_states(0)
                    if s == 1:
                        new_states(2)
                    if s == 5:
                        old_states(1)
                        new_states(4)
                    if s == 6:
                        new_states(6)
                    if s == 9:
                        pe.wait_ge(sg_sq, g)
                        for p in range(4):
                            op = M.matmul(bank[4][:, 0:T], ones, ysq[:, p], start=p == 0, stop=p == 3)
                        op.then_inc(sg_ms, 1)
                if not gemm:
                    continue
                if s == 6:
                    pe.wait_ge(sg_silu, g * XT + 2)
                    if not first:
                        pe.wait_ge(sg_spe, g)
                    M.transpose(bank[0][:, 0:P], bf[:, 0:P], ident)
                    M.transpose(bank[0][:, P:TP], bf[:, P:TP], ident)
                    M.transpose(bank[0][0:32, TP:TP + P], bf[:, TP:T], ident)
                    M.matmul(bank[1][:, 0:TP], bf[:, 0:P], cf[:, 0:TP], start=True, stop=True)
                    M.matmul(bank[1][:, TP:TP + P], bf[:, P:TP], cf[:, P:TP], start=True, stop=True)
                    M.matmul(bank[1][0:32, 384:416], bf[:, TP:T], cf[:, TP:T], start=True,
                             stop=True).then_inc(sg_bc, 1)
                if s == 14:
                    pe.wait_ge(sg_silu, g * XT + 6)
                    for c in range(4):
                        M.transpose(bank[2][:, P * c:P * c + P], xf[:, c, 0:P], ident)
                        M.transpose(bank[3][:, P * c:P * c + P], xf[:, c, P:TP], ident)
                        op = M.transpose(bank[4][0:32, P * c:P * c + P], xf[:, c, TP:T], ident)
                    op.then_inc(sg_xt, 1)
                if s == 17:
                    pe.wait_ge(sg_bt, g + 1)
                    for p in range(4):
                        for b in range(2):
                            op = M.matmul(bank[1][:, P * p:P * p + P], xw[:, b, P * p:P * p + P], bt[:, b],
                                          start=b == 0, stop=b == 1)
                    op.then_inc(sg_sp, 1)
                if s >= 16:
                    p = s - 16
                    if p == 0:
                        pe.wait_ge(sg_xd, g + 1)
                        pe.wait_ge(sg_m, g * 2 + 1)
                        pe.wait_ge(sg_bt, g + 1)
                    if p == 2:
                        pe.wait_ge(sg_m, g * 2 + 2)
                    if p >= 2:
                        pe.wait_ge(sg_yf, g * 4 + (p - 1))
                    y = bank[(5, 0)[p % 2]]
                    for hh in range(2):
                        j = 2 * p + hh
                        lo, at = HD * hh, HD * j
                        M.matmul(y[lo:lo + HD, 0:TP], xd[:, 0, at:at + HD], me[:, j, 0:TP], start=True, stop=True)
                        M.matmul(y[lo:lo + HD, P:TP], xd[:, 1, at:at + HD], me[:, j, TP:TP + P], start=False,
                                 stop=True, skip_group_check=True)
                        op = M.matmul(y[lo:lo + HD, TP:T], xd[0:32, 2, at:at + HD], me[0:32, j, 384:416],
                                      start=True, stop=True)
                    op.then_inc(sg_y, 1)

        ssd(0, True, True)
        with pe.Fori(1, GROUPS) as g:
            ssd(g, False, True)
        ssd(GROUPS, False, False)

        def branch_a(i, first):
            for j in range(2):
                for s in range(GA_SLABS):
                    if s in (0, 2):
                        free(T_GA + 2 * j + s // 2, i * 4)
                    at = slab(U_GA, 2 * GA_SLABS, i, GA_SLABS * j + s)
                    if s < 2:
                        multiply(*at, ps[0][:, 0:T], h_hi, h_lo, SK * s, s == 0, s == 1)
                    else:
                        if first and j == 0:
                            pe.wait_ge(y_los, 2 * (s - 1))
                        multiply(*at, ps[1][:, 0:T], y_hi, y_lo, SK * (s - 2), s == 2, s == 5)

        branch_a(0, True)
        with pe.Fori(1, KT // 2) as i:
            branch_a(i, False)

        pe.wait_ge(ga_lo, KT)
        with pe.Fori(0, KT // 2) as i:
            for j in range(2):
                free(T_OUT + j, i * 2)
                for s in range(2):
                    multiply(*slab(U_OUT, 4, i, 2 * j + s), ps[j][:, 0:T], m_hi, m_lo, SK * s, s == 0, s == 1)
        pe.wait_ge(o_acc, KT)
        M.matmul(b_ms[:, 0:T], ones, acc[:, :], start=True, stop=True).then_inc(n_ms, 1)
        sum_squares(nsq, 3, 4)
        pe.wait_ge(n_lo, 8)

        for half in range(2):
            fu, tu = U_FFN + HALF_U * half, T_FFN + HALF_T * half
            with pe.Fori(0, FT // 2) as i:
                for j in range(2):
                    free(tu + j, i * 2)
                    for s in range(2):
                        multiply(*slab(fu, 4, i, 2 * j + s), ps[j][:, 0:T], h_hi, h_lo, SK * s, s == 0, s == 1)
            pe.wait_ge(up_lo, FT * (half + 1))
            with pe.Fori(0, KT // 2) as i:
                for j in range(2):
                    free(tu + FT + j, i * 2)
                    for s in range(4):
                        multiply(*slab(fu + 2 * FT, 8, i, 4 * j + s), ps[j][:, 0:T], u_hi, u_lo, SK * s,
                                 s == 0, s == 3)

        pe.wait_ge(dn_acc, KT)
        M.matmul(b_ms[:, 0:T], ones, acc[:, :], start=True, stop=True).then_inc(n_ms, 1)
        pe.wait_ge(p_los, 1)
        for s in range(4):
            m, k = slab(U_PROJ, 4, 0, s)
            pe.wait_ge(lo_done, m * RING + k + 1)
            for j in range(4):
                free(T_PROJ + 4 * s + j, 0)
                out = ps[j % 2][:, 0:T]
                for i in range(2):
                    w = 2 * j + i
                    M.matmul(out, w_hi[:, k, w], p_hi[:, i], start=i == 0, stop=False)
                    M.matmul(out, w_hi[:, k, w], p_lo[:, i], start=False, stop=False)
                    op = M.matmul(out, w_lo[:, k, w], p_hi[:, i], start=False, stop=i == 1)
                op.then_inc(pj_tile if j < 3 else slab_used, 1)
        sum_squares(nsq3, 5, 8)
        pe.wait_ge(n_lo, 12)
        with pe.Fori(0, KT // 2) as i:
            for j in range(2):
                free(T_PLE + j, i * 2)
                for s in range(2):
                    multiply(*slab(U_PLE, 4, i, 2 * j + s), ps[j][:, 0:T], h_hi, h_lo, SK * s, s == 0, s == 1)

    @block.gpsimd
    def _(pool):
        def row(ap, i):
            if isinstance(i, int):
                return ap[i]
            v = ap[bass.ds(i, 1)]
            if len(v.shape) == 3:
                return v.rearrange("a p n -> (a p) n")
            if len(v.shape) == 4:
                return v.rearrange("a p b n -> (a p) b n")
            return v.rearrange("a p c b n -> (a p) c b n")

        pool.wait_ge(dve_pro, 17)
        pool.dma_start(cum_d, cum[:, :]).then_inc(scr_out, 16)
        pool.dma_start(ecum_d, ecum[:, :]).then_inc(scr_out, 16)
        pool.dma_start(elast_d, elast[:, :]).then_inc(scr_out, 16)
        pool.wait_ge(scr_out, 48)

        def hgrn(r, last):
            pool.wait_ge(hg_tlo, r + 1)
            mask = consts[0:96, K_BATCH:K_BATCH + NB].unsqueeze(2).to_broadcast([96, NB, P])
            v3 = hv3[:, :].bitcast(F32).unsqueeze(1).to_broadcast([96, NB, P])
            nc.gpsimd.tensor_tensor(hvbd[:, :, :], v3, mask,
                                    ALU.mult).then_inc(hg_vbd, 1)
            pool.wait_ge(hg_st, r + 1)
            if not last:
                pool.dma_start(hs0[:, :, :], row(io["s0"], r + 1)).then_inc(hg_s0, 16)
            pool.dma_start(row(io["hg_s"], r), hsn[:, :, :]).then_inc(hg_out, 16)
            pool.dma_start(row(io["hg_p"], r), hsp[:, :]).then_inc(hg_out, 16)
            pool.wait_ge(hg_out, (r + 1) * 32)

        pool.wait_ge(hg_zero, 1)
        pool.dma_start(hs0[:, :, :], io["s0"][0]).then_inc(hg_s0, 16)
        with pool.Fori(0, HEADS - 1) as r:
            hgrn(r, False)
        hgrn(HEADS - 1, True)

        with pool.Fori(0, KT) as j:
            pool.wait_ge(gb_mb, j + 1)
            pool.dma_start(row(mixb, j), bmb[:, :]).then_inc(gb_out, 16)

        def load_parameters(g):
            pool.dma_start(prm[:, :, :], row(io["convp"], g)).then_inc(sg_par_in, 16)
            pool.dma_start(cst[:, :, :, :], row(io["convs"], g)).then_inc(sg_par_in, 16)

        def rows(ap, first, n):
            return ap[first:first + n] if isinstance(first, int) else ap[bass.ds(first, n)]

        def load_cum(g):
            src = rows(cum_d, g * GH, GH).rearrange("h t -> (h t)")
            pool.dma_start(cbc[:, :, :].rearrange("p h t -> p (h t)"), src.partition_broadcast(P)).then_inc(sg_cbc_in, 16)

        def load_decays(g):
            src = rows(ecum_d, g * GH, GH).rearrange("(q a) t -> a q t", a=2)
            for a in range(2):
                pool.dma_start(ecp[HD * a:HD * a + HD], src[a].partition_broadcast(HD)).then_inc(sg_ec_in, 16)
            src = rows(elast_d, g * GH, GH).rearrange("h b -> (h b)")
            pool.dma_start(el[:, :, :].rearrange("p h b -> p (h b)"), src.partition_broadcast(P)).then_inc(sg_ec_in, 16)

        def load_state(g, seq):
            pool.dma_start(ht[:, seq % 4], row(io["ht"], g)[:, seq]).then_inc(sg_ht_in[seq % 4], 16)

        def exponents(g, q):
            for j in range(4 * q, 4 * q + 4):
                nc.gpsimd.tensor_scalar(me[:, j, 0:TP], cbc[:, j, 0:TP], tcur[:, 1, 0, j:j + 1], 0.0,
                                        ALU.subtract, ALU.min)
                nc.gpsimd.tensor_scalar(me[:, j, TP:TP + P], cbc[:, j, P:TP], tcur[:, 1, 1, j:j + 1], 0.0,
                                        ALU.subtract, ALU.min)
                op = nc.gpsimd.tensor_scalar(me[0:32, j, 384:416], cbc[0:32, j, TP:T], tcur[0:32, 1, 2, j:j + 1],
                                             0.0, ALU.subtract, ALU.min)
            op.then_inc(sg_seg, 1)

        def ssd(g, first, last):
            pool.wait_ge(sg_btlo, g + 1)
            if not first:
                pool.wait_ge(sg_su, g * NB)
            pool.wait_ge(sg_cur, g + 1)
            pool.wait_ge(sg_cbc_in, (g + 1) * 16)
            if not first:
                pool.wait_ge(sg_ms, g)
            mask = consts[0:96, K_BATCH:K_BATCH + NB].unsqueeze(2).to_broadcast([96, NB, P])
            b3 = bt3[:, :].bitcast(F32).unsqueeze(1).to_broadcast([96, NB, P])
            nc.gpsimd.tensor_tensor(bbd[:, :, :], b3, mask,
                                    ALU.mult).then_inc(sg_bbd, 1)
            exponents(g, 0)
            exponents(g, 1)
            pool.wait_ge(sg_nc, (g + 1) * XT)
            pool.dma_start(row(io["conv"], g), ncv[:, :, :]).then_inc(sg_nc_out, 16)
            if not last:
                load_parameters(g + 1)
                pool.wait_ge(sg_seg, g * 2 + 2)
                load_cum(g + 1)
            pool.wait_ge(sg_spe, g + 1)
            pool.dma_start(row(io["ssm_p"], g), ssp[:, :, :]).then_inc(sg_sp_out, 16)
            def renew(seq):
                pool.wait_ge(sg_ht_out[seq % 4], g * 32 + 16 * (seq // 4 + 1))
                if seq < 4:
                    load_state(g, seq + 4)
                elif not last:
                    load_state(g + 1, seq - 4)

            for seq in range(NB):
                pool.wait_ge(sg_up, g * NB + seq + 1)
                pool.dma_start(row(io["ssm_s"], g * 2 + seq // 4)[:, seq % 4],
                               ht[:, seq % 4]).then_inc(sg_ht_out[seq % 4], 16)
                if seq % 4:
                    renew(seq - 1)
                if seq % 4 == 3:
                    renew(seq)
            if not last:
                pool.wait_ge(sg_g, g + 1)
                load_decays(g + 1)

        pool.wait_ge(sg_raw0, 1)
        load_parameters(0)
        load_cum(0)
        for seq in range(4):
            load_state(0, seq)
        load_decays(0)
        ssd(0, True, False)
        with pool.Fori(1, GROUPS - 1) as g:
            ssd(g, False, False)
        ssd(GROUPS - 1, False, True)

        pool.wait_ge(sg_y32, GROUPS)
        pool.wait_ge(sg_nc_out, 16 * GROUPS)
        pool.wait_ge(sg_sp_out, 16 * GROUPS)
        pool.dma_start(amb[:, :], mixb[0]).then_inc(ga_in, 16)
        with pool.Fori(1, KT) as j:
            pool.wait_ge(ga_m, j)
            pool.dma_start(amb[:, :], row(mixb, j)).then_inc(ga_in, 16)

        pool.wait_ge(slab_used, U_OUT)
        pool.dma_start(x_res[:, :, :], io["x"]).then_inc(xr_in, 16)
        pool.wait_ge(slab_used, U_PROJ)
        pool.dma_start(p_in[:, :, :], io["p"]).then_inc(p_land, 16)
        with pool.Fori(0, KT) as j:
            pool.wait_ge(g_y, j + 1)
            pool.dma_start(io["y"][:, bass.ds(j, 1)], x2[:, bass.ds(j, 1)]).then_inc(y_out, 16)
        pool.wait_ge(y_out, 16 * KT)

    stack.close()


def slabs(w):
    k, n = w.shape
    v = w.reshape(k // (SK * P), SK, P, n // P, P)
    return v.transpose(3, 0, 2, 1, 4).reshape(-1, P, SK, P)


def feature_major(prompt, sample):
    v = np.concatenate([prompt.reshape(TP, -1), sample.reshape(TS, -1)]).T
    return np.ascontiguousarray(v.reshape(-1, P, T).transpose(1, 0, 2))


def columns(v):
    return v.reshape(-1, P).T


def kernel(**inputs):
    import concourse.bacc as _bacc
    from concourse.bass_utils import run_bass_kernel_spmd as _run

    a = {k: np.asarray(v) for k, v in inputs.items()}
    w_in = a["w_in"][0]
    dx, bc = 2 * D, GROUPS * P
    z, xbc = w_in[:, 0:dx], w_in[:, dx:2 * dx + 2 * bc]
    o = 2 * dx + 2 * bc
    w_dt = w_in[:, o:o + HD]
    o += HD
    q, f, v, g, ga, gb = (w_in[:, o + D * i:o + D * (i + 1)] for i in range(6))

    def tiles(w, per):
        s = slabs(w)
        return s.reshape(-1, per, P, SK, P)

    hg = np.stack([tiles(w, 2) for w in (f, q, v, g)], 1).reshape(-1, P, SK, P)
    br_b = np.concatenate([tiles(gb, 2), tiles(a["w_br_b"][0], 2)], 1).reshape(-1, P, SK, P)
    zt, xt = tiles(z, 2).reshape(GROUPS, 4, 2, P, SK, P), tiles(xbc, 2)
    xs = xt[0:32].reshape(GROUPS, 4, 2, P, SK, P)
    sg = np.concatenate([xt[32:40, None], xt[40:48, None], xs, zt], 1).reshape(-1, P, SK, P)
    br_a = np.concatenate([tiles(ga, 2), tiles(a["w_br_a"][0], 4)], 1).reshape(-1, P, SK, P)
    up, down = tiles(a["w_up"][0], 2), a["w_down"][0]
    ffn = []
    for half in range(2):
        ffn += [up[FT * half:FT * half + FT].reshape(-1, P, SK, P), slabs(down[FT * P * half:FT * P * (half + 1)])]
    proj = a["w_ple_proj"][0].reshape(2, P, 4, 4, P).transpose(2, 1, 3, 0, 4).reshape(4, P, SK, P)
    w = np.concatenate([hg, br_b, sg, br_a, slabs(a["w_out"][0])] + ffn + [proj, slabs(a["w_ple_gate"][0])])

    def conv_tiles(m):
        n = m.shape[0]
        x = m[:, 0:dx].reshape(n, GROUPS, 4, P)
        b = m[:, dx:dx + bc].reshape(n, GROUPS, 1, P)
        c = m[:, dx + bc:].reshape(n, GROUPS, 1, P)
        return np.concatenate([b, c, x], 2).transpose(1, 3, 2, 0)

    arrays = {
        "w": w,
        "wdt": w_dt.reshape(KT, P, HD).transpose(1, 0, 2),
        "x": feature_major(a["x_prompt"], a["x_sample"]),
        "p": feature_major(a["p_prompt"][0], a["p_sample"][0]),
        "consts": constants(),
        "cols": np.concatenate(
            [columns(a[n][0]) for n in ("norm_mix_pre", "norm_mix_post", "norm_ffn_pre", "norm_ffn_post",
                                        "norm_ple", "hg_norm", "ssm_norm")]
            + [columns(np.repeat(a["d_skip"][0], HD)), columns(a["hg_lb"][0]), columns(a["hg_lb"][1])], 1),
        "hv": np.stack([a["dt_bias"][0], a["a_log"][0]], 1),
        "convp": conv_tiles(np.concatenate([a["conv_w"][0], a["conv_b"]])),
        "convs": conv_tiles(a["state_conv"][0].reshape(NB * (CW - 1), -1)).reshape(GROUPS, P, XT, NB, CW - 1),
        "s0": a["state_hgrn"][0].transpose(1, 2, 0, 3),
        "ht": a["state_ssm"][0].reshape(NB, GROUPS, GH * HD, P).transpose(1, 3, 0, 2),
    }
    outs = {
        "y": (P, KT, T), "ssm_p": (GROUPS, P, 4, P), "conv": (GROUPS, P, XT, (1 + NB) * (CW - 1)),
        "hg_p": (HEADS, P, P), "ssm_s": (GROUPS * 2, P, NB // 2, GH * HD), "hg_s": (HEADS, P, NB, P),
    }
    nc = _bacc.Bacc("TRN2", target_bir_lowering=False, num_devices=1)
    io, feed = {}, {}
    for name, v in arrays.items():
        v = np.ascontiguousarray(v)
        feed[f"in_{name}"] = v
        io[name] = nc.dram_tensor(f"in_{name}", v.shape, F32, kind="ExternalInput").ap()
    for name, shape in outs.items():
        io[name] = nc.dram_tensor(f"out_{name}", shape, F32, kind="ExternalOutput").ap()
    layer_program(nc, io)
    got = _run(nc, [feed], core_ids=[0]).results[0]
    got = {n: np.asarray(got[f"out_{n}"]) for n in outs}

    y = got["y"].transpose(2, 1, 0).reshape(T, D)
    cv = got["conv"].transpose(3, 0, 2, 1)
    n = cv.shape[0]
    cv = np.concatenate([cv[:, :, 2:].reshape(n, dx), cv[:, :, 0].reshape(n, bc), cv[:, :, 1].reshape(n, bc)], 1)
    sp = got["ssm_p"].transpose(0, 2, 1, 3).reshape(1, 1, GROUPS * GH, HD, P)
    ss = got["ssm_s"].reshape(GROUPS, 2, P, NB // 2, GH * HD).transpose(1, 3, 0, 4, 2).reshape(1, NB, GROUPS * GH, HD, P)
    return (
        np.ascontiguousarray(y[0:TP].reshape(1, TP, D)),
        np.ascontiguousarray(y[TP:].reshape(NB, SB, D)),
        np.ascontiguousarray(sp),
        np.ascontiguousarray(cv[0:CW - 1].reshape(1, 1, CW - 1, -1)),
        np.ascontiguousarray(got["hg_p"].reshape(1, 1, HEADS, P, P)),
        np.ascontiguousarray(ss),
        np.ascontiguousarray(cv[CW - 1:].reshape(1, NB, CW - 1, -1)),
        np.ascontiguousarray(got["hg_s"].transpose(2, 0, 1, 3).reshape(1, NB, HEADS, P, P)),
    )
```

```python
from contextlib import ExitStack

import numpy as np

import concourse.bass as bass
from concourse import mybir

F32 = mybir.dt.float32
F32R = mybir.dt.float32r
ALU = mybir.AluOpType
ACT = mybir.ActivationFunctionType
AX = mybir.AxisListType

P = 128
D = 2048
KT = D // P
TP = 256
NB, SB = 8, 4
TS = NB * SB
T = TP + TS
GROUPS = 8
GH = 8
HD = 64
HEADS = 16
PLE = 256
FFN = 8192
FT = FFN // P // 2
CW = 4
XT = 6
EPS = 1e-6

RING = 4
AHEAD = 3
SK = 8

HG_SLABS, HG_TILES = 8, 4
GB_SLABS = 4
SG_SLABS, SG_TILES = 20, 10
GA_SLABS = 6
U_HG, T_HG = 0, 0
U_GB, T_GB = U_HG + HEADS * HG_SLABS, T_HG + HEADS * HG_TILES
U_SG, T_SG = U_GB + KT * GB_SLABS, T_GB + KT * 2
U_GA, T_GA = U_SG + GROUPS * SG_SLABS, T_SG + GROUPS * SG_TILES
U_OUT, T_OUT = U_GA + KT * GA_SLABS, T_GA + KT * 2
U_FFN, T_FFN = U_OUT + KT * 2, T_OUT + KT
HALF_U, HALF_T = FT * 2 + KT * 4, FT + KT
U_PROJ, T_PROJ = U_FFN + 2 * HALF_U, T_FFN + 2 * HALF_T
U_PLE, T_PLE = U_PROJ + 4, T_PROJ + KT
SLABS = U_PLE + KT * 2

LEVELS = (64, 32, 16, 8, 4, 2, 1)
LOFF = {}
_o = 0
for _h in LEVELS:
    LOFF[_h] = _o
    _o += T if _h <= 2 else TP
LAST_OFF = _o
E_COLS = _o + TS
DIAG = (16, 8, 4, 2, 1, 0)
DIAG_S = (2, 1, 0)

C_MIXPRE, C_MIXPOST, C_FFNPRE, C_FFNPOST, C_PLE = (KT * i for i in range(5))
C_HGN = 5 * KT
C_SSMN = C_HGN + 1
C_DSKIP = C_SSMN + 32
C_LB = C_DSKIP + 32
N_COLS = C_LB + 2 * HEADS
K_IDENT, K_ONES = 0, P
K_RESET = 2 * P
K_DIAG = K_RESET + T
K_DIAGS = K_DIAG + len(DIAG) * 64
K_CB = K_DIAGS + len(DIAG_S) * TS
K_BATCH = K_CB + 416
K_EPS = K_BATCH + NB
N_CONST = K_EPS + 1

PW = CW + 1
RAWC = (CW - 1) + TP + NB * (CW - 1 + SB)
CVC = RAWC - (CW - 1)
SOFF = CW - 1 + TP


def constants():
    c = np.zeros((P, N_CONST), np.float32)
    c[:, K_IDENT:K_IDENT + P] = np.eye(P)
    c[:, K_ONES:K_ONES + P] = 1.0
    c[:, K_RESET:K_RESET + T] = 1.0
    c[:, K_RESET] = 0.0
    c[:, K_RESET + TP:K_RESET + T:SB] = 0.0
    s = np.arange(32)[:, None]
    t = np.arange(32)[None, :]

    def pairs(h):
        if h == 0:
            return s == t
        return (s // (2 * h) == t // (2 * h)) & (s % (2 * h) < h) & (t % (2 * h) >= h)
    for n, h in enumerate(DIAG):
        for q in range(4):
            for b in range(2):
                at = K_DIAG + n * 64 + b * 32
                c[32 * q:32 * q + 32, at:at + 32] = pairs(h)
    for n, h in enumerate(DIAG_S):
        c[0:32, K_DIAGS + n * TS:K_DIAGS + (n + 1) * TS] = pairs(h)
    r = np.arange(P)[:, None]
    c[:, K_CB:K_CB + TP] = r <= np.arange(TP)[None, :]
    c[:, K_CB + TP:K_CB + TP + P] = r <= np.arange(P)[None, :]
    c[0:32, K_CB + 384:K_CB + 416] = (s // SB == t // SB) & (s <= t)
    for q in range(3):
        c[32 * q:32 * q + 32, K_BATCH:K_BATCH + NB] = s // SB == np.arange(NB)[None, :]
    c[:, K_EPS] = EPS
    return c


def layer_program(nc, io):
    stack = ExitStack()

    def sem(name):
        return stack.enter_context(nc.semaphore(name))

    base = (nc.sbuf_base + 31) // 32 * 32
    top = nc.sbuf_usable_end // 32 * 32
    place = [base]

    def sb(name, shape, dt=F32):
        t = nc.alloc_sbuf_tensor_at(name, shape, dt, offset=place[0])
        place[0] += (int(np.prod(shape[1:])) * 4 + 31) // 32 * 32
        assert place[0] <= top, (name, place[0] - top)
        return t

    raw = sb("raw", [P, RING, SK, P])
    w_hi = sb("w_hi", [P, RING, SK, P], F32R)
    w_lo = sb("w_lo", [P, RING, SK, P], F32R)
    h_hi = sb("h_hi", [P, KT, T], F32R)
    h_lo = sb("h_lo", [P, KT, T], F32R)
    consts = sb("consts", [P, N_CONST])
    cols = sb("cols", [P, N_COLS])
    lbc = sb("lbc", [P, HEADS, 3])
    tok = sb("tok", [P, 3, 3, HD])
    ident = consts[:, K_IDENT:K_IDENT + P]
    ones = consts[:, K_ONES:K_ONES + P]
    eps = consts[:, K_EPS:K_EPS + 1]
    phase = place[0]

    x_in = sb("x_in", [P, KT, T])
    x_sq = sb("x_sq", [P, KT, T])
    x_rs = sb("x_rs", [P, T])
    x_sum = sb("x_sum", [P, T])
    place[0] = dt_at = top - 4 * (KT * HD + KT * T + 6 * T + TS + NB + 4 * HEADS) - 64
    wdt = sb("wdt", [P, KT, HD])
    hn32 = sb("hn32", [P, KT, T])
    hv = sb("hv", [HD, 2])
    dtz = sb("dtz", [HD, T])
    dta = sb("dta", [HD, T])
    dte = sb("dte", [HD, T])
    dts = sb("dts", [HD, T])
    cum = sb("cum", [HD, T])
    dtw = sb("dtw", [HD, T])
    ecum = sb("ecum", [HD, TS])
    elast = sb("elast", [HD, NB])
    an = sb("an", [HD, 1])
    lbm = sb("lbm", [P, 4, HEADS])

    place[0] = phase
    o_hi = sb("o_hi", [P, HEADS, T], F32R)
    o_lo = sb("o_lo", [P, HEADS, T], F32R)
    after_o = place[0]
    hth = sb("hth", [P, T])
    hq = sb("hq", [P, T])
    hvv = sb("hvv", [P, T])
    hg = sb("hg", [P, T])
    htg = sb("htg", [P, T])
    hf = sb("hf", [P, T])
    hk = sb("hk", [P, T])
    hlf = sb("hlf", [P, T])
    hcum = sb("hcum", [P, T])
    hcur = sb("hcur", [P, 3])
    hnc = sb("hnc", [P, 1])
    he = sb("he", [P, E_COLS])
    hkw = sb("hkw", [P, TP])
    hkt = sb("hkt", [P, P])
    hqt = sb("hqt", [P, P])
    hec = sb("hec", [P, TS])
    hqs = sb("hqs", [P, TS])
    hks = sb("hks", [P, TS])
    hel = sb("hel", [P, NB])
    hdm = sb("hdm", [P, len(DIAG) * 64])
    hab = sb("hab", [P, 2, 32])
    hatt = sb("hatt", [P, 2, P])
    htop = sb("htop", [P, P])
    hdms = sb("hdms", [32, len(DIAG_S) * TS])
    hats = sb("hats", [32, TS])
    hvt = sb("hvt", [P, 3, P])
    hkwt = sb("hkwt", [P, 3, P])
    hv3 = sb("hv3", [96, P], F32R)
    hk3 = sb("hk3", [96, P], F32R)
    hvbd = sb("hvbd", [96, NB, P], F32R)
    hs0 = sb("hs0", [P, NB, P])
    hsn = sb("hsn", [P, NB, P])
    hsp = sb("hsp", [P, P])
    hsq = sb("hsq", [P, T])
    hrs = sb("hrs", [P, T])
    hsg = sb("hsg", [P, T])
    hon = sb("hon", [P, T])
    hso = sb("hso", [P, T])
    assert place[0] <= dt_at, place[0] - dt_at

    place[0] = after_o
    btg = sb("btg", [P, T])
    byb = sb("byb", [P, T])
    bmb = sb("bmb", [P, T])

    y_bytes = 2 * KT * T * 4
    y_at = top - y_bytes
    y32 = nc.alloc_sbuf_tensor_at("y32", [P, 2 * KT, T], F32, offset=y_at)
    m_hi = nc.alloc_sbuf_tensor_at("m_hi", [P, KT, T], F32R, offset=y_at)
    m_lo = nc.alloc_sbuf_tensor_at("m_lo", [P, KT, T], F32R, offset=y_at + y_bytes // 2)
    x2 = nc.alloc_sbuf_tensor_at("x2", [P, KT, T], F32, offset=y_at)
    ffn = nc.alloc_sbuf_tensor_at("ffn", [P, KT, T], F32, offset=y_at + y_bytes // 2)
    place[0] = phase
    craw = sb("craw", [P, 2, RAWC])
    ccv = sb("ccv", [P, RAWC])
    cth = sb("cth", [P, T])
    xf = sb("xf", [P, 4, T])
    bf = sb("bf", [P, T])
    cf = sb("cf", [P, T])
    cbm = sb("cbm", [P, 416])
    cbc = sb("cbc", [P, GH, T])
    assert place[0] >= phase + KT * T * 4
    me = sb("me", [P, GH, 416])
    xd = sb("xd", [P, 3, GH * HD])
    xw = sb("xw", [P, 3, GH * HD])
    bt = sb("bt", [P, 3, P])
    bt3 = sb("bt3", [96, P], F32R)
    bbd = sb("bbd", [96, NB, P], F32R)
    xw3 = sb("xw3", [96, GH * HD], F32R)
    sz = sb("sz", [P, 4, T])
    yf = sb("yf", [P, 4, T])
    yrs = sb("yrs", [P, T])
    ecp = sb("ecp", [P, 4, TS])
    el = sb("el", [P, GH, NB])
    ssp = sb("ssp", [P, 4, P])
    ht = sb("ht", [P, 4, GH * HD])
    prm = sb("prm", [P, XT, PW])
    prh = sb("prh", [P, XT, PW])
    cst = sb("cst", [P, XT, NB, CW - 1])
    ncv = sb("ncv", [P, XT, (1 + NB) * (CW - 1)])
    cfs = sb("cfs", [P, TS])
    tcur = sb("tcur", [P, 3, 3, GH])
    ncur = sb("ncur", [P, 4])
    dcur = sb("dcur", [P, 4])
    yti = sb("yti", [P, 4, TS])
    assert place[0] <= y_at, place[0] - y_at
    cv_samples = ccv[:, SOFF:RAWC].rearrange("p (b s) -> p b s", b=NB)[:, :, 0:SB]
    ysq = me[:, 0:3, :].rearrange("p h n -> p (h n)")[:, 0:4 * T].rearrange("p (c n) -> p c n", c=4)

    place[0] = phase
    y_hi = sb("y_hi", [P, 2 * KT, T], F32R)
    y_lo = sb("y_lo", [P, 2 * KT, T], F32R)
    after_y = place[0]
    atg = sb("atg", [P, T])
    aya = sb("aya", [P, T])
    amb = sb("amb", [P, T])
    assert place[0] <= y_at, place[0] - y_at

    place[0] = phase
    x_res = sb("x_res", [P, KT, T])
    mo = sb("mo", [P, KT, T])
    nsq = sb("nsq", [P, KT, T])
    assert place[0] <= after_y
    u_hi = nc.alloc_sbuf_tensor_at("u_hi", [P, FT, T], F32R, offset=phase)
    u_lo = nc.alloc_sbuf_tensor_at("u_lo", [P, FT, T], F32R, offset=phase + y_bytes)
    place[0] = phase
    e_out = sb("e_out", [P, KT, T])
    p_in = sb("p_in", [P, 2, T])
    p_hi = sb("p_hi", [P, 2, T], F32R)
    p_lo = sb("p_lo", [P, 2, T], F32R)
    nsq3 = sb("nsq3", [P, KT, T])
    gtg = sb("gtg", [P, 2, T])
    place[0] = after_y
    acc = sb("acc", [P, T])
    nrs = sb("nrs", [P, T])
    tmp = sb("tmp", [P, T])
    assert place[0] <= y_at, place[0] - y_at
    ru1 = sb("ru1", [P, T])
    assert place[0] <= y_at, place[0] - y_at
    ru = [acc, ru1]

    ps = [stack.enter_context(nc.psum_tensor(f"acc{i}", [P, 512], F32)) for i in range(2)]
    bank = [stack.enter_context(nc.psum_tensor(f"bank{i}", [P, 512], F32)) for i in range(6)]
    b_tv, b_tk, b_diag, b_att, b_o, b_ms = bank

    mixb = nc.dram_tensor("mixb", (KT, P, T), F32, kind="Internal").ap()
    cum_d = nc.dram_tensor("cum_d", (HD, T), F32, kind="Internal").ap()
    ecum_d = nc.dram_tensor("ecum_d", (HD, TS), F32, kind="Internal").ap()
    elast_d = nc.dram_tensor("elast_d", (HD, NB), F32, kind="Internal").ap()

    raw_in = [sem(f"raw_in{k}") for k in range(RING)]
    hi_done = sem("hi_done")
    lo_done = sem("lo_done")
    slab_used = sem("slab_used")
    evac = sem("evac")
    x_land = [sem(f"x_land{i}") for i in range(4)]
    cst_land = sem("cst_land")
    cols_land = sem("cols_land")
    wdt_land = sem("wdt_land")
    act_pro = sem("act_pro")
    dve_pro = sem("dve_pro")
    pe_pro = sem("pe_pro")
    dt_u, dt_l = sem("dt_u"), sem("dt_ln_u")
    n_add = sem("norm_add")
    scr_out = sem("scr_out")
    n_sq, n_ms, n_ln, n_rs, n_xn, n_hi, n_lo = (
        sem(f"norm_{s}") for s in ("sq", "ms", "ln", "rs", "xn", "hi", "lo"))

    hg_fk, hg_lf, hg_cum, hg_arg, hg_exp, hg_w = (
        sem(f"hg_{s}") for s in ("fk", "lf", "cum", "arg", "exp", "w"))
    hg_cur = sem("hg_cur")
    hg_tr, hg_attn, hg_tok, hg_tlo, hg_dm, hg_red, hg_ab, hg_vbd, hg_p2 = (
        sem(f"hg_{s}") for s in ("tr", "attn", "tok", "tlo", "dm", "red", "ab", "vbd", "p2"))
    hg_sq, hg_ms, hg_ln, hg_rs, hg_on, hg_so, hg_ohi, hg_olo, hg_st = (
        sem(f"hg_{s}") for s in ("sq", "ms", "ln", "rs", "on", "so", "ohi", "olo", "st"))
    hg_zero = sem("hg_zero")
    hg_s0 = sem("hg_s0_in")
    hg_out = sem("hg_state_out")

    gb_mb, gb_out = sem("gb_mb"), sem("gb_out")

    sg_raw0, sg_prh, sg_conv, sg_th, sg_silu, sg_nc, sg_cur = (
        sem(f"sg_{s}") for s in ("raw0", "prh", "conv", "th", "silu", "nc", "cur"))
    sg_bc, sg_bt, sg_bbd, sg_cbm, sg_seg, sg_exp, sg_m, sg_cfs = (
        sem(f"sg_{s}") for s in ("bc", "bt", "bbd", "cbm", "seg", "exp", "m", "cfs"))
    sg_xt, sg_xd, sg_y, sg_yf, sg_sp, sg_spe, sg_sz, sg_it, sg_su, sg_upa, sg_up = (
        sem(f"sg_{s}") for s in ("xt", "xd", "y", "yf", "sp", "spe", "sz", "it", "su", "upa", "up"))
    sg_cv, sg_ncur = sem("sg_cv"), sem("sg_ncur")
    sg_segp, sg_xw, sg_btlo, sg_xwhi, sg_xwlo = sem("sg_segp"), sem("sg_xw"), sem("sg_btlo"), sem("sg_xwhi"), sem("sg_xwlo")
    sg_yi, sg_g, sg_sq, sg_ms, sg_ln, sg_rs, sg_y32 = (
        sem(f"sg_{s}") for s in ("yi", "g", "sq", "ms", "ln", "rs", "y32"))
    sg_par_in, sg_cbc_in, sg_nc_out, sg_sp_out, sg_ec_in = (
        sem(f"sg_{s}") for s in ("par_in", "cbc_in", "nc_out", "sp_out", "ec_in"))
    sg_ht_in = [sem(f"sg_ht_in{i}") for i in range(4)]
    sg_ht_out = [sem(f"sg_ht_out{i}") for i in range(4)]

    y_his, y_los = sem("y_hi_done"), sem("y_lo_done")
    ga_in, ga_t, ga_m, ga_hi, ga_lo = (sem(f"ga_{s}") for s in ("in", "t", "m", "hi", "lo"))
    o_acc, o_w = sem("out_acc"), sem("out_weighted")
    xr_in = sem("x_res_in")
    x2_a, x2_b = sem("x2_scaled"), sem("x2_done")
    x2_pa, x2_pb = sem("x2_pool_scaled"), sem("x2_pool_done")
    up_n, up_sq, up_hi, up_lo = sem("up_n"), sem("up_sq"), sem("up_hi"), sem("up_lo")
    dn_add, dn_sq, dn_acc, dn_w = sem("dn_add"), sem("dn_sq"), sem("dn_acc"), sem("dn_weighted")
    pj_tile = sem("pj_tile")
    p_land, p_his, p_los = sem("p_land"), sem("p_hi_done"), sem("p_lo_done")
    g_s, g_t, g_y, y_out = sem("g_s"), sem("g_t"), sem("g_y"), sem("y_out")

    XV = 3

    def four(ap):
        return one(ap).to_broadcast([P, 4, T])

    def exponents(engine, me, cbc, tcur, q):
        for j in range(4 * q, 4 * q + 4):
            engine.tensor_scalar(me[:, j, 0:TP], cbc[:, j, 0:TP], tcur[:, 1, 0, j:j + 1], 0.0,
                                 ALU.subtract, ALU.min)
            engine.tensor_scalar(me[:, j, TP:TP + P], cbc[:, j, P:TP], tcur[:, 1, 1, j:j + 1], 0.0,
                                 ALU.subtract, ALU.min)
            op = engine.tensor_scalar(me[0:32, j, 384:416], cbc[0:32, j, TP:T], tcur[0:32, 1, 2, j:j + 1],
                                      0.0, ALU.subtract, ALU.min)
        return op

    def x2_ready(engine, norm, c):
        if c < XV:
            engine.wait_ge(x2_b, XV * norm + c + 1)
        else:
            engine.wait_ge(x2_pb, norm + 1)

    def one(ap):
        return ap.rearrange("p (a n) -> p a n", a=1)

    def tile_at(t, i):
        return t[:, i:i + 1] if isinstance(i, int) else t[:, bass.ds(i, 1)]

    def blocks(ap, n):
        return ap.rearrange("p (b n) -> p b n", b=n)

    def slab(first, per, it, s):
        return first // RING + it * (per // RING) + s // RING, s % RING

    block = stack.enter_context(nc.Block())

    @block.sync
    def _(sp):
        def load_slab(m, k):
            src = io["w"][bass.ds(m * RING + k, 1)].rearrange("a p s n -> p (a s) n") \
                if not isinstance(m, int) else io["w"][m * RING + k]
            sp.dma_start(raw[:, k], src).then_inc(raw_in[k], 16)

        for c in range(4):
            sp.dma_start(x_in[:, 4 * c:4 * c + 4], io["x"][:, 4 * c:4 * c + 4]).then_inc(x_land[c], 16)
        sp.dma_start(consts[:, :], io["consts"]).then_inc(cst_land, 16)
        sp.dma_start(cols[:, :], io["cols"]).then_inc(cols_land, 16)
        sp.dma_start(hv[:, :], io["hv"]).then_inc(cols_land, 16)
        for k in range(RING):
            load_slab(0, k)
        sp.dma_start(wdt[:, :, :], io["wdt"]).then_inc(wdt_land, 16)
        with sp.Fori(1, SLABS // RING) as m:
            for k in range(RING):
                sp.wait_ge(lo_done, m * RING + (k + 1 - RING))
                load_slab(m, k)

    @block.scalar
    def _(act):
        def split_hi(m, k):
            act.wait_ge(raw_in[k], (m + 1) * 16)
            if not (isinstance(m, int) and m == 0):
                act.wait_ge(slab_used, m * RING + (k + 1 - RING))
            nc.scalar.activation(w_hi[:, k], raw[:, k], ACT.Copy).then_inc(hi_done, 1)

        def ahead(first, per, it, s):
            split_hi(*slab(first, per, it, s + AHEAD))

        def tile_done(first, per, it, s):
            m, k = slab(first, per, it, s)
            act.wait_ge(slab_used, m * RING + (k + 1))

        for c in range(4):
            act.wait_ge(x_land[c], 16)
            nc.scalar.activation(x_sq[:, 4 * c:4 * c + 4], x_in[:, 4 * c:4 * c + 4],
                                 ACT.Square).then_inc(n_sq, 1)
        act.wait_ge(cst_land, 16)
        act.wait_ge(n_ms, 1)
        nc.scalar.activation(x_rs[:, :], b_ms[:, 0:T], ACT.Ln, bias=eps, scale=1.0 / D).then_inc(n_ln, 1)
        act.wait_ge(n_ln, 1)
        nc.scalar.activation(x_rs[:, :], x_rs[:, :], ACT.Exp, scale=-0.5).then_inc(n_rs, 1)
        split_hi(0, 0)
        for c in range(4):
            act.wait_ge(n_xn, 4 * c + 4)
            nc.scalar.activation(h_hi[:, 4 * c:4 * c + 4], hn32[:, 4 * c:4 * c + 4],
                                 ACT.Copy).then_inc(n_hi, 1)
            if c in (1, 2):
                split_hi(0, c)
        act.wait_ge(cols_land, 32)
        nc.scalar.activation(an[:, :], hv[:, 1:2], ACT.Exp).then_inc(act_pro, 1)
        act.wait_ge(dve_pro, 2)
        nc.scalar.activation(lbm[:, 1:3], lbm[:, 1:3], ACT.Exp).then_inc(act_pro, 1)

        def dt_softplus():
            act.wait_ge(pe_pro, 1)
            nc.scalar.activation(dtz[:, :], b_tv[0:HD, 0:T], ACT.Identity,
                                 bias=hv[:, 0:1]).then_inc(act_pro, 1)
            act.wait_ge(dve_pro, 9)
            nc.scalar.activation(dte[:, :], dta[:, :], ACT.Exp, scale=-1.0).then_inc(act_pro, 1)
            act.wait_ge(dt_u, 1)
            nc.scalar.activation(dts[:, :], dta[:, :], ACT.Ln).then_inc(dt_l, 1)
            act.wait_ge(dt_l, 1)
            nc.scalar.activation(cum[:, :], dts[:, :], ACT.Exp, scale=-1.0).then_inc(act_pro, 1)

        def dt_decays():
            act.wait_ge(dve_pro, 15)
            nc.scalar.activation(ecum[:, :], cum[:, TP:T], ACT.Exp).then_inc(act_pro, 1)
            nc.scalar.activation(dtw[:, :], dtw[:, :], ACT.Exp).then_inc(act_pro, 1)

        def dt_token_major():
            act.wait_ge(pe_pro, 2)
            src = b_o[:, 0:384].rearrange("p (q b h) -> p q b h", q=3, b=2)
            nc.scalar.activation(tok[:, :, 0:2, :], src, ACT.Copy).then_inc(act_pro, 1)
            src = b_ms[0:32, 0:192].rearrange("p (q h) -> p q h", q=3)
            nc.scalar.activation(tok[0:32, :, 2, :], src, ACT.Copy).then_inc(act_pro, 1)

        def hgrn(it, first, gemm):
            r = it - 1

            def nxt(s):
                if gemm:
                    ahead(U_HG, HG_SLABS, it, s)

            nxt(0)
            nxt(1)
            if not first:
                act.wait_ge(hg_tr, it)
                nc.scalar.activation(hvt[:, 0:2], b_tv[:, 0:256].rearrange("p (b n) -> p b n", b=2), ACT.Copy)
                nc.scalar.activation(hvt[0:32, 2], b_tv[0:32, 256:384], ACT.Copy)
                nc.scalar.activation(hkwt[:, 0:2], b_tk[:, 0:256].rearrange("p (b n) -> p b n", b=2), ACT.Copy)
                nc.scalar.activation(hkwt[0:32, 2], b_tk[0:32, 256:384], ACT.Copy)
                for dst, src in ((hv3[0:32], b_tv), (hv3[64:96], b_tv), (hk3[0:32], b_tk), (hk3[32:64], b_tk)):
                    op = nc.scalar.activation(dst, src[0:32, 256:384], ACT.Copy)
                op.then_inc(hg_tok, 1)
            if gemm:
                tile_done(U_HG, HG_SLABS, it, 1)
                nc.scalar.activation(hth[:, :], ps[0][:, 0:T], ACT.Tanh, scale=0.5).then_inc(evac, 1)
                nxt(2)
                act.wait_ge(hg_fk, it + 1)
                nc.scalar.activation(hlf[:, :], hf[:, :], ACT.Ln).then_inc(hg_lf, 1)
            if first:
                dt_softplus()
                dt_decays()
            nxt(3)
            if not first:
                act.wait_ge(hg_p2, it)
                nc.scalar.activation(hsq[:, :], b_o[:, 0:T], ACT.Square).then_inc(hg_sq, 1)
            if gemm:
                tile_done(U_HG, HG_SLABS, it, 3)
                nc.scalar.activation(hq[:, :], ps[1][:, 0:T], ACT.Copy).then_inc(evac, 1)
                nxt(4)
                act.wait_ge(hg_arg, it + 1)
                nc.scalar.activation(he[:, :], he[:, :], ACT.Exp)
                nc.scalar.activation(hkw[:, :], hcum[:, 0:TP], ACT.Exp, bias=hcum[:, TP - 1:TP], scale=-1.0)
                nc.scalar.activation(hkt[:, :], hcum[:, 0:P], ACT.Exp, bias=hcum[:, P - 1:P], scale=-1.0)
                nc.scalar.activation(hqt[:, :], hcum[:, P:TP], ACT.Exp, bias=hnc[:, 0:1])
                nc.scalar.activation(hec[:, :], hcum[:, TP:T], ACT.Exp).then_inc(hg_exp, 1)
            nxt(5)
            if not first:
                act.wait_ge(hg_ms, it)
                nc.scalar.activation(hrs[:, :], b_ms[:, 0:T], ACT.Ln, bias=eps, scale=1.0 / P).then_inc(hg_ln, 1)
                act.wait_ge(hg_ln, it)
                nc.scalar.activation(hrs[:, :], hrs[:, :], ACT.Exp, scale=-0.5).then_inc(hg_rs, 1)
            if gemm:
                tile_done(U_HG, HG_SLABS, it, 5)
                nc.scalar.activation(hvv[:, :], ps[0][:, 0:T], ACT.Copy).then_inc(evac, 1)
            if not first:
                act.wait_ge(hg_so, it)
            nxt(6)
            if not first:
                nc.scalar.activation(tile_at(o_hi, r), one(hso[:, :]), ACT.Copy).then_inc(hg_ohi, 1)
            nxt(7)
            if gemm:
                tile_done(U_HG, HG_SLABS, it, 7)
                nc.scalar.activation(htg[:, :], ps[1][:, 0:T], ACT.Tanh, scale=0.5)
                nc.scalar.activation(hg[:, :], ps[1][:, 0:T], ACT.Copy).then_inc(evac, 1)
            if first:
                dt_token_major()

        hgrn(0, True, True)
        with act.Fori(1, HEADS) as it:
            hgrn(it, False, True)
        hgrn(HEADS, False, False)

        def branch_b(j, first):
            ahead(U_GB, GB_SLABS, j, 0)
            ahead(U_GB, GB_SLABS, j, 1)
            tile_done(U_GB, GB_SLABS, j, 1)
            if not first:
                act.wait_ge(gb_mb, j)
            nc.scalar.activation(btg[:, :], ps[0][:, 0:T], ACT.Tanh, scale=0.5).then_inc(evac, 1)
            ahead(U_GB, GB_SLABS, j, 2)
            ahead(U_GB, GB_SLABS, j, 3)
            tile_done(U_GB, GB_SLABS, j, 3)
            nc.scalar.activation(byb[:, :], ps[1][:, 0:T], ACT.Copy).then_inc(evac, 1)

        branch_b(0, True)
        with act.Fori(1, KT) as j:
            branch_b(j, False)

        def ssd(g, first, gemm):
            def nxt(s):
                if gemm:
                    ahead(U_SG, SG_SLABS, g, s)

            def conv_in(c):
                tile_done(U_SG, SG_SLABS, g, 2 * c + 1)
                if c >= 2 or not first:
                    act.wait_ge(sg_nc, g * XT + (c - 1))
                dst = craw[:, c % 2]
                nc.scalar.activation(dst[:, CW - 1:SOFF], ps[c % 2][:, 0:TP], ACT.Copy)
                seqs = dst[:, SOFF:RAWC].rearrange("p (b s) -> p b s", b=NB)
                nc.scalar.activation(seqs[:, :, CW - 1:], ps[c % 2][:, TP:T].rearrange("p (b s) -> p b s", b=NB),
                                     ACT.Copy).then_inc(evac, 1)

            def conv_tanh(c):
                act.wait_ge(sg_conv, g * XT + c + 1)
                nc.scalar.activation(cth[:, 0:TP], ccv[:, 0:TP], ACT.Tanh)
                nc.scalar.activation(cth[:, TP:T].rearrange("p (b s) -> p b s", b=NB), cv_samples,
                                     ACT.Tanh).then_inc(sg_th, 1)

            def z_in(c):
                tile_done(U_SG, SG_SLABS, g, 13 + 2 * c)
                act.wait_ge(sg_silu, (g + 1) * XT) if c == 0 else act.wait_ge(sg_sz, g * 4 + c)
                nc.scalar.activation(cth[:, :], ps[c % 2][:, 0:T], ACT.Tanh, scale=0.5)
                nc.scalar.activation(sz[:, c], ps[c % 2][:, 0:T], ACT.Copy, scale=0.5).then_inc(evac, 1)

            for s in range(SG_SLABS):
                if not gemm and s > 10:
                    break
                nxt(s)
                if not first and s == 8:
                    act.wait_ge(sg_g, g)
                    nc.scalar.activation(ysq, yf[:, :, :], ACT.Square).then_inc(sg_sq, 1)
                if not first and s == 10:
                    act.wait_ge(sg_ms, g)
                    nc.scalar.activation(yrs[:, :], b_o[:, 0:T], ACT.Ln, bias=eps, scale=1.0 / 512).then_inc(sg_ln, 1)
                    act.wait_ge(sg_ln, g)
                    nc.scalar.activation(yrs[:, :], yrs[:, :], ACT.Exp, scale=-0.5).then_inc(sg_rs, 1)
                if not gemm:
                    continue
                if s in (12, 14):
                    q = (s - 12) // 2
                    act.wait_ge((sg_seg, sg_segp)[q], g + 1)
                    nc.scalar.activation(me[:, 4 * q:4 * q + 4, 0:384], me[:, 4 * q:4 * q + 4, 0:384], ACT.Exp)
                    nc.scalar.activation(me[0:32, 4 * q:4 * q + 4, 384:416], me[0:32, 4 * q:4 * q + 4, 384:416],
                                         ACT.Exp).then_inc(sg_exp, 1)
                if s % 2 == 0 and 2 <= s <= 12:
                    conv_tanh(s // 2 - 1)
                if s == 7:
                    act.wait_ge(sg_bc, g + 1)
                    nc.scalar.activation(bt[:, 0:2], bank[0][:, 0:256].rearrange("p (b n) -> p b n", b=2), ACT.Copy)
                    for dst in (bt[0:32, 2], bt3[0:32], bt3[32:64]):
                        op = nc.scalar.activation(dst, bank[0][0:32, 256:384], ACT.Copy)
                    op.then_inc(sg_bt, 1)
                if s == 17:
                    act.wait_ge(sg_xw, g + 1)
                    nc.scalar.activation(xw3[0:32], xw[0:32, 2], ACT.Copy)
                    nc.scalar.activation(xw3[64:96], xw[0:32, 2], ACT.Copy).then_inc(sg_xwhi, 1)
                if s == 18:
                    act.wait_ge(sg_sp, g + 1)
                    if not first:
                        act.wait_ge(sg_sp_out, g * 16)
                    nc.scalar.activation(ssp[:, :, :], bank[1][:, :].rearrange("p (b n) -> p b n", b=4),
                                         ACT.Copy).then_inc(sg_spe, 1)
                if s % 2 == 1 and s < 12:
                    conv_in(s // 2)
                if s % 2 == 1 and s > 12:
                    z_in((s - 13) // 2)

        act.wait_ge(sg_raw0, 1)
        ssd(0, True, True)
        with act.Fori(1, GROUPS) as g:
            ssd(g, False, True)
        def y_hi_chunk(c):
            nc.scalar.activation(y_hi[:, 4 * c:4 * c + 4], y32[:, 4 * c:4 * c + 4], ACT.Copy).then_inc(y_his, 1)

        act.wait_ge(sg_yf, 4 * GROUPS)
        act.wait_ge(sg_sz, 4 * GROUPS)
        act.wait_ge(sg_y32, GROUPS // 2)
        for c in range(4):
            y_hi_chunk(c)
        ssd(GROUPS, False, False)

        act.wait_ge(sg_y32, GROUPS)
        for c in range(4, 8):
            y_hi_chunk(c)
            if c < 6:
                ahead(U_GA, 2 * GA_SLABS, 0, c - 4)
        for i in range(4):
            act.wait_ge(sg_ht_out[i], 32 * GROUPS)

        def branch_a(i, first):
            for j in range(2):
                t = 2 * i + j
                s0 = GA_SLABS * j
                if not (first and j == 0):
                    ahead(U_GA, 2 * GA_SLABS, i, s0)
                    ahead(U_GA, 2 * GA_SLABS, i, s0 + 1)
                tile_done(U_GA, 2 * GA_SLABS, i, s0 + 1)
                if not (first and j == 0):
                    act.wait_ge(ga_lo, t)
                nc.scalar.activation(atg[:, :], ps[0][:, 0:T], ACT.Tanh, scale=0.5).then_inc(evac, 1)
                for s in range(2, 6):
                    ahead(U_GA, 2 * GA_SLABS, i, s0 + s)
                tile_done(U_GA, 2 * GA_SLABS, i, s0 + 5)
                nc.scalar.activation(aya[:, :], ps[1][:, 0:T], ACT.Copy).then_inc(evac, 1)
                act.wait_ge(ga_m, t + 1)
                nc.scalar.activation(tile_at(m_hi, t), one(aya[:, :]), ACT.Copy, scale=0.5).then_inc(ga_hi, 1)

        branch_a(0, True)
        with act.Fori(1, KT // 2) as i:
            branch_a(i, False)

        def out_tiles(i, first):
            for j in range(2):
                t = 2 * i + j
                ahead(U_OUT, 4, i, 2 * j)
                ahead(U_OUT, 4, i, 2 * j + 1)
                tile_done(U_OUT, 4, i, 2 * j + 1)
                if not (first and j == 0):
                    act.wait_ge(o_acc, t)
                nc.scalar.activation(tmp[:, :], ps[j][:, 0:T], ACT.Square)
                nc.scalar.activation(tile_at(mo, t), one(ps[j][:, 0:T]), ACT.Copy).then_inc(evac, 1)

        out_tiles(0, True)
        with act.Fori(1, KT // 2) as i:
            out_tiles(i, False)

        def rstd(n, count):
            act.wait_ge(n_ms, n)
            nc.scalar.activation(nrs[:, :], b_ms[:, 0:T], ACT.Ln, bias=eps, scale=1.0 / count).then_inc(n_ln, 1)
            act.wait_ge(n_ln, n)
            nc.scalar.activation(nrs[:, :], nrs[:, :], ACT.Exp, scale=-0.5).then_inc(n_rs, 1)

        def norm_in(norm, sq, col):
            for c in range(4):
                x2_ready(act, norm, c)
                for t in range(4 * c, 4 * c + 4):
                    op = nc.scalar.activation(h_hi[:, t], x2[:, t], ACT.Identity, scale=cols[:, col + t:col + t + 1])
                op.then_inc(n_hi, 1)
            for c in range(4):
                nc.scalar.activation(sq[:, 4 * c:4 * c + 4], x2[:, 4 * c:4 * c + 4], ACT.Square).then_inc(n_sq, 1)

        rstd(2, D)
        norm_in(0, nsq, C_FFNPRE)

        def up(i, first, half):
            for j in range(2):
                t = 2 * i + j
                tt = FT * half + t
                fu = U_FFN + HALF_U * half
                ahead(fu, 4, i, 2 * j)
                ahead(fu, 4, i, 2 * j + 1)
                tile_done(fu, 4, i, 2 * j + 1)
                if not (first and half == 0 and j == 0):
                    act.wait_ge(up_lo, tt)
                nc.scalar.activation(ru[j][:, :], ps[j][:, 0:T], ACT.Relu).then_inc(evac, 1)
                if first and half == 0 and j == 0:
                    rstd(3, D)
                act.wait_ge(up_sq, tt + 1)
                nc.scalar.activation(tile_at(u_hi, t), one(tmp[:, :]), ACT.Copy).then_inc(up_hi, 1)

        def down(i, first, half):
            for j in range(2):
                t = 2 * i + j
                fd = U_FFN + HALF_U * half + 2 * FT
                for s in range(4):
                    ahead(fd, 8, i, 4 * j + s)
                tile_done(fd, 8, i, 4 * j + 3)
                if half == 0:
                    nc.scalar.activation(tile_at(ffn, t), one(ps[j][:, 0:T]), ACT.Copy).then_inc(evac, 1)
                else:
                    if not (first and j == 0):
                        act.wait_ge(dn_acc, t)
                    nc.scalar.activation(tmp[:, :], ps[j][:, 0:T], ACT.Copy).then_inc(evac, 1)
                    act.wait_ge(dn_add, t + 1)
                    nc.scalar.activation(one(tmp[:, :]), tile_at(ffn, t), ACT.Square).then_inc(dn_sq, 1)

        for half in range(2):
            up(0, True, half)
            with act.Fori(1, FT // 2) as i:
                up(i, False, half)
            down(0, True, half)
            with act.Fori(1, KT // 2) as i:
                down(i, False, half)

        rstd(4, D)
        act.wait_ge(p_land, 16)
        nc.scalar.activation(p_hi[:, :, :], p_in[:, :, :], ACT.Copy).then_inc(p_his, 1)
        for s in range(4):
            ahead(U_PROJ, 4, 0, s)
            for j in range(4):
                if j < 3:
                    act.wait_ge(pj_tile, 3 * s + j + 1)
                else:
                    act.wait_ge(slab_used, U_PROJ + s + 1)
                nc.scalar.activation(e_out[:, 4 * s + j], ps[j % 2][:, 0:T], ACT.Copy).then_inc(evac, 1)
        norm_in(1, nsq3, C_PLE)

        def ple(i, first, last):
            for j in range(2):
                t = 2 * i + j
                for s in (2 * j, 2 * j + 1):
                    if not (last and s + AHEAD >= 4):
                        ahead(U_PLE, 4, i, s)
                if first and j == 0:
                    rstd(5, D)
                act.wait_ge(g_s, t + 1)
                nc.scalar.activation(gtg[:, j], gtg[:, j], ACT.Tanh, scale=0.5).then_inc(evac, 1)

        ple(0, True, False)
        with act.Fori(1, KT // 2 - 1) as i:
            ple(i, False, False)
        ple(KT // 2 - 1, False, True)

    @block.vector
    def _(dve):
        V = nc.vector

        def split_lo(m, k):
            dve.wait_ge(hi_done, m * RING + (k + 1))
            V.tensor_tensor(w_lo[:, k], raw[:, k], w_hi[:, k].bitcast(F32), ALU.subtract).then_inc(lo_done, 1)

        def ahead(first, per, it, s):
            split_lo(*slab(first, per, it, s + AHEAD))

        def steps(n):
            dve.wait_ge(dve_pro, n)

        for c in range(4):
            dve.wait_ge(n_sq, c + 1)
            V.tensor_tensor(x_sq[:, 4 * c:4 * c + 2], x_sq[:, 4 * c:4 * c + 2], x_sq[:, 4 * c + 2:4 * c + 4],
                            ALU.add).then_inc(n_add, 1)
            dve.wait_ge(n_add, 3 * c + 1)
            V.tensor_tensor(x_sq[:, 4 * c], x_sq[:, 4 * c], x_sq[:, 4 * c + 1], ALU.add).then_inc(n_add, 1)
            dve.wait_ge(n_add, 3 * c + 2)
            if c == 0:
                V.tensor_copy(x_sum[:, :], x_sq[:, 0]).then_inc(n_add, 1)
            else:
                V.tensor_tensor(x_sum[:, :], x_sum[:, :], x_sq[:, 4 * c], ALU.add).then_inc(n_add, 1)
        dve.wait_ge(cols_land, 32)
        lb2 = cols[:, C_LB:C_LB + 32].rearrange("p (r h) -> p r h", r=2)
        V.tensor_tensor(lbm[:, 0], lb2[:, 0], lb2[:, 1], ALU.max).then_inc(dve_pro, 1)
        steps(1)
        V.tensor_tensor(lbm[:, 1:3], lb2, lbm[:, 0:1].to_broadcast([P, 2, HEADS]),
                        ALU.subtract).then_inc(dve_pro, 1)

        def normalise(c):
            for t in range(4 * c, 4 * c + 4):
                V.scalar_tensor_tensor(hn32[:, t], x_in[:, t], cols[:, C_MIXPRE + t:C_MIXPRE + t + 1], x_rs[:, :],
                                       ALU.mult, ALU.mult).then_inc(n_xn, 1)

        def normalised_lo(c):
            dve.wait_ge(n_hi, c + 1)
            V.tensor_tensor(h_lo[:, 4 * c:4 * c + 4], hn32[:, 4 * c:4 * c + 4],
                            h_hi[:, 4 * c:4 * c + 4].bitcast(F32), ALU.subtract).then_inc(n_lo, 1)

        dve.wait_ge(n_rs, 1)
        normalise(0)
        split_lo(0, 0)
        normalise(1)
        for c in range(4):
            normalised_lo(c)
            if c < 2:
                normalise(c + 2)
                split_lo(0, c + 1)
        dve.wait_ge(act_pro, 2)
        V.tensor_tensor(lbm[:, 3], lbm[:, 1], lbm[:, 2], ALU.add).then_inc(dve_pro, 1)
        steps(3)
        V.reciprocal(lbm[:, 3], lbm[:, 3]).then_inc(dve_pro, 1)
        steps(4)
        V.tensor_tensor(lbm[:, 0], lbm[:, 1], lbm[:, 3], ALU.mult).then_inc(dve_pro, 1)
        steps(5)
        V.tensor_scalar(lbc[:, :, 0], lbm[:, 0], 0.5, 0.5, ALU.mult, ALU.add).then_inc(dve_pro, 1)
        V.tensor_scalar(lbc[:, :, 1], lbm[:, 0], -0.5, 0.5, ALU.mult, ALU.add).then_inc(dve_pro, 1)
        V.tensor_scalar(lbc[:, :, 2], lbm[:, 0], 0.5, -0.5, ALU.mult, ALU.add).then_inc(dve_pro, 1)
        def dt_absolute():
            dve.wait_ge(act_pro, 3)
            V.scalar_tensor_tensor(dta[:, :], dtz[:, :], -1.0, dtz[:, :], ALU.mult, ALU.max).then_inc(dve_pro, 1)
            V.tensor_scalar(an[:, :], an[:, :], -1.0, None, ALU.mult).then_inc(dve_pro, 1)

        def dt_cumulated():
            dve.wait_ge(act_pro, 4)
            V.tensor_scalar(dta[:, :], dte[:, :], 1.0, None, ALU.add).then_inc(dt_u, 1)
            dve.wait_ge(dt_u, 1)
            V.scalar_tensor_tensor(dtw[:, :], dta[:, :], -1.0, dte[:, :], ALU.add, ALU.subtract).then_inc(dt_u, 1)
            dve.wait_ge(act_pro, 5)
            dve.wait_ge(dt_u, 2)
            V.tensor_tensor(dtw[:, :], dtw[:, :], cum[:, :], ALU.mult).then_inc(dt_u, 1)
            dve.wait_ge(dt_u, 3)
            V.tensor_tensor(dte[:, :], dts[:, :], dtw[:, :], ALU.subtract).then_inc(dt_u, 1)
            dve.wait_ge(dt_u, 4)
            V.scalar_tensor_tensor(dts[:, :], dtz[:, :], 0.0, dte[:, :], ALU.max, ALU.add).then_inc(dve_pro, 1)
            steps(11)
            V.tensor_scalar(dta[:, :], dts[:, :], an[:, 0:1], None, ALU.mult).then_inc(dve_pro, 1)
            steps(12)
            V.tensor_tensor_scan(cum[:, :], consts[0:HD, K_RESET:K_RESET + T], dta[:, :], 0.0,
                                 ALU.mult, ALU.add).then_inc(dve_pro, 1)
            steps(13)
            V.tensor_scalar(dtw[:, 0:TP], cum[:, 0:TP], cum[:, TP - 1:TP], -1.0,
                            ALU.subtract, ALU.mult).then_inc(dve_pro, 1)
            cs = blocks(cum[:, TP:T], NB)
            V.tensor_tensor(blocks(dtw[:, TP:T], NB), cs[:, :, SB - 1:SB].to_broadcast([HD, NB, SB]), cs,
                            ALU.subtract).then_inc(dve_pro, 1)

        def dt_weights():
            dve.wait_ge(act_pro, 7)
            V.tensor_tensor(dtw[:, :], dtw[:, :], dts[:, :], ALU.mult).then_inc(dve_pro, 1)
            V.tensor_copy(elast[:, :].rearrange("p (b a) -> p b a", a=1),
                          blocks(ecum[:, :], NB)[:, :, SB - 1:SB]).then_inc(dve_pro, 1)

        def level(buf, off, h):
            width = T if h <= 2 else TP
            return buf[:, off:off + width].rearrange("p (b a j) -> p b a j", a=2, j=h)

        def hgrn(it, first, gemm):
            def nxt(s):
                if gemm:
                    ahead(U_HG, HG_SLABS, it, s)

            nxt(0)
            nxt(1)
            if not first:
                dve.wait_ge(hg_tok, it)
                V.tensor_tensor(hv3[32:64], hvt[0:32, 2], hv3[0:32].bitcast(F32), ALU.subtract)
                V.tensor_tensor(hk3[64:96], hkwt[0:32, 2], hk3[0:32].bitcast(F32),
                                ALU.subtract).then_inc(hg_tlo, 1)
                dve.wait_ge(hg_attn, it)
                V.tensor_tensor(hdm[:, :], b_diag[:, 0:384], consts[:, K_DIAG:K_DIAG + 384], ALU.mult)
                V.tensor_tensor(hdms[:, :], b_diag[0:32, 384:480], consts[0:32, K_DIAGS:K_DIAGS + 96],
                                ALU.mult).then_inc(hg_dm, 1)
                dve.wait_ge(hg_dm, it)
                V.tensor_reduce(hab[:, :, :], hdm[:, :].rearrange("p (l b t) -> p b t l", b=2, t=32),
                                AX.X, ALU.add)
                V.tensor_reduce(hats[:, :], hdms[:, :].rearrange("p (l t) -> p t l", t=32),
                                AX.X, ALU.add).then_inc(hg_red, 1)
                att = b_att[:, 0:256].rearrange("p (b t) -> p b t", b=2)
                V.tensor_copy(hatt[0:64, :, 64:128], att[0:64, :, 64:128])
                V.tensor_copy(hatt[0:32, :, 32:64], att[0:32, :, 32:64])
                V.tensor_copy(hatt[64:96, :, 96:128], att[64:96, :, 96:128])
                V.tensor_copy(htop[:, :], b_att[:, 256:384])
                dve.wait_ge(hg_red, it)
                for q in range(4):
                    op = V.tensor_copy(hatt[32 * q:32 * q + 32, :, 32 * q:32 * q + 32],
                                       hab[32 * q:32 * q + 32, :, :])
                op.then_inc(hg_ab, 1)
            if gemm:
                nxt(2)
                dve.wait_ge(evac, T_HG + it * HG_TILES + 1)
                V.tensor_copy(one(hcur[:, :]), tile_at(lbc, it)).then_inc(hg_cur, 1)
                dve.wait_ge(hg_cur, it + 1)
                V.tensor_scalar(hf[:, :], hth[:, :], hcur[:, 1:2], hcur[:, 0:1], ALU.mult, ALU.add)
                V.tensor_scalar(hk[:, :], hth[:, :], hcur[:, 2:3], hcur[:, 1:2], ALU.mult,
                                ALU.add).then_inc(hg_fk, 1)
                if first:
                    dt_absolute()
                    dt_cumulated()
                    dt_weights()
                nxt(3)
                dve.wait_ge(hg_lf, it + 1)
                V.tensor_tensor_scan(hcum[:, :], consts[:, K_RESET:K_RESET + T], hlf[:, :], 0.0,
                                     ALU.mult, ALU.add).then_inc(hg_cum, 1)
                dve.wait_ge(hg_cum, it + 1)
                V.tensor_scalar(hnc[:, :], hcum[:, P - 1:P], -1.0, None, ALU.mult)
                for h in LEVELS:
                    c4 = level(hcum, 0, h)
                    e4 = level(he, LOFF[h], h)
                    nb = (T if h <= 2 else TP) // (2 * h)
                    ref = c4[:, :, 0, h - 1:h].to_broadcast([P, nb, h])
                    V.tensor_tensor(e4[:, :, 1, :], c4[:, :, 1, :], ref, ALU.subtract)
                    V.tensor_tensor(e4[:, :, 0, :], ref, c4[:, :, 0, :], ALU.subtract)
                c3 = blocks(hcum[:, TP:T], NB)
                V.tensor_tensor(blocks(he[:, LAST_OFF:LAST_OFF + TS], NB),
                                c3[:, :, SB - 1:SB].to_broadcast([P, NB, SB]), c3,
                                ALU.subtract).then_inc(hg_arg, 1)
            nxt(4)
            if not first:
                dve.wait_ge(hg_p2, it)
                dve.wait_ge(hg_s0, it * 16)
                for b in range(NB):
                    half = (b_tv, b_tk)[b // 4]
                    V.scalar_tensor_tensor(hsn[:, b], hs0[:, b], hel[:, b:b + 1],
                                           half[:, P * (b % 4):P * (b % 4) + P], ALU.mult, ALU.add)
                V.tensor_copy(hsp[:, :], b_att[:, 3 * P:4 * P]).then_inc(hg_st, 1)
            if gemm:
                nxt(5)
                dve.wait_ge(hg_exp, it + 1)
                if not first:
                    dve.wait_ge(hg_st, it)
                for h in LEVELS:
                    e4, k4, q4 = level(he, LOFF[h], h), level(hk, 0, h), level(hq, 0, h)
                    V.tensor_tensor(e4[:, :, 0, :], e4[:, :, 0, :], k4[:, :, 0, :], ALU.mult)
                    V.tensor_tensor(e4[:, :, 1, :], e4[:, :, 1, :], q4[:, :, 1, :], ALU.mult)
                V.tensor_tensor(hkw[:, :], hkw[:, :], hk[:, 0:TP], ALU.mult)
                V.tensor_tensor(hkt[:, :], hkt[:, :], hk[:, 0:P], ALU.mult)
                V.tensor_tensor(hqt[:, :], hqt[:, :], hq[:, P:TP], ALU.mult)
                V.tensor_tensor(hqs[:, :], hec[:, :], hq[:, TP:T], ALU.mult)
                V.tensor_tensor(hks[:, :], he[:, LAST_OFF:LAST_OFF + TS], hk[:, TP:T], ALU.mult)
                V.tensor_copy(hel[:, :].rearrange("p (b a) -> p b a", a=1),
                              blocks(hec[:, :], NB)[:, :, SB - 1:SB]).then_inc(hg_w, 1)
            if not first:
                dve.wait_ge(hg_rs, it)
                V.scalar_tensor_tensor(hsg[:, :], htg[:, :], 1.0, hg[:, :], ALU.add, ALU.mult)
                V.scalar_tensor_tensor(hon[:, :], b_o[:, 0:T], cols[:, C_HGN:C_HGN + 1], hrs[:, :],
                                       ALU.mult, ALU.mult).then_inc(hg_on, 1)
                dve.wait_ge(hg_on, it)
                V.scalar_tensor_tensor(hso[:, :], hon[:, :], 0.5, hsg[:, :], ALU.mult,
                                       ALU.mult).then_inc(hg_so, 1)
            nxt(6)
            if not first:
                dve.wait_ge(hg_ohi, it)
                V.tensor_tensor(tile_at(o_lo, it - 1), one(hso[:, :]), tile_at(o_hi, it - 1).bitcast(F32),
                                ALU.subtract).then_inc(hg_olo, 1)
            nxt(7)

        V.memset(hatt[:, :, :], 0.0).then_inc(hg_zero, 1)
        dve.wait_ge(hg_zero, 1)
        hgrn(0, True, True)
        with dve.Fori(1, HEADS) as it:
            hgrn(it, False, True)
        hgrn(HEADS, False, False)

        def branch_b(j, first):
            for s in range(GB_SLABS):
                ahead(U_GB, GB_SLABS, j, s)
            dve.wait_ge(evac, j * 2 + (T_GB + 2))
            if not first:
                dve.wait_ge(gb_out, j * 16)
            V.scalar_tensor_tensor(bmb[:, :], btg[:, :], 1.0, byb[:, :], ALU.add, ALU.mult).then_inc(gb_mb, 1)

        branch_b(0, True)
        with dve.Fori(1, KT) as j:
            branch_b(j, False)

        def cur_cols(first_col, g):
            if isinstance(g, int):
                return cols[:, first_col + 4 * g:first_col + 4 * g + 4]
            return cols[:, bass.ds(g * 4 + first_col, 4)]

        def ssd(g, first, gemm):
            r = g - 1

            def y_pair(gg, p):
                dve.wait_ge(sg_y, gg * 4 + (p + 1))
                V.scalar_tensor_tensor(yf[:, p], xf[:, p], dcur[:, p:p + 1], bank[(5, 0)[p % 2]][:, 0:T],
                                       ALU.mult, ALU.add).then_inc(sg_yf, 1)

            def silu_z(gg, c):
                dve.wait_ge(evac, gg * SG_TILES + (T_SG + 7 + c))
                V.scalar_tensor_tensor(sz[:, c], cth[:, :], 1.0, sz[:, c], ALU.add, ALU.mult).then_inc(sg_sz, 1)

            def update(b):
                for i in (b, b + 1):
                    v = ht[:, i % 4].rearrange("p (h d) -> p h d", h=GH)
                    V.tensor_tensor(v, v, el[:, :, i:i + 1].to_broadcast([P, GH, HD]), ALU.mult).then_inc(sg_upa, 1)
                for i in (b, b + 1):
                    dve.wait_ge(sg_upa, r * NB + (i + 1))
                    dve.wait_ge(sg_su, r * NB + (i + 1))
                    V.tensor_tensor(ht[:, i % 4], ht[:, i % 4], bank[2 + i % 2][:, :], ALU.add).then_inc(sg_up, 1)

            def conv(c):
                n = g * (4 * XT) + 4 * c
                dve.wait_ge(evac, g * SG_TILES + (T_SG + 1 + c))
                src = craw[:, c % 2]
                seqs = blocks(src[:, SOFF:RAWC], NB)
                V.tensor_copy(seqs[:, :, 0:CW - 1], cst[:, c]).then_inc(sg_cv, 1)
                dve.wait_ge(sg_cv, n + 1)
                V.tensor_scalar(ccv[:, 0:CVC], src[:, 0:CVC], prh[:, c, 0:1], prh[:, c, CW:CW + 1],
                                ALU.mult, ALU.add).then_inc(sg_cv, 1)
                for w in range(1, CW):
                    dve.wait_ge(sg_cv, n + (w + 1))
                    op = V.scalar_tensor_tensor(ccv[:, 0:CVC], src[:, w:w + CVC], prh[:, c, w:w + 1],
                                                ccv[:, 0:CVC], ALU.mult, ALU.add)
                    op.then_inc(sg_cv if w < CW - 1 else sg_conv, 1)
                V.tensor_copy(ncv[:, c, 0:CW - 1], src[:, TP:SOFF])
                V.tensor_copy(blocks(ncv[:, c, CW - 1:], NB), seqs[:, :, SB:]).then_inc(sg_nc, 1)

            def silu(c):
                dst = (bf[:, :], cf[:, :])[c] if c < 2 else xf[:, c - 2]
                dve.wait_ge(sg_th, g * XT + (c + 1))
                V.scalar_tensor_tensor(dst[:, 0:TP], cth[:, 0:TP], 1.0, ccv[:, 0:TP], ALU.add, ALU.mult)
                V.scalar_tensor_tensor(blocks(dst[:, TP:T], NB), blocks(cth[:, TP:T], NB), 1.0, cv_samples,
                                       ALU.add, ALU.mult).then_inc(sg_silu, 1)

            def mask_exponentials(q):
                dve.wait_ge(sg_exp, g * 2 + (q + 1))
                if q == 0:
                    dve.wait_ge(sg_cbm, g + 1)
                v = me[:, 4 * q:4 * q + 4, 0:384]
                V.tensor_tensor(v, v, cbm[:, 0:384].unsqueeze(1).to_broadcast([P, 4, 384]), ALU.mult)
                v = me[0:32, 4 * q:4 * q + 4, 384:416]
                V.tensor_tensor(v, v, cbm[0:32, 384:416].unsqueeze(1).to_broadcast([32, 4, 32]),
                                ALU.mult).then_inc(sg_m, 1)

            def weighted_x(dst, q):
                for b in range(3):
                    n = 32 if b == 2 else P
                    src = bank[2 + b][0:n, :].rearrange("p (h d) -> p h d", h=GH)
                    op = V.tensor_tensor(dst[0:n, b].rearrange("p (h d) -> p h d", h=GH), src,
                                         tcur[0:n, q, b, :].unsqueeze(2).to_broadcast([n, GH, HD]), ALU.mult)
                return op

            for s in range(SG_SLABS):
                if not gemm and s > 11:
                    break
                if not first:
                    if s == 0:
                        y_pair(r, 3)
                        silu_z(r, 3)
                        dve.wait_ge(sg_yf, g * 4)
                        dve.wait_ge(sg_sz, g * 4)
                    if s == 1:
                        dve.wait_ge(sg_ec_in, g * 48)
                        dve.wait_ge(sg_it, r * 2 + 1)
                    if s == 6:
                        dve.wait_ge(sg_it, r * 2 + 2)
                    if s in (1, 2, 6, 7):
                        update({1: 0, 2: 2, 6: 4, 7: 6}[s])
                    if s == 7:
                        V.tensor_tensor(yti[:, :, :], blocks(bank[4][:, T:T + 4 * TS], 4), ecp[:, :, :],
                                        ALU.mult).then_inc(sg_yi, 1)
                        dve.wait_ge(sg_yi, r * 2 + 1)
                        V.tensor_tensor(yf[:, :, TP:T], yf[:, :, TP:T], yti[:, :, :], ALU.add).then_inc(sg_yi, 1)
                        dve.wait_ge(sg_yi, r * 2 + 2)
                        V.tensor_tensor(yf[:, :, :], yf[:, :, :], sz[:, :, :], ALU.mult).then_inc(sg_g, 1)
                    if s == 11:
                        V.tensor_copy(ncur[:, :], cur_cols(C_SSMN, r)).then_inc(sg_ncur, 1)
                        dve.wait_ge(sg_ncur, g)
                        dve.wait_ge(sg_rs, g)
                        for p in range(4):
                            dst = y32[:, 4 * r + p:4 * r + p + 1] if not gemm else y32[:, bass.ds(r * 4 + p, 1)]
                            op = V.scalar_tensor_tensor(dst, yf[:, p:p + 1], ncur[:, p:p + 1], one(yrs[:, :]),
                                                        ALU.mult, ALU.mult)
                        op.then_inc(sg_y32, 1)
                if not gemm:
                    continue
                if s % 2 == 1 and 3 <= s <= 13:
                    silu(s // 2 - 1)
                if s == 13:
                    mask_exponentials(0)
                ahead(U_SG, SG_SLABS, g, s)
                if s == 0:
                    if first:
                        dve.wait_ge(act_pro, 9)
                    dve.wait_ge(sg_par_in, (g + 1) * 32)
                    V.tensor_scalar(prh[:, :, :], prm[:, :, :], 0.5, None, ALU.mult).then_inc(sg_prh, 1)
                    hs = slice(GH * g, GH * g + GH) if isinstance(g, int) else bass.ds(g * GH, GH)
                    V.tensor_copy(tcur[:, :, 0:2, :], tok[:, :, 0:2, hs])
                    V.tensor_copy(tcur[0:32, :, 2, :], tok[0:32, :, 2, hs])
                    V.tensor_copy(dcur[:, :], cur_cols(C_DSKIP, g)).then_inc(sg_cur, 1)
                    dve.wait_ge(sg_prh, g + 1)
                    dve.wait_ge(sg_cur, g + 1)
                    if not first:
                        dve.wait_ge(sg_nc_out, g * 16)
                if s % 2 == 0 and 2 <= s <= 12:
                    conv(s // 2 - 1)
                if s == 8:
                    if not first:
                        dve.wait_ge(sg_it, g * 2)
                    dve.wait_ge(sg_silu, g * XT + 2)
                    V.tensor_copy(cfs[:, :], cf[:, TP:T]).then_inc(sg_cfs, 1)
                if s == 8:
                    dve.wait_ge(sg_bt, g + 1)
                    V.tensor_tensor(bt3[64:96], bt[0:32, 2], bt3[0:32].bitcast(F32),
                                    ALU.subtract).then_inc(sg_btlo, 1)
                    dve.wait_ge(sg_bc, g + 1)
                    V.tensor_tensor(cbm[:, 0:384], bank[1][:, 0:384], consts[:, K_CB:K_CB + 384], ALU.mult)
                    V.tensor_tensor(cbm[0:32, 384:416], bank[1][0:32, 384:416],
                                    consts[0:32, K_CB + 384:K_CB + 416], ALU.mult).then_inc(sg_cbm, 1)
                if s == 10:
                    dve.wait_ge(sg_cbc_in, (g + 1) * 16)
                    if not first:
                        dve.wait_ge(sg_ms, g)
                    exponents(V, me, cbc, tcur, 0).then_inc(sg_seg, 1)
                if s == 14:
                    dve.wait_ge(sg_xt, g + 1)
                    weighted_x(xd, 0).then_inc(sg_xd, 1)
                if s == 15:
                    mask_exponentials(1)
                    weighted_x(xw, 2).then_inc(sg_xw, 1)
                if s in (14, 16, 18):
                    silu_z(g, (s - 14) // 2)
                if s == 18:
                    dve.wait_ge(sg_xwhi, g + 1)
                    V.tensor_tensor(xw3[32:64], xw[0:32, 2], xw3[0:32].bitcast(F32),
                                    ALU.subtract).then_inc(sg_xwlo, 1)
                if s in (17, 18, 19):
                    y_pair(g, s - 17)

        dve.wait_ge(slab_used, U_SG)
        dve.wait_ge(hg_out, 32 * HEADS)
        dve.wait_ge(gb_out, 16 * KT)
        V.memset(craw[:, :, 0:CW - 1], 0.0).then_inc(sg_raw0, 1)
        dve.wait_ge(sg_raw0, 1)
        ssd(0, True, True)
        with dve.Fori(1, GROUPS) as g:
            ssd(g, False, True)
        ssd(GROUPS, False, False)

        for i in range(4):
            dve.wait_ge(sg_ht_out[i], 32 * GROUPS)
        dve.wait_ge(sg_nc_out, 16 * GROUPS)
        dve.wait_ge(sg_sp_out, 16 * GROUPS)
        for c in range(8):
            dve.wait_ge(y_his, c + 1)
            V.tensor_tensor(y_lo[:, 4 * c:4 * c + 4], y32[:, 4 * c:4 * c + 4],
                            y_hi[:, 4 * c:4 * c + 4].bitcast(F32), ALU.subtract).then_inc(y_los, 1)
            if c in (1, 3):
                ahead(U_GA, 2 * GA_SLABS, 0, c // 2)

        def branch_a(i, first):
            for j in range(2):
                t = i * 2 + j
                for s in range(2 if first and j == 0 else 0, GA_SLABS):
                    ahead(U_GA, 2 * GA_SLABS, i, GA_SLABS * j + s)
                dve.wait_ge(evac, t * 2 + (T_GA + 2))
                dve.wait_ge(ga_in, t * 16 + 16)
                V.scalar_tensor_tensor(aya[:, :], atg[:, :], 1.0, aya[:, :], ALU.add, ALU.mult).then_inc(ga_t, 1)
                dve.wait_ge(ga_t, t + 1)
                V.tensor_tensor(aya[:, :], aya[:, :], amb[:, :], ALU.add).then_inc(ga_m, 1)
                dve.wait_ge(ga_hi, t + 1)
                V.scalar_tensor_tensor(tile_at(m_lo, t), one(aya[:, :]), 0.5, tile_at(m_hi, t).bitcast(F32),
                                       ALU.mult, ALU.subtract).then_inc(ga_lo, 1)

        branch_a(0, True)
        with dve.Fori(1, KT // 2) as i:
            branch_a(i, False)

        def weight(col, t):
            return cols[:, col + t:col + t + 1] if isinstance(t, int) else cols[:, bass.ds(t + col, 1)]

        def out_tiles(i, first):
            for j in range(2):
                t = i * 2 + j
                ahead(U_OUT, 4, i, 2 * j)
                ahead(U_OUT, 4, i, 2 * j + 1)
                dve.wait_ge(evac, t + (T_OUT + 1))
                if first and j == 0:
                    V.tensor_copy(acc[:, :], tmp[:, :]).then_inc(o_acc, 1)
                else:
                    dve.wait_ge(o_acc, t)
                    V.tensor_tensor(acc[:, :], acc[:, :], tmp[:, :], ALU.add).then_inc(o_acc, 1)
                V.tensor_scalar(tile_at(mo, t), tile_at(mo, t), weight(C_MIXPOST, t), None, ALU.mult).then_inc(o_w, 1)

        out_tiles(0, True)
        with dve.Fori(1, KT // 2) as i:
            out_tiles(i, False)

        def add_normed(norm, c, src, residual):
            v = src[:, 4 * c:4 * c + 4]
            V.tensor_tensor(v, v, four(nrs[:, :]), ALU.mult).then_inc(x2_a, 1)
            dve.wait_ge(x2_a, XV * norm + c + 1)
            V.tensor_tensor(x2[:, 4 * c:4 * c + 4], v, residual[:, 4 * c:4 * c + 4], ALU.add).then_inc(x2_b, 1)

        def norm_lo(norm, c, col):
            dve.wait_ge(n_hi, 4 * (norm + 1) + c + 1)
            for t in range(4 * c, 4 * c + 4):
                op = V.scalar_tensor_tensor(h_lo[:, t], x2[:, t], cols[:, col + t:col + t + 1],
                                            h_hi[:, t].bitcast(F32), ALU.mult, ALU.subtract)
            op.then_inc(n_lo, 1)

        def sum_tiles(norm, sq):
            n = 12 + 5 * norm
            for c in range(1, 4):
                dve.wait_ge(n_sq, 4 * norm + 4 + c + 1)
                if c > 1:
                    dve.wait_ge(n_add, n + c - 1)
                V.tensor_tensor(sq[:, 0:4], sq[:, 0:4], sq[:, 4 * c:4 * c + 4], ALU.add).then_inc(n_add, 1)
            for k, m in ((4, 2), (5, 1)):
                dve.wait_ge(n_add, n + k - 1)
                V.tensor_tensor(sq[:, 0:m], sq[:, 0:m], sq[:, m:2 * m], ALU.add).then_inc(n_add, 1)

        dve.wait_ge(n_rs, 2)
        dve.wait_ge(xr_in, 16)
        dve.wait_ge(o_w, KT)
        add_normed(0, 0, mo, x_res)
        add_normed(0, 1, mo, x_res)
        norm_lo(0, 0, C_FFNPRE)
        add_normed(0, 2, mo, x_res)
        for c in range(1, 4):
            norm_lo(0, c, C_FFNPRE)
        sum_tiles(0, nsq)

        def up(i, first, half):
            for j in range(2):
                t = i * 2 + j
                tt = t + FT * half
                fu = U_FFN + HALF_U * half
                ahead(fu, 4, i, 2 * j)
                ahead(fu, 4, i, 2 * j + 1)
                dve.wait_ge(evac, t + (T_FFN + HALF_T * half + 1))
                if first and half == 0 and j == 0:
                    dve.wait_ge(n_rs, 3)
                V.tensor_tensor(ru[j][:, :], ru[j][:, :], nrs[:, :], ALU.mult).then_inc(up_n, 1)
                dve.wait_ge(up_n, tt + 1)
                V.tensor_tensor(tmp[:, :], ru[j][:, :], ru[j][:, :], ALU.mult).then_inc(up_sq, 1)
                dve.wait_ge(up_hi, tt + 1)
                V.tensor_tensor(tile_at(u_lo, t), one(tmp[:, :]), tile_at(u_hi, t).bitcast(F32),
                                ALU.subtract).then_inc(up_lo, 1)

        def down(i, first, half):
            for j in range(2):
                t = i * 2 + j
                for s in range(4):
                    ahead(U_FFN + HALF_U * half + 2 * FT, 8, i, 4 * j + s)
                if half == 0:
                    continue
                dve.wait_ge(evac, t + (T_FFN + HALF_T + FT + 1))
                V.tensor_tensor(tile_at(ffn, t), tile_at(ffn, t), one(tmp[:, :]), ALU.add).then_inc(dn_add, 1)
                dve.wait_ge(dn_sq, t + 1)
                if first and j == 0:
                    V.tensor_copy(acc[:, :], tmp[:, :]).then_inc(dn_acc, 1)
                else:
                    dve.wait_ge(dn_acc, t)
                    V.tensor_tensor(acc[:, :], acc[:, :], tmp[:, :], ALU.add).then_inc(dn_acc, 1)
                V.tensor_scalar(tile_at(ffn, t), tile_at(ffn, t), weight(C_FFNPOST, t), None,
                                ALU.mult).then_inc(dn_w, 1)

        for half in range(2):
            up(0, True, half)
            with dve.Fori(1, FT // 2) as i:
                up(i, False, half)
            down(0, True, half)
            with dve.Fori(1, KT // 2) as i:
                down(i, False, half)

        dve.wait_ge(p_his, 1)
        V.tensor_tensor(p_lo[:, :, :], p_in[:, :, :], p_hi[:, :, :].bitcast(F32), ALU.subtract).then_inc(p_los, 1)
        ahead(U_PROJ, 4, 0, 0)
        ahead(U_PROJ, 4, 0, 1)
        dve.wait_ge(n_rs, 4)
        dve.wait_ge(dn_w, KT)
        add_normed(1, 0, ffn, x2)
        ahead(U_PROJ, 4, 0, 2)
        add_normed(1, 1, ffn, x2)
        ahead(U_PROJ, 4, 0, 3)
        add_normed(1, 2, ffn, x2)
        for c in range(4):
            norm_lo(1, c, C_PLE)
        sum_tiles(1, nsq3)

        def ple(i, last):
            for j in range(2):
                t = i * 2 + j
                for s in (2 * j, 2 * j + 1):
                    if not (last and s + AHEAD >= 4):
                        ahead(U_PLE, 4, i, s)
                dve.wait_ge(slab_used, i * 4 + (U_PLE + 2 * j + 2))
                if isinstance(i, int) and i == 0 and j == 0:
                    dve.wait_ge(n_rs, 5)
                if not (isinstance(i, int) and i == 0):
                    dve.wait_ge(g_y, t - 1)
                V.tensor_tensor(gtg[:, j], ps[j][:, 0:T], nrs[:, :], ALU.mult).then_inc(g_s, 1)
                dve.wait_ge(evac, t + (T_PLE + 1))
                V.scalar_tensor_tensor(one(gtg[:, j]), one(gtg[:, j]), 1.0, tile_at(e_out, t),
                                       ALU.add, ALU.mult).then_inc(g_t, 1)
                dve.wait_ge(g_t, t + 1)
                V.scalar_tensor_tensor(tile_at(x2, t), one(gtg[:, j]), 0.5, tile_at(x2, t),
                                       ALU.mult, ALU.add).then_inc(g_y, 1)

        ple(0, False)
        with dve.Fori(1, KT // 2 - 1) as i:
            ple(i, False)
        ple(KT // 2 - 1, True)

    @block.tensor
    def _(pe):
        M = nc.tensor

        def multiply(m, k, out, hi, lo, kt0, first, last, chunks=None):
            pe.wait_ge(lo_done, m * RING + (k + 1))
            for i in range(SK):
                if chunks is not None and i % 4 == 0:
                    pe.wait_ge(chunks[0], chunks[1] + (kt0 + i) // 4 + 1)
                M.matmul(out, w_hi[:, k, i], hi[:, kt0 + i], start=first and i == 0, stop=False)
                M.matmul(out, w_hi[:, k, i], lo[:, kt0 + i], start=False, stop=False)
                op = M.matmul(out, w_lo[:, k, i], hi[:, kt0 + i], start=False, stop=last and i == SK - 1)
            op.then_inc(slab_used, 1)

        def free(tile, n):
            pe.wait_ge(evac, n + (tile - 1))

        def mean_square(sq, norm):
            pe.wait_ge(n_add, 12 + 5 * (norm + 1))
            M.matmul(b_ms[:, 0:T], ones, sq[:, 0], start=True, stop=True).then_inc(n_ms, 1)

        pe.wait_ge(cst_land, 16)
        pe.wait_ge(n_add, 12)
        M.matmul(b_ms[:, 0:T], ones, x_sum[:, :], start=True, stop=True).then_inc(n_ms, 1)

        def dt_product():
            pe.wait_ge(wdt_land, 16)
            for t in range(KT):
                op = M.matmul(b_tv[0:HD, 0:T], wdt[:, t], hn32[:, t], start=t == 0, stop=t == KT - 1)
            op.then_inc(pe_pro, 1)

        def dt_transposes():
            pe.wait_ge(dve_pro, 16)
            for q, src in enumerate((dts, cum, dtw)):
                for b in range(2):
                    M.transpose(b_o[:, (2 * q + b) * HD:(2 * q + b + 1) * HD], src[:, P * b:P * b + P],
                                ident[0:HD, 0:HD])
                op = M.transpose(b_ms[0:32, q * HD:(q + 1) * HD], src[:, TP:T], ident[0:HD, 0:HD])
            op.then_inc(pe_pro, 1)

        def hgrn(it, first, gemm):
            def nxt(s):
                if not gemm:
                    if s in (1, 3):
                        if s == 1:
                            free(T_GB, 0)
                        multiply(*slab(U_GB, GB_SLABS, 0, s // 2), ps[0][:, 0:T], h_hi, h_lo, SK * (s // 2),
                                 s == 1, s == 3)
                    return
                if s % 2 == 0 and not (first and s < 4):
                    free(T_HG + s // 2, it * HG_TILES)
                multiply(*slab(U_HG, HG_SLABS, it, s), ps[s // 2 % 2][:, 0:T], h_hi, h_lo, SK * (s % 2),
                         s % 2 == 0, s % 2 == 1, (n_lo, 0) if first and s < 2 else None)
                if first and s == 1:
                    dt_product()
                if first and s == 5:
                    dt_transposes()

            nxt(0)
            if not first:
                pe.wait_ge(hg_w, it)
                pe.wait_ge(evac, it * HG_TILES + (T_HG - 1))
                M.transpose(b_tv[:, 0:P], hvv[:, 0:P], ident)
                M.transpose(b_tv[:, P:TP], hvv[:, P:TP], ident)
                M.transpose(b_tv[0:32, TP:TP + P], hvv[:, TP:T], ident)
                M.transpose(b_tk[:, 0:P], hkw[:, 0:P], ident)
                M.transpose(b_tk[:, P:TP], hkw[:, P:TP], ident)
                M.transpose(b_tk[0:32, TP:TP + P], hks[:, :], ident).then_inc(hg_tr, 1)
                for b in range(2):
                    c, o = P * b, LOFF[64]
                    M.matmul(b_att[0:64, c + 64:c + P], he[:, o + c:o + c + 64], he[:, o + c + 64:o + c + P],
                             start=True, stop=True)
                    o = LOFF[32]
                    for q in (0, 64):
                        M.matmul(b_att[q:q + 32, c + q + 32:c + q + 64], he[:, o + c + q:o + c + q + 32],
                                 he[:, o + c + q + 32:o + c + q + 64], start=True, stop=True)
                M.matmul(b_att[:, TP:TP + P], hkt[:, :], hqt[:, :], start=True, stop=True)
                for n, h in enumerate(DIAG):
                    for b in range(2):
                        for q in range(4):
                            c = P * b + 32 * q
                            ks = hk[:, c:c + 32] if h == 0 else he[:, LOFF[h] + c:LOFF[h] + c + 32]
                            qs = hq[:, c:c + 32] if h == 0 else he[:, LOFF[h] + c:LOFF[h] + c + 32]
                            M.matmul(b_diag[32 * q:32 * q + 32, 64 * n + 32 * b:64 * n + 32 * b + 32], ks, qs,
                                     start=True, stop=True)
                for n, h in enumerate(DIAG_S):
                    ks = hk[:, TP:T] if h == 0 else he[:, LOFF[h] + TP:LOFF[h] + T]
                    qs = hq[:, TP:T] if h == 0 else he[:, LOFF[h] + TP:LOFF[h] + T]
                    op = M.matmul(b_diag[0:32, 384 + 32 * n:416 + 32 * n], ks, qs, start=True, stop=True)
                op.then_inc(hg_attn, 1)
            nxt(1)
            nxt(2)
            if not first:
                pe.wait_ge(hg_tok, it)
                pe.wait_ge(hg_ab, it)
                pe.wait_ge(hg_s0, it * 16)
                pe.wait_ge(hg_vbd, it)
                M.matmul(b_o[:, 0:P], hvt[:, 0], hatt[:, 0], start=True, stop=True)
                M.matmul(b_o[:, P:TP], hvt[:, 1], hatt[:, 1], start=True, stop=False)
                M.matmul(b_o[:, P:TP], hvt[:, 0], htop[:, :], start=False, stop=True)
                M.matmul(b_o[:, TP:T], hvt[0:32, 2], hats[:, :], start=True, stop=True)
                for b in range(NB):
                    M.matmul(b_o[:, TP + SB * b:TP + SB * b + SB], hs0[:, b], hqs[:, SB * b:SB * b + SB],
                             start=False, stop=True, skip_group_check=True)
                M.matmul(b_att[:, 3 * P:4 * P], hkwt[:, 0], hvt[:, 0], start=True, stop=False)
                M.matmul(b_att[:, 3 * P:4 * P], hkwt[:, 1], hvt[:, 1], start=False, stop=True)
                M.matmul(b_tv[:, :], hk3[:, :], hvbd[:, 0:4].rearrange("p b n -> p (b n)"), start=True, stop=True)
                M.matmul(b_tk[:, :], hk3[:, :], hvbd[:, 4:8].rearrange("p b n -> p (b n)"), start=True,
                         stop=True).then_inc(hg_p2, 1)
            nxt(3)
            nxt(4)
            if not first:
                pe.wait_ge(hg_sq, it)
                M.matmul(b_ms[:, 0:T], ones, hsq[:, :], start=True, stop=True).then_inc(hg_ms, 1)
            for s in range(5, HG_SLABS):
                nxt(s)

        hgrn(0, True, True)
        with pe.Fori(1, HEADS) as it:
            hgrn(it, False, True)
        hgrn(HEADS, False, False)

        def branch_b(j, first):
            for s in range(2 if first else 0, GB_SLABS):
                if s % 2 == 0:
                    free(T_GB + s // 2, j * 2)
                if first:
                    pe.wait_ge(hg_olo, HEADS // 2 * (s - 1))
                hi, lo = (h_hi, h_lo) if s < 2 else (o_hi, o_lo)
                multiply(*slab(U_GB, GB_SLABS, j, s), ps[s // 2][:, 0:T], hi, lo, SK * (s % 2), s % 2 == 0, s % 2 == 1)

        branch_b(0, True)
        with pe.Fori(1, KT) as j:
            branch_b(j, False)

        def ssd(g, first, gemm):
            r = g - 1

            def old_states(half):
                for b in range(4):
                    pe.wait_ge(sg_ht_in[b], r * 32 + 16 * (half + 1))
                pe.wait_ge(sg_cfs, g)
                for p in range(4):
                    for b in range(4):
                        seq = 4 * half + b
                        o = T + TS * p + SB * seq
                        op = M.matmul(bank[4][:, o:o + SB], ht[:, b, P * p:P * p + P], cfs[:, SB * seq:SB * seq + SB],
                                      start=True, stop=True)
                op.then_inc(sg_it, 1)

            def new_states(b):
                for i in (b, b + 1):
                    if i >= 2:
                        pe.wait_ge(sg_up, r * NB + (i - 1))
                    M.matmul(bank[2 + i % 2][:, :], bbd[:, i], xw3[:, :], start=True, stop=True).then_inc(sg_su, 1)

            for s in range(SG_SLABS):
                if not gemm and s > 9:
                    break
                if gemm:
                    t = s // 2
                    if s % 2 == 0:
                        free(T_SG + t, g * SG_TILES)
                    multiply(*slab(U_SG, SG_SLABS, g, s), ps[t % 2][:, 0:T], h_hi, h_lo, SK * (s % 2),
                             s % 2 == 0, s % 2 == 1)
                if not first:
                    if s == 0:
                        old_states(0)
                        pe.wait_ge(sg_bbd, g)
                        pe.wait_ge(sg_xwlo, g)
                        new_states(0)
                    if s == 1:
                        new_states(2)
                    if s in (2, 3) and not gemm:
                        if s == 2:
                            free(T_GA, 0)
                        multiply(*slab(U_GA, 2 * GA_SLABS, 0, s - 2), ps[0][:, 0:T], h_hi, h_lo, SK * (s - 2),
                                 s == 2, s == 3)
                    if s == 5:
                        old_states(1)
                        new_states(4)
                    if s == 6:
                        new_states(6)
                    if s == 9:
                        pe.wait_ge(sg_sq, g)
                        for p in range(4):
                            op = M.matmul(bank[4][:, 0:T], ones, ysq[:, p], start=p == 0, stop=p == 3)
                        op.then_inc(sg_ms, 1)
                if not gemm:
                    continue
                if s == 6:
                    pe.wait_ge(sg_silu, g * XT + 2)
                    if not first:
                        pe.wait_ge(sg_spe, g)
                    M.transpose(bank[0][:, 0:P], bf[:, 0:P], ident)
                    M.transpose(bank[0][:, P:TP], bf[:, P:TP], ident)
                    M.transpose(bank[0][0:32, TP:TP + P], bf[:, TP:T], ident)
                    M.matmul(bank[1][:, 0:TP], bf[:, 0:P], cf[:, 0:TP], start=True, stop=True)
                    M.matmul(bank[1][:, TP:TP + P], bf[:, P:TP], cf[:, P:TP], start=True, stop=True)
                    M.matmul(bank[1][0:32, 384:416], bf[:, TP:T], cf[:, TP:T], start=True,
                             stop=True).then_inc(sg_bc, 1)
                if s == 14:
                    pe.wait_ge(sg_silu, g * XT + 6)
                    for c in range(4):
                        M.transpose(bank[2][:, P * c:P * c + P], xf[:, c, 0:P], ident)
                        M.transpose(bank[3][:, P * c:P * c + P], xf[:, c, P:TP], ident)
                        op = M.transpose(bank[4][0:32, P * c:P * c + P], xf[:, c, TP:T], ident)
                    op.then_inc(sg_xt, 1)
                if s == 17:
                    pe.wait_ge(sg_xw, g + 1)
                    for p in range(4):
                        for b in range(2):
                            op = M.matmul(bank[1][:, P * p:P * p + P], xw[:, b, P * p:P * p + P], bt[:, b],
                                          start=b == 0, stop=b == 1)
                    op.then_inc(sg_sp, 1)
                if s >= 16:
                    p = s - 16
                    if p == 0:
                        pe.wait_ge(sg_xd, g + 1)
                        pe.wait_ge(sg_m, g * 2 + 1)
                        pe.wait_ge(sg_bt, g + 1)
                    if p == 2:
                        pe.wait_ge(sg_m, g * 2 + 2)
                    if p >= 2:
                        pe.wait_ge(sg_yf, g * 4 + (p - 1))
                    y = bank[(5, 0)[p % 2]]
                    for hh in range(2):
                        j = 2 * p + hh
                        lo, at = HD * hh, HD * j
                        M.matmul(y[lo:lo + HD, 0:TP], xd[:, 0, at:at + HD], me[:, j, 0:TP], start=True, stop=True)
                        M.matmul(y[lo:lo + HD, P:TP], xd[:, 1, at:at + HD], me[:, j, TP:TP + P], start=False,
                                 stop=True, skip_group_check=True)
                        op = M.matmul(y[lo:lo + HD, TP:T], xd[0:32, 2, at:at + HD], me[0:32, j, 384:416],
                                      start=True, stop=True)
                    op.then_inc(sg_y, 1)

        ssd(0, True, True)
        with pe.Fori(1, GROUPS) as g:
            ssd(g, False, True)
        ssd(GROUPS, False, False)

        def branch_a(i, first):
            for j in range(2):
                for s in range(2 if first and j == 0 else 0, GA_SLABS):
                    if s in (0, 2):
                        free(T_GA + 2 * j + s // 2, i * 4)
                    at = slab(U_GA, 2 * GA_SLABS, i, GA_SLABS * j + s)
                    if s < 2:
                        multiply(*at, ps[0][:, 0:T], h_hi, h_lo, SK * s, s == 0, s == 1)
                    else:
                        multiply(*at, ps[1][:, 0:T], y_hi, y_lo, SK * (s - 2), s == 2, s == 5,
                                 (y_los, 0) if first and j == 0 else None)

        branch_a(0, True)
        with pe.Fori(1, KT // 2) as i:
            branch_a(i, False)

        def out_tiles(i, first):
            for j in range(2):
                free(T_OUT + j, i * 2)
                for s in range(2):
                    if first and j == 0:
                        pe.wait_ge(ga_lo, SK * (s + 1))
                    multiply(*slab(U_OUT, 4, i, 2 * j + s), ps[j][:, 0:T], m_hi, m_lo, SK * s, s == 0, s == 1)

        out_tiles(0, True)
        with pe.Fori(1, KT // 2) as i:
            out_tiles(i, False)
        pe.wait_ge(o_acc, KT)
        M.matmul(b_ms[:, 0:T], ones, acc[:, :], start=True, stop=True).then_inc(n_ms, 1)

        for half in range(2):
            fu, tu = U_FFN + HALF_U * half, T_FFN + HALF_T * half

            def up(i, first):
                for j in range(2):
                    free(tu + j, i * 2)
                    for s in range(2):
                        multiply(*slab(fu, 4, i, 2 * j + s), ps[j][:, 0:T], h_hi, h_lo, SK * s, s == 0, s == 1,
                                 (n_lo, 4) if first and j == 0 else None)
                        if first and j == 1 and s == 0:
                            mean_square(nsq, 0)

            up(0, half == 0)
            with pe.Fori(1, FT // 2) as i:
                up(i, False)

            def down(i, first):
                for j in range(2):
                    free(tu + FT + j, i * 2)
                    for s in range(4):
                        if first and j == 0:
                            pe.wait_ge(up_lo, FT * half + SK * (s + 1))
                        multiply(*slab(fu + 2 * FT, 8, i, 4 * j + s), ps[j][:, 0:T], u_hi, u_lo, SK * s,
                                 s == 0, s == 3)

            down(0, True)
            with pe.Fori(1, KT // 2) as i:
                down(i, False)

        pe.wait_ge(dn_acc, KT)
        M.matmul(b_ms[:, 0:T], ones, acc[:, :], start=True, stop=True).then_inc(n_ms, 1)
        pe.wait_ge(p_los, 1)
        for s in range(4):
            m, k = slab(U_PROJ, 4, 0, s)
            pe.wait_ge(lo_done, m * RING + k + 1)
            for j in range(4):
                free(T_PROJ + 4 * s + j, 0)
                out = ps[j % 2][:, 0:T]
                for i in range(2):
                    w = 2 * j + i
                    M.matmul(out, w_hi[:, k, w], p_hi[:, i], start=i == 0, stop=False)
                    M.matmul(out, w_hi[:, k, w], p_lo[:, i], start=False, stop=False)
                    op = M.matmul(out, w_lo[:, k, w], p_hi[:, i], start=False, stop=i == 1)
                op.then_inc(pj_tile if j < 3 else slab_used, 1)

        def ple(i, first):
            for j in range(2):
                free(T_PLE + j, i * 2)
                for s in range(2):
                    multiply(*slab(U_PLE, 4, i, 2 * j + s), ps[j][:, 0:T], h_hi, h_lo, SK * s, s == 0, s == 1,
                             (n_lo, 8) if first and j == 0 else None)
                    if first and j == 1 and s == 0:
                        mean_square(nsq3, 1)

        ple(0, True)
        with pe.Fori(1, KT // 2) as i:
            ple(i, False)

    @block.gpsimd
    def _(pool):
        def row(ap, i):
            if isinstance(i, int):
                return ap[i]
            v = ap[bass.ds(i, 1)]
            if len(v.shape) == 3:
                return v.rearrange("a p n -> (a p) n")
            if len(v.shape) == 4:
                return v.rearrange("a p b n -> (a p) b n")
            return v.rearrange("a p c b n -> (a p) c b n")

        pool.wait_ge(hg_zero, 1)
        pool.dma_start(hs0[:, :, :], io["s0"][0]).then_inc(hg_s0, 16)
        pool.wait_ge(dve_pro, 17)
        pool.dma_start(cum_d, cum[:, :]).then_inc(scr_out, 16)
        pool.dma_start(ecum_d, ecum[:, :]).then_inc(scr_out, 16)
        pool.dma_start(elast_d, elast[:, :]).then_inc(scr_out, 16)
        pool.wait_ge(scr_out, 48)

        def hgrn(r, last):
            pool.wait_ge(hg_tlo, r + 1)
            mask = consts[0:96, K_BATCH:K_BATCH + NB].unsqueeze(2).to_broadcast([96, NB, P])
            v3 = hv3[:, :].bitcast(F32).unsqueeze(1).to_broadcast([96, NB, P])
            nc.gpsimd.tensor_tensor(hvbd[:, :, :], v3, mask,
                                    ALU.mult).then_inc(hg_vbd, 1)
            pool.wait_ge(hg_st, r + 1)
            if not last:
                pool.dma_start(hs0[:, :, :], row(io["s0"], r + 1)).then_inc(hg_s0, 16)
            pool.dma_start(row(io["hg_s"], r), hsn[:, :, :]).then_inc(hg_out, 16)
            pool.dma_start(row(io["hg_p"], r), hsp[:, :]).then_inc(hg_out, 16)
            pool.wait_ge(hg_out, (r + 1) * 32)

        with pool.Fori(0, HEADS - 1) as r:
            hgrn(r, False)
        hgrn(HEADS - 1, True)

        with pool.Fori(0, KT) as j:
            pool.wait_ge(gb_mb, j + 1)
            pool.dma_start(row(mixb, j), bmb[:, :]).then_inc(gb_out, 16)

        def load_parameters(g):
            pool.dma_start(prm[:, :, :], row(io["convp"], g)).then_inc(sg_par_in, 16)
            pool.dma_start(cst[:, :, :, :], row(io["convs"], g)).then_inc(sg_par_in, 16)

        def rows(ap, first, n):
            return ap[first:first + n] if isinstance(first, int) else ap[bass.ds(first, n)]

        def load_cum(g):
            src = rows(cum_d, g * GH, GH).rearrange("h t -> (h t)")
            pool.dma_start(cbc[:, :, :].rearrange("p h t -> p (h t)"), src.partition_broadcast(P)).then_inc(sg_cbc_in, 16)

        def load_decays(g):
            src = rows(ecum_d, g * GH, GH).rearrange("(q a) t -> a q t", a=2)
            for a in range(2):
                pool.dma_start(ecp[HD * a:HD * a + HD], src[a].partition_broadcast(HD)).then_inc(sg_ec_in, 16)
            src = rows(elast_d, g * GH, GH).rearrange("h b -> (h b)")
            pool.dma_start(el[:, :, :].rearrange("p h b -> p (h b)"), src.partition_broadcast(P)).then_inc(sg_ec_in, 16)

        def load_state(g, seq):
            pool.dma_start(ht[:, seq % 4], row(io["ht"], g)[:, seq]).then_inc(sg_ht_in[seq % 4], 16)

        def ssd(g, first, last):
            pool.wait_ge(sg_btlo, g + 1)
            if not first:
                pool.wait_ge(sg_su, g * NB)
            pool.wait_ge(sg_cur, g + 1)
            pool.wait_ge(sg_cbc_in, (g + 1) * 16)
            if not first:
                pool.wait_ge(sg_ms, g)
            mask = consts[0:96, K_BATCH:K_BATCH + NB].unsqueeze(2).to_broadcast([96, NB, P])
            b3 = bt3[:, :].bitcast(F32).unsqueeze(1).to_broadcast([96, NB, P])
            nc.gpsimd.tensor_tensor(bbd[:, :, :], b3, mask,
                                    ALU.mult).then_inc(sg_bbd, 1)
            exponents(nc.gpsimd, me, cbc, tcur, 1).then_inc(sg_segp, 1)
            pool.wait_ge(sg_nc, (g + 1) * XT)
            pool.dma_start(row(io["conv"], g), ncv[:, :, :]).then_inc(sg_nc_out, 16)
            if not last:
                load_parameters(g + 1)
                pool.wait_ge(sg_segp, g + 1)
                pool.wait_ge(sg_seg, g + 1)
                load_cum(g + 1)
            pool.wait_ge(sg_spe, g + 1)
            pool.dma_start(row(io["ssm_p"], g), ssp[:, :, :]).then_inc(sg_sp_out, 16)
            def renew(seq):
                pool.wait_ge(sg_ht_out[seq % 4], g * 32 + 16 * (seq // 4 + 1))
                if seq < 4:
                    load_state(g, seq + 4)
                elif not last:
                    load_state(g + 1, seq - 4)

            for seq in range(NB):
                pool.wait_ge(sg_up, g * NB + seq + 1)
                pool.dma_start(row(io["ssm_s"], g * 2 + seq // 4)[:, seq % 4],
                               ht[:, seq % 4]).then_inc(sg_ht_out[seq % 4], 16)
                if seq % 4:
                    renew(seq - 1)
                if seq % 4 == 3:
                    renew(seq)
            if not last:
                pool.wait_ge(sg_g, g + 1)
                load_decays(g + 1)

        pool.wait_ge(sg_raw0, 1)
        load_parameters(0)
        load_cum(0)
        for seq in range(4):
            load_state(0, seq)
        load_decays(0)
        ssd(0, True, False)
        with pool.Fori(1, GROUPS - 1) as g:
            ssd(g, False, False)
        ssd(GROUPS - 1, False, True)

        pool.wait_ge(sg_y32, GROUPS)
        pool.wait_ge(sg_nc_out, 16 * GROUPS)
        pool.wait_ge(sg_sp_out, 16 * GROUPS)
        pool.dma_start(amb[:, :], mixb[0]).then_inc(ga_in, 16)
        with pool.Fori(1, KT) as j:
            pool.wait_ge(ga_m, j)
            pool.dma_start(amb[:, :], row(mixb, j)).then_inc(ga_in, 16)

        pool.wait_ge(slab_used, U_OUT)
        pool.dma_start(x_res[:, :, :], io["x"]).then_inc(xr_in, 16)

        def add_normed(norm, src, residual):
            v = src[:, 4 * XV:KT]
            nc.gpsimd.tensor_tensor(v, v, four(nrs[:, :]), ALU.mult).then_inc(x2_pa, 1)
            pool.wait_ge(x2_pa, norm + 1)
            nc.gpsimd.tensor_tensor(x2[:, 4 * XV:KT], v, residual[:, 4 * XV:KT], ALU.add).then_inc(x2_pb, 1)

        pool.wait_ge(n_rs, 2)
        pool.wait_ge(o_w, KT)
        pool.wait_ge(xr_in, 16)
        add_normed(0, mo, x_res)
        pool.wait_ge(slab_used, U_PROJ)
        pool.dma_start(p_in[:, :, :], io["p"]).then_inc(p_land, 16)
        pool.wait_ge(n_rs, 4)
        pool.wait_ge(dn_w, KT)
        add_normed(1, ffn, x2)
        with pool.Fori(0, KT) as j:
            pool.wait_ge(g_y, j + 1)
            pool.dma_start(io["y"][:, bass.ds(j, 1)], x2[:, bass.ds(j, 1)]).then_inc(y_out, 16)
        pool.wait_ge(y_out, 16 * KT)

    stack.close()


def slabs(w):
    k, n = w.shape
    v = w.reshape(k // (SK * P), SK, P, n // P, P)
    return v.transpose(3, 0, 2, 1, 4).reshape(-1, P, SK, P)


def feature_major(prompt, sample):
    v = np.concatenate([prompt.reshape(TP, -1), sample.reshape(TS, -1)]).T
    return np.ascontiguousarray(v.reshape(-1, P, T).transpose(1, 0, 2))


def columns(v):
    return v.reshape(-1, P).T


def kernel(**inputs):
    import concourse.bacc as _bacc
    from concourse.bass_utils import run_bass_kernel_spmd as _run

    a = {k: np.asarray(v) for k, v in inputs.items()}
    w_in = a["w_in"][0]
    dx, bc = 2 * D, GROUPS * P
    z, xbc = w_in[:, 0:dx], w_in[:, dx:2 * dx + 2 * bc]
    o = 2 * dx + 2 * bc
    w_dt = w_in[:, o:o + HD]
    o += HD
    q, f, v, g, ga, gb = (w_in[:, o + D * i:o + D * (i + 1)] for i in range(6))

    def tiles(w, per):
        s = slabs(w)
        return s.reshape(-1, per, P, SK, P)

    hg = np.stack([tiles(w, 2) for w in (f, q, v, g)], 1).reshape(-1, P, SK, P)
    br_b = np.concatenate([tiles(gb, 2), tiles(a["w_br_b"][0], 2)], 1).reshape(-1, P, SK, P)
    zt, xt = tiles(z, 2).reshape(GROUPS, 4, 2, P, SK, P), tiles(xbc, 2)
    xs = xt[0:32].reshape(GROUPS, 4, 2, P, SK, P)
    sg = np.concatenate([xt[32:40, None], xt[40:48, None], xs, zt], 1).reshape(-1, P, SK, P)
    br_a = np.concatenate([tiles(ga, 2), tiles(a["w_br_a"][0], 4)], 1).reshape(-1, P, SK, P)
    up, down = tiles(a["w_up"][0], 2), a["w_down"][0]
    ffn = []
    for half in range(2):
        ffn += [up[FT * half:FT * half + FT].reshape(-1, P, SK, P), slabs(down[FT * P * half:FT * P * (half + 1)])]
    proj = a["w_ple_proj"][0].reshape(2, P, 4, 4, P).transpose(2, 1, 3, 0, 4).reshape(4, P, SK, P)
    w = np.concatenate([hg, br_b, sg, br_a, slabs(a["w_out"][0])] + ffn + [proj, slabs(a["w_ple_gate"][0])])

    def conv_tiles(m):
        n = m.shape[0]
        x = m[:, 0:dx].reshape(n, GROUPS, 4, P)
        b = m[:, dx:dx + bc].reshape(n, GROUPS, 1, P)
        c = m[:, dx + bc:].reshape(n, GROUPS, 1, P)
        return np.concatenate([b, c, x], 2).transpose(1, 3, 2, 0)

    arrays = {
        "w": w,
        "wdt": w_dt.reshape(KT, P, HD).transpose(1, 0, 2),
        "x": feature_major(a["x_prompt"], a["x_sample"]),
        "p": feature_major(a["p_prompt"][0], a["p_sample"][0]),
        "consts": constants(),
        "cols": np.concatenate(
            [columns(a[n][0]) for n in ("norm_mix_pre", "norm_mix_post", "norm_ffn_pre", "norm_ffn_post",
                                        "norm_ple", "hg_norm", "ssm_norm")]
            + [columns(np.repeat(a["d_skip"][0], HD)), columns(a["hg_lb"][0]), columns(a["hg_lb"][1])], 1),
        "hv": np.stack([a["dt_bias"][0], a["a_log"][0]], 1),
        "convp": conv_tiles(np.concatenate([a["conv_w"][0], a["conv_b"]])),
        "convs": conv_tiles(a["state_conv"][0].reshape(NB * (CW - 1), -1)).reshape(GROUPS, P, XT, NB, CW - 1),
        "s0": a["state_hgrn"][0].transpose(1, 2, 0, 3),
        "ht": a["state_ssm"][0].reshape(NB, GROUPS, GH * HD, P).transpose(1, 3, 0, 2),
    }
    outs = {
        "y": (P, KT, T), "ssm_p": (GROUPS, P, 4, P), "conv": (GROUPS, P, XT, (1 + NB) * (CW - 1)),
        "hg_p": (HEADS, P, P), "ssm_s": (GROUPS * 2, P, NB // 2, GH * HD), "hg_s": (HEADS, P, NB, P),
    }
    nc = _bacc.Bacc("TRN2", target_bir_lowering=False, num_devices=1)
    io, feed = {}, {}
    for name, v in arrays.items():
        v = np.ascontiguousarray(v)
        feed[f"in_{name}"] = v
        io[name] = nc.dram_tensor(f"in_{name}", v.shape, F32, kind="ExternalInput").ap()
    for name, shape in outs.items():
        io[name] = nc.dram_tensor(f"out_{name}", shape, F32, kind="ExternalOutput").ap()
    layer_program(nc, io)
    got = _run(nc, [feed], core_ids=[0]).results[0]
    got = {n: np.asarray(got[f"out_{n}"]) for n in outs}

    y = got["y"].transpose(2, 1, 0).reshape(T, D)
    cv = got["conv"].transpose(3, 0, 2, 1)
    n = cv.shape[0]
    cv = np.concatenate([cv[:, :, 2:].reshape(n, dx), cv[:, :, 0].reshape(n, bc), cv[:, :, 1].reshape(n, bc)], 1)
    sp = got["ssm_p"].transpose(0, 2, 1, 3).reshape(1, 1, GROUPS * GH, HD, P)
    ss = got["ssm_s"].reshape(GROUPS, 2, P, NB // 2, GH * HD).transpose(1, 3, 0, 4, 2).reshape(1, NB, GROUPS * GH, HD, P)
    return (
        np.ascontiguousarray(y[0:TP].reshape(1, TP, D)),
        np.ascontiguousarray(y[TP:].reshape(NB, SB, D)),
        np.ascontiguousarray(sp),
        np.ascontiguousarray(cv[0:CW - 1].reshape(1, 1, CW - 1, -1)),
        np.ascontiguousarray(got["hg_p"].reshape(1, 1, HEADS, P, P)),
        np.ascontiguousarray(ss),
        np.ascontiguousarray(cv[CW - 1:].reshape(1, NB, CW - 1, -1)),
        np.ascontiguousarray(got["hg_s"].transpose(2, 0, 1, 3).reshape(1, NB, HEADS, P, P)),
    )
```
